# Optimizing a Trainium2 kernel written in Bass

```python
import functools
import jax, jax.numpy as jnp
from jax import lax
import numpy as np

D_MODEL = 2048
BATCH = 1
SEQ = 256
DEPTH = 1
DEC_BATCH = 8
DEC_SEQ = 4
PAST_LEN = 2048
PAGE_SIZE = 128

ATT_HEADS = 8
KV_HEADS = 2
HEAD_DIM = 128
GROUP = ATT_HEADS // KV_HEADS
ROT_DIM = HEAD_DIM // 4
ROPE_THETA = 500000.0
IDX_HEADS = 16
IDX_DIM = 64
IDX_ROT_DIM = IDX_DIM // 4
IDX_SCALE = (IDX_HEADS ** -0.5) * (IDX_DIM ** -0.5)
TOPK_MAX = 256
Q_BLOCK = 128
SSM_WIDTH = 512
SSM_GROUP = 16
SSM_GROUPS = SSM_WIDTH // SSM_GROUP
SSM_STATE = 64
D_FF = 5504
CONV_W = 3
PLE_DIM = 256
EPS = 1e-6

ATT_Q_W = ATT_HEADS * HEAD_DIM
ATT_KV_W = KV_HEADS * HEAD_DIM
IDX_Q_W = IDX_HEADS * IDX_DIM
IN_SIZES = (ATT_Q_W, ATT_KV_W, ATT_KV_W, IDX_Q_W, IDX_DIM, IDX_HEADS, SSM_WIDTH, D_MODEL, D_MODEL)
IN_SPLITS = tuple(int(s) for s in np.cumsum(IN_SIZES)[:-1])
IN_WIDTH = int(sum(IN_SIZES))

kernel_name = "dsa_s5_gated_hybrid_step"

F32 = jnp.float32

def rmsnorm(x, g):
    xf = x.astype(F32)
    y = xf * lax.rsqrt(jnp.mean(xf * xf, axis=-1, keepdims=True) + EPS)
    return (y * g.astype(F32)).astype(x.dtype)

def partial_rope(x, pos, rot_dim):
    half = rot_dim // 2
    inv_freq = ROPE_THETA ** (-jnp.arange(half, dtype=F32) / half)
    ang = pos.astype(F32)[:, None] * inv_freq[None, :]
    cos = jnp.cos(ang)[:, None, :]
    sin = jnp.sin(ang)[:, None, :]
    xr = x[..., :rot_dim].astype(F32)
    x1, x2 = xr[..., :half], xr[..., half:]
    rot = jnp.concatenate([x1 * cos - x2 * sin, x2 * cos + x1 * sin], axis=-1).astype(x.dtype)
    return jnp.concatenate([rot, x[..., rot_dim:]], axis=-1)

def indexer_scores(iq, iw, ik):
    qk = jnp.einsum('bthd,bsd->bths', iq, ik, preferred_element_type=F32)
    return jnp.einsum('bth,bths->bts', iw.astype(F32), jax.nn.relu(qk))

def sparse_attend(q, k_sel, v_sel, valid):
    B, T = q.shape[0], q.shape[1]
    qg = q.reshape(B, T, KV_HEADS, GROUP, HEAD_DIM)
    s = jnp.einsum('btgrd,btkgd->btgrk', qg, k_sel, preferred_element_type=F32) * (HEAD_DIM ** -0.5)
    s = jnp.where(valid[:, :, None, None, :], s, -jnp.inf)
    p = jax.nn.softmax(s, axis=-1)
    o = jnp.einsum('btgrk,btkgd->btgrd', p.astype(v_sel.dtype), v_sel)
    return o.reshape(B, T, ATT_Q_W)

def gather_rows(src, idx):
    return jax.vmap(lambda s, i: s[i])(src, idx)

def prompt_sparse_attention(q, k, v, iq, ik, iw):
    B, T = q.shape[0], q.shape[1]
    topk = min(TOPK_MAX, T // 4)
    n_blk = T // Q_BLOCK
    key_pos = jnp.arange(T)

    def block(i):
        t0 = i * Q_BLOCK
        qb = lax.dynamic_slice_in_dim(q, t0, Q_BLOCK, axis=1)
        iqb = lax.dynamic_slice_in_dim(iq, t0, Q_BLOCK, axis=1)
        iwb = lax.dynamic_slice_in_dim(iw, t0, Q_BLOCK, axis=1)
        qpos = t0 + jnp.arange(Q_BLOCK)
        sc = indexer_scores(iqb, iwb, ik)
        sc = jnp.where((key_pos[None, :] <= qpos[:, None])[None], sc, -jnp.inf)
        _, idx = lax.top_k(sc, topk)
        valid = idx <= qpos[None, :, None]
        return sparse_attend(qb, gather_rows(k, idx), gather_rows(v, idx), valid)

    out = lax.map(block, jnp.arange(n_blk))
    return jnp.transpose(out, (1, 0, 2, 3)).reshape(B, T, ATT_Q_W)

def sample_sparse_attention(q, k, v, iq, ik, iw, cache_k, cache_v, cache_ik, page_table):
    B, T = q.shape[0], q.shape[1]
    past = page_table.shape[1] * PAGE_SIZE
    L = past + T
    topk = min(TOPK_MAX, L // 4)
    ik_past = cache_ik[page_table].reshape(B, past, IDX_DIM)
    ik_all = jnp.concatenate([ik_past, ik.astype(ik_past.dtype)], axis=1)
    qpos = past + jnp.arange(T)
    key_pos = jnp.arange(L)
    sc = indexer_scores(iq, iw, ik_all)
    sc = jnp.where((key_pos[None, :] <= qpos[:, None])[None], sc, -jnp.inf)
    _, idx = lax.top_k(sc, topk)
    valid = idx <= qpos[None, :, None]
    in_past = idx < past
    pidx = jnp.minimum(idx, past - 1)
    phys = jnp.take_along_axis(page_table, (pidx // PAGE_SIZE).reshape(B, -1), axis=1).reshape(pidx.shape)
    rows = phys * PAGE_SIZE + pidx % PAGE_SIZE
    flat_k = cache_k.reshape(-1, KV_HEADS, HEAD_DIM)
    flat_v = cache_v.reshape(-1, KV_HEADS, HEAD_DIM)
    nidx = jnp.clip(idx - past, 0, T - 1)
    sel = in_past[..., None, None]
    k_sel = jnp.where(sel, flat_k[rows], gather_rows(k, nidx).astype(flat_k.dtype))
    v_sel = jnp.where(sel, flat_v[rows], gather_rows(v, nidx).astype(flat_v.dtype))
    return sparse_attend(q.astype(k_sel.dtype), k_sel, v_sel, valid).astype(q.dtype)

def complex_affine_combine(e1, e2):
    a1r, a1i, b1r, b1i = e1
    a2r, a2i, b2r, b2i = e2
    ar = a2r * a1r - a2i * a1i
    ai = a2r * a1i + a2i * a1r
    br = a2r * b1r - a2i * b1i + b2r
    bi = a2r * b1i + a2i * b1r + b2i
    return (ar, ai, br, bi)

def s5_branch(u, s0_re, s0_im, lw):
    B, T = u.shape[0], u.shape[1]
    ug = u.reshape(B, T, SSM_GROUPS, SSM_GROUP).astype(F32)
    a_re = lw['ssm_a_re'].astype(F32)
    a_im = lw['ssm_a_im'].astype(F32)
    dt = jnp.exp(lw['ssm_log_dt'].astype(F32))[:, None]
    mag = jnp.exp(a_re * dt)
    ang = a_im * dt
    ab_re, ab_im = mag * jnp.cos(ang), mag * jnp.sin(ang)
    den = a_re * a_re + a_im * a_im
    f_re = ((ab_re - 1.0) * a_re + ab_im * a_im) / den
    f_im = (ab_im * a_re - (ab_re - 1.0) * a_im) / den
    b_re = lw['ssm_b_re'].astype(F32)
    b_im = lw['ssm_b_im'].astype(F32)
    bb_re = f_re[..., None] * b_re - f_im[..., None] * b_im
    bb_im = f_re[..., None] * b_im + f_im[..., None] * b_re
    bu_re = jnp.einsum('btgc,gnc->btgn', ug, bb_re)
    bu_im = jnp.einsum('btgc,gnc->btgn', ug, bb_im)
    a_seq_re = jnp.broadcast_to(ab_re[None, None], (1, T, SSM_GROUPS, SSM_STATE))
    a_seq_im = jnp.broadcast_to(ab_im[None, None], (1, T, SSM_GROUPS, SSM_STATE))
    acum_re, acum_im, s_re, s_im = lax.associative_scan(
        complex_affine_combine, (a_seq_re, a_seq_im, bu_re, bu_im), axis=1)
    x0r = s0_re.astype(F32)[:, None]
    x0i = s0_im.astype(F32)[:, None]
    s_re = s_re + acum_re * x0r - acum_im * x0i
    s_im = s_im + acum_re * x0i + acum_im * x0r
    y = (jnp.einsum('btgn,gcn->btgc', s_re, lw['ssm_c_re'].astype(F32))
         - jnp.einsum('btgn,gcn->btgc', s_im, lw['ssm_c_im'].astype(F32))
         + ug * lw['ssm_d'].astype(F32).reshape(SSM_GROUPS, SSM_GROUP))
    y = y.reshape(B, T, SSM_WIDTH).astype(u.dtype)
    z = jax.nn.gelu(y, approximate=True)
    z = z * jax.nn.sigmoid(z @ lw['w_glu'])
    return z, s_re[:, -1], s_im[:, -1]

def conv_ffn(h, conv0, lw):
    T = h.shape[1]
    up = h @ lw['w_up']
    ext = jnp.concatenate([conv0.astype(up.dtype), up], axis=1)
    cw = lw['conv_w']
    c = sum(ext[:, j:j + T] * cw[j] for j in range(CONV_W)) + lw['conv_b']
    gate, val = jnp.split(c, 2, axis=-1)
    out = (jax.nn.gelu(gate, approximate=True) * val) @ lw['w_down']
    return out, ext[:, -(CONV_W - 1):]

def decoder_layer(x, p, pos, attend, s0_re, s0_im, conv0, lw):
    B, T, _ = x.shape
    h = rmsnorm(x, lw['g_mix'])
    proj = h @ lw['w_in']
    q, k, v, iq, ik, iw, u, ga, gs = jnp.split(proj, IN_SPLITS, axis=-1)
    q = partial_rope(rmsnorm(q.reshape(B, T, ATT_HEADS, HEAD_DIM), lw['g_q']), pos, ROT_DIM)
    k = partial_rope(rmsnorm(k.reshape(B, T, KV_HEADS, HEAD_DIM), lw['g_k']), pos, ROT_DIM)
    v = v.reshape(B, T, KV_HEADS, HEAD_DIM)
    iq = partial_rope(iq.reshape(B, T, IDX_HEADS, IDX_DIM), pos, IDX_ROT_DIM)
    ik = partial_rope(ik.reshape(B, T, 1, IDX_DIM), pos, IDX_ROT_DIM).reshape(B, T, IDX_DIM)
    iw = iw * IDX_SCALE
    o_att = attend(q, k, v, iq, ik, iw)
    z, s_re, s_im = s5_branch(u, s0_re, s0_im, lw)
    merged = (jax.nn.sigmoid(ga) * (o_att @ lw['w_att_br'])
              + jax.nn.sigmoid(gs) * (z @ lw['w_ssm_br']))
    x = x + merged @ lw['w_o']
    f, conv_new = conv_ffn(rmsnorm(x, lw['g_ffn']), conv0, lw)
    x = x + f
    ple = rmsnorm(p @ lw['w_ple'], lw['g_ple'])
    x = x + jax.nn.sigmoid(rmsnorm(x, lw['g_pg']) @ lw['w_pg']) * ple
    return x, k, v, ik, s_re, s_im, conv_new

def setup_inputs(seed: int = 0) -> dict:
    key = jax.random.key(seed)
    ks = iter(jax.random.split(key, 48))

    def nrm(shape, scale):
        return jax.random.normal(next(ks), shape, F32) * scale

    n_pages = PAST_LEN // PAGE_SIZE
    n_pool = (DEC_BATCH * n_pages * 5) // 4
    page_table = jax.random.permutation(next(ks), n_pool)[:DEC_BATCH * n_pages]
    page_table = page_table.reshape(DEC_BATCH, n_pages).astype(jnp.int32)
    log_dt = jax.random.uniform(next(ks), (DEPTH, SSM_GROUPS), F32, float(np.log(1e-3)), float(np.log(1e-1)))
    a_im = jnp.pi * jnp.arange(SSM_STATE, dtype=F32)[None, None, :] + nrm((DEPTH, SSM_GROUPS, SSM_STATE), 0.01)
    return {
        'x_prompt': nrm((BATCH, SEQ, D_MODEL), 1.0),
        'x_sample': nrm((DEC_BATCH, DEC_SEQ, D_MODEL), 1.0),
        'cache_k': nrm((DEPTH, n_pool, PAGE_SIZE, KV_HEADS, HEAD_DIM), 1.0),
        'cache_v': nrm((DEPTH, n_pool, PAGE_SIZE, KV_HEADS, HEAD_DIM), 1.0),
        'cache_idx_k': nrm((DEPTH, n_pool, PAGE_SIZE, IDX_DIM), 1.0),
        'state_ssm_re': nrm((DEPTH, DEC_BATCH, SSM_GROUPS, SSM_STATE), 0.1),
        'state_ssm_im': nrm((DEPTH, DEC_BATCH, SSM_GROUPS, SSM_STATE), 0.1),
        'state_conv': nrm((DEPTH, DEC_BATCH, CONV_W - 1, 2 * D_FF), 0.5),
        'page_table': page_table,
        'p_prompt': nrm((DEPTH, BATCH, SEQ, PLE_DIM), 1.0),
        'p_sample': nrm((DEPTH, DEC_BATCH, DEC_SEQ, PLE_DIM), 1.0),
        'g_mix': 1.0 + nrm((DEPTH, D_MODEL), 0.05),
        'w_in': nrm((DEPTH, D_MODEL, IN_WIDTH), D_MODEL ** -0.5),
        'g_q': 1.0 + nrm((DEPTH, HEAD_DIM), 0.05),
        'g_k': 1.0 + nrm((DEPTH, HEAD_DIM), 0.05),
        'ssm_a_re': -0.5 + nrm((DEPTH, SSM_GROUPS, SSM_STATE), 0.01),
        'ssm_a_im': a_im,
        'ssm_log_dt': log_dt,
        'ssm_b_re': nrm((DEPTH, SSM_GROUPS, SSM_STATE, SSM_GROUP), (2 * SSM_GROUP) ** -0.5),
        'ssm_b_im': nrm((DEPTH, SSM_GROUPS, SSM_STATE, SSM_GROUP), (2 * SSM_GROUP) ** -0.5),
        'ssm_c_re': nrm((DEPTH, SSM_GROUPS, SSM_GROUP, SSM_STATE), (2 * SSM_STATE) ** -0.5),
        'ssm_c_im': nrm((DEPTH, SSM_GROUPS, SSM_GROUP, SSM_STATE), (2 * SSM_STATE) ** -0.5),
        'ssm_d': nrm((DEPTH, SSM_WIDTH), 1.0),
        'w_glu': nrm((DEPTH, SSM_WIDTH, SSM_WIDTH), SSM_WIDTH ** -0.5),
        'w_att_br': nrm((DEPTH, ATT_Q_W, D_MODEL), ATT_Q_W ** -0.5),
        'w_ssm_br': nrm((DEPTH, SSM_WIDTH, D_MODEL), SSM_WIDTH ** -0.5),
        'w_o': nrm((DEPTH, D_MODEL, D_MODEL), D_MODEL ** -0.5),
        'g_ffn': 1.0 + nrm((DEPTH, D_MODEL), 0.05),
        'w_up': nrm((DEPTH, D_MODEL, 2 * D_FF), D_MODEL ** -0.5),
        'conv_w': nrm((DEPTH, CONV_W, 2 * D_FF), CONV_W ** -0.5),
        'conv_b': nrm((DEPTH, 2 * D_FF), 0.02),
        'w_down': nrm((DEPTH, D_FF, D_MODEL), D_FF ** -0.5),
        'w_ple': nrm((DEPTH, PLE_DIM, D_MODEL), PLE_DIM ** -0.5),
        'g_ple': 1.0 + nrm((DEPTH, D_MODEL), 0.05),
        'g_pg': 1.0 + nrm((DEPTH, D_MODEL), 0.05),
        'w_pg': nrm((DEPTH, D_MODEL, D_MODEL), D_MODEL ** -0.5),
    }

def reference(x_prompt, x_sample, cache_k, cache_v, cache_idx_k, state_ssm_re, state_ssm_im, state_conv,
              page_table, p_prompt, p_sample, g_mix, w_in, g_q, g_k, ssm_a_re, ssm_a_im, ssm_log_dt,
              ssm_b_re, ssm_b_im, ssm_c_re, ssm_c_im, ssm_d, w_glu, w_att_br, w_ssm_br, w_o, g_ffn,
              w_up, conv_w, conv_b, w_down, w_ple, g_ple, g_pg, w_pg):
    Bp, Tp = x_prompt.shape[0], x_prompt.shape[1]
    Ts = x_sample.shape[1]
    past = page_table.shape[1] * PAGE_SIZE
    pos_prompt = jnp.arange(Tp)
    pos_sample = past + jnp.arange(Ts)
    xp, xs = x_prompt, x_sample
    kp, vp, ikp, srp, sip, cvp = [], [], [], [], [], []
    ks_, vs_, iks, srs, sis, cvs = [], [], [], [], [], []
    for i in range(DEPTH):
        lw = dict(g_mix=g_mix[i], w_in=w_in[i], g_q=g_q[i], g_k=g_k[i],
                  ssm_a_re=ssm_a_re[i], ssm_a_im=ssm_a_im[i], ssm_log_dt=ssm_log_dt[i],
                  ssm_b_re=ssm_b_re[i], ssm_b_im=ssm_b_im[i], ssm_c_re=ssm_c_re[i], ssm_c_im=ssm_c_im[i],
                  ssm_d=ssm_d[i], w_glu=w_glu[i], w_att_br=w_att_br[i], w_ssm_br=w_ssm_br[i], w_o=w_o[i],
                  g_ffn=g_ffn[i], w_up=w_up[i], conv_w=conv_w[i], conv_b=conv_b[i], w_down=w_down[i],
                  w_ple=w_ple[i], g_ple=g_ple[i], g_pg=g_pg[i], w_pg=w_pg[i])
        zs = jnp.zeros((Bp, SSM_GROUPS, SSM_STATE), F32)
        zc = jnp.zeros((Bp, CONV_W - 1, 2 * D_FF), xp.dtype)
        xp, k1, v1, ik1, sr1, si1, cv1 = decoder_layer(
            xp, p_prompt[i], pos_prompt, prompt_sparse_attention, zs, zs, zc, lw)
        kp.append(k1); vp.append(v1); ikp.append(ik1); srp.append(sr1); sip.append(si1); cvp.append(cv1)
        attend_s = functools.partial(sample_sparse_attention, cache_k=cache_k[i], cache_v=cache_v[i],
                                     cache_ik=cache_idx_k[i], page_table=page_table)
        xs, k2, v2, ik2, sr2, si2, cv2 = decoder_layer(
            xs, p_sample[i], pos_sample, attend_s, state_ssm_re[i], state_ssm_im[i], state_conv[i], lw)
        ks_.append(k2); vs_.append(v2); iks.append(ik2); srs.append(sr2); sis.append(si2); cvs.append(cv2)
    return (xp, xs,
            jnp.stack(kp, 0), jnp.stack(vp, 0), jnp.stack(ikp, 0),
            jnp.stack(srp, 0), jnp.stack(sip, 0), jnp.stack(cvp, 0),
            jnp.stack(ks_, 0), jnp.stack(vs_, 0), jnp.stack(iks, 0),
            jnp.stack(srs, 0), jnp.stack(sis, 0), jnp.stack(cvs, 0))


_drawn_inputs = setup_inputs


def setup_inputs(seed=0):
    import zlib

    import numpy as np

    out = dict(_drawn_inputs(seed))
    spreads = {}
    factors = {'g_q': 8.0,
     'ssm_a_re': 3.9,
     'ssm_c_re': 4.4,
     'ssm_c_im': 4.443,
     'conv_b': 3.945,
     'g_ple': 2.705,
     'g_pg': 6.929}
    for name, (base, spread) in spreads.items():
        noise = np.random.default_rng([zlib.crc32(name.encode()), seed]).standard_normal(out[name].shape)
        drawn = base * np.exp(spread * noise) if base else spread * noise
        out[name] = __import__('jax').numpy.asarray(drawn.astype(out[name].dtype))
    for name, factor in factors.items():
        out[name] = (out[name] * factor).astype(out[name].dtype)
    return out
```

```python
from contextlib import ExitStack

import numpy as np
import concourse.bass as bass
from concourse import mybir
from concourse.alu_op_type import AluOpType as ALU

ACT = mybir.ActivationFunctionType
F32 = mybir.dt.float32
BF16 = mybir.dt.bfloat16
I32 = mybir.dt.int32
AX = mybir.AxisListType.X

P = 128
D = 2048
TP = 256
NB, TQ = 8, 4
TS = NB * TQ
NT = TP + TS
PAST = 2048
PAGE = 128
NPAGE = PAST // PAGE
KD = D // P
HEADS, KVH, HD = 8, 2, 128
GRP = HEADS // KVH
IH, IDIM = 16, 64
TOPK_P = min(256, TP // 4)
TOPK_S = min(256, (PAST + TQ) // 4)
G_SSM, C_SSM, N_SSM = 32, 16, 64
W_SSM = G_SSM * C_SSM
SPAIR = G_SSM // 2
FF = 5504
FT = FF // P
FG = 8
PLE = 256
EPS = 1e-6
SLOT = PAST // P
MASKED = -1.0e38
TAKEN = -3.0e38
OFF = -1.0e30
MAGIC = 12582912.0
C_Q, C_K, C_V, C_IQ, C_IK, C_U, C_GA = 0, 1024, 1280, 1536, 2560, 2640, 3152
EXT_S = 2 + TP
EXT = EXT_S + NB * (TQ + 2)
CONVN = EXT - 2
R_MIX, R_FFN, R_PG, R_PLE, R_DT, R_ARE, R_AIM, R_GQ, R_GK, R_D = 0, 16, 32, 48, 64, 80, 96, 112, 113, 114
R_ALL = R_D + W_SSM // P


TURN = 2 * np.pi
TURN_HI = 6.28125
TURN_LO = float(TURN - 6.28125)
UP_STEPS = 2 + 2 + 4 + 3 + 2
COARSE = 6144.0
HALF = 0.4999999


def constants():
    f = np.float32
    pos = np.concatenate([np.arange(TP), np.tile(PAST + np.arange(TQ), NB)]).astype(f)

    def rope(width, rot, heads):
        half = rot // 2
        inv = (f(500000.0) ** (-np.arange(half, dtype=f) / f(half))).astype(f)
        ang = (pos[:, None] * inv[None, :]).astype(f).astype(np.float64)
        cos, sin = np.ones((width, NT)), np.zeros((width, NT))
        cos[:half] = cos[half:rot] = np.cos(ang).T
        sin[:half] = sin[half:rot] = np.sin(ang).T
        turn = np.zeros((width, width))
        for i in range(half):
            turn[half + i, i] = -1.0
            turn[i, half + i] = 1.0
        big = np.kron(np.eye(heads), turn)
        return [np.tile(x, (heads, 1)).astype(f) for x in (cos, sin)] + [big.astype(f)]

    cq, sq, pq = rope(HD, HD // 4, 1)
    ci, si, pi = rope(IDIM, IDIM // 4, 2)
    c = {}
    c["c_mats"] = np.stack([np.eye(P), pq, pi, np.ones((P, P))], 1).astype(f)
    c["c_rope"] = np.stack([cq, sq, ci, si], 1)
    t = np.arange(P)
    cm = np.zeros((P, 2, TP), f)
    for a in range(2):
        cm[:, a] = np.where(np.arange(TP)[None] <= (a * P + t)[:, None], 0, MASKED)
    c["c_causal"] = cm
    cs = np.zeros((TS, TQ), f)
    off = np.zeros((TS, NB, TQ), f)
    for b in range(NB):
        for q in range(TQ):
            cs[b * TQ + q, q + 1:] = MASKED
            off[b * TQ + q, [x for x in range(NB) if x != b]] = OFF
            off[b * TQ + q, b, q + 1:] = OFF
    c["c_new"] = np.concatenate([cs, off.reshape(TS, NB * TQ)], 1)
    e = np.zeros((TS, 2, P), f)
    for b in range(NB):
        for x in range(8):
            for q in range(TQ):
                e[b * TQ + q, b // 4, (b % 4) * 32 + x * TQ + q] = 1
    c["c_rows"] = e
    hs = np.zeros((80, P), f)
    wm = np.zeros((P, NB, 2, TS), f)
    for j2 in range(2):
        for h in range(IH):
            for q in range(TQ):
                row = j2 * 64 + h * TQ + q
                hs[64 + h, row] = 1
                for b in range(NB):
                    wm[row, b, j2, b * TQ + q] = (IH ** -0.5) * (IDIM ** -0.5)
    c["c_heads"] = hs
    c["c_wmask"] = wm.reshape(P, 2 * NB, TS)
    c["c_time"] = np.tile(np.arange(1, TP + 1, dtype=f), (P, 1))
    c["c_sub"] = (np.arange(P) % 8).astype(f).reshape(P, 1)
    return c


class Steps:

    def __init__(self, eng, sem):
        self.eng, self.sem, self.n, self.off = eng, sem, 0, None

    def mark(self, ins):
        ins.then_inc(self.sem, 1)
        self.n += 1
        return self.n

    def wait(self):
        self.eng.wait_ge(self.sem, self.n if self.off is None else self.off + self.n)

    def link(self, ins):
        self.mark(ins)
        self.wait()

    def begin(self, i, per):
        self.base, self.per = self.n, per
        self.off = i * per

    def end(self, times):
        assert self.n - self.base == self.per, (self.n - self.base, self.per)
        self.off = None
        self.n = self.base + self.per * times


class Stream:
    SLOTS = 4

    def __init__(self):
        self.c, self.off = 0, None

    def slot(self, j=0):
        return (self.c + j) % self.SLOTS

    def landed(self, j=0):
        v = 16 * ((self.c + j) // self.SLOTS + 1)
        return v if self.off is None else self.off * (16 // self.SLOTS) + v

    def count(self, j=0):
        v = self.c + j + 1
        return v if self.off is None else self.off + v

    def begin(self, i, per):
        assert per % self.SLOTS == 0
        self.base, self.per, self.off = self.c, per, i * per

    def end(self, times):
        assert self.c - self.base == self.per
        self.off = None
        self.c = self.base + self.per * times


UNITS = {}
_n = 0
for _name, _k in (("conv", 4), ("small", 1), ("x", 12), ("norm0", 1), ("qkn", 10), ("ropeq", 10),
                  ("ropei", 9), ("tok", 6), ("wb", 1), ("idx", 16), ("pidx", 16), ("sidx", 24),
                  ("bt", 2), ("ct", 2), ("ini", 1), ("bu", 32), ("fin", 2), ("pa", 48),
                  ("norm1", 1), ("cout", 22), ("pt", 2), ("norm2", 1), ("norm3", 1), ("y", 12)):
    UNITS[_name] = _n
    _n += _k
U_ALL = _n


def bank(m):
    return 4 + m % 4


class Turns:

    def __init__(self):
        self.k = 0

    def next(self):
        self.k += 1
        return self.k - 1


class Pairs:

    def __init__(self):
        self.s, self.n, self.off = 0, [0, 0], None

    def before(self):
        v = self.n[self.s]
        return v if self.off is None else self.off + v

    def step(self):
        self.n[self.s] += 1
        self.s ^= 1

    def begin(self, i, per):
        self.base, self.per, self.off, self.s0 = list(self.n), per, i * per, self.s

    def end(self, times):
        assert self.s == self.s0 and all(x - y == self.per for x, y in zip(self.n, self.base))
        self.off, self.n = None, [x + self.per * times for x in self.base]


def build(nc, a, o):
    ctx = ExitStack()
    with ctx:
        def sb(name, shape, dt=F32):
            return ctx.enter_context(nc.sbuf_tensor(name, shape, dt))

        def sem(name):
            return ctx.enter_context(nc.semaphore(name))

        xT = sb("xT", [P, KD, NT])
        hT = sb("hT", [P, KD, NT])
        gates = sb("gates", [P, 2 * KD, NT])
        qkvT = sb("qkvT", [P, 12, NT])
        iqT = sb("iqT", [P, 8, NT])
        ikT = sb("ikT", [P, NT])
        ik2 = sb("ik2", [P, NT])
        uT = sb("uT", [P, 4, NT])
        ring = sb("ring", [P, Stream.SLOTS, 2048])
        mats = sb("mats", [P, 4, P])
        ropes = sb("ropes", [P, 4, NT])
        causal = sb("causal", [P, 2, TP])
        cnew = sb("cnew", [TS, TQ + TS])
        rowsf = sb("rowsf", [TS, 2, P])
        rowsb = sb("rowsb", [TS, 2, P], BF16)
        headsel = sb("headsel", [80, P])
        wmask = sb("wmask", [P, 2 * NB, TS])
        small = sb("small", [R_ALL, P])
        cols = sb("cols", [P, R_ALL])
        convT = sb("convT", [P, 2 * FT, 20])
        tok = sb("tok", [P, 3, 512 + 80])
        sc = sb("sc", [P, 64])
        rstd = sb("rstd", [P, 2, NT])
        pidx = sb("pidx", [P, NB], I32)
        pidf = sb("pidf", [P, NB])
        csub = sb("csub", [P, 1])
        oT = sb("oT", [P, HEADS, NT])
        work = sb("work", [P, 2, 2052])
        pscore = sb("pscore", [P, 2, 2, TP])
        selb = sb("selb", [TS, PAST + TS], BF16)
        ssmv = sb("ssmv", [P, 28, SPAIR])
        cout = sb("cout", [P, 2, FT, 18])

        ident, turn_q, turn_i, ones = (mats[:, k, :] for k in range(4))
        fg = gates[:].rearrange("p k t -> p (k t)")
        fh = hT[:].rearrange("p k t -> p (k t)")
        fr = ring[:].rearrange("p s n -> p (s n)")
        fw = work[:].rearrange("p a n -> p (a n)")
        fq = qkvT[:].rearrange("p k t -> p (k t)")
        ps = ctx.enter_context(nc.psum_tensor("ps", [P, 8, 512], F32))

        landed = [sem(f"weights_landed{s}") for s in range(Stream.SLOTS)]
        used = sem("weights_used")
        out = [sem(f"products_out{s}") for s in range(2)]
        filled = sem("unit_filled")
        freed = [sem(f"unit_freed{s}") for s in range(4)]
        small_ready = sem("small_ready")
        consts_in, x_in, conv_in, small_in = sem("consts_in"), sem("x_in"), sem("conv_in"), sem("small_in")
        table_in, table_ready = sem("table_in"), sem("table_ready")
        idx_in = [sem(f"idx_keys_in{s}") for s in range(2)]
        x_ready = sem("x_transposed")
        squares, squares_used = sem("squares_ready"), sem("squares_used")
        var_ready, rstd_ready = sem("variance_ready"), sem("rstd_ready")
        normed = sem("normed")
        a_out = sem("projections_out")
        head_normed, roped, tok_ready = sem("head_normed"), sem("roped"), sem("tok_ready")
        wb_ready = sem("indexer_weights_ready")
        relu_ready, relu_summed, relu_weighed = sem("relu_ready"), sem("relu_summed"), sem("relu_weighed")
        blk_scored, blk_out = sem("block_scored"), sem("block_out")
        pb_ready = sem("prompt_mask_ready")
        sb_ready = sem("sample_mask_ready")
        ssm_in, ssm_tabs = sem("ssm_in"), sem("ssm_tables_ready")
        trig_in, trig_out = sem("angles_ready"), sem("sines_ready")
        state_ready, state_used = sem("states_ready"), sem("states_used")
        y_ready, z_ready, glu_ready = sem("y_ready"), sem("z_ready"), sem("glu_ready")
        ssm_done, state_out = sem("ssm_done"), sem("state_rows_ready")
        p_max, p_exp, p_norm, p_turned = sem("p_max"), sem("p_exp"), sem("p_norm"), sem("p_turned")
        k_in, v_in = sem("k_in"), [sem(f"v_in{s}") for s in range(2)]
        k_turned, s_scored, s_exp = sem("k_turned"), sem("s_scored"), sem("s_exp")
        s_max, s_norm, s_turned, s_pv = sem("s_max"), sem("s_norm"), sem("s_turned"), sem("s_pv")
        qz_ready, os_ready, o_ready = sem("qz_ready"), sem("os_ready"), sem("o_ready")
        k_used, v_used, s_free = sem("k_used"), sem("v_used"), sem("s_free")
        merged, x_step = sem("merged"), sem("residual_ready")
        ext_ready, conv_ready, gelu_ready = sem("ext_ready"), sem("conv_ready"), sem("gelu_ready")
        act_ready = sem("ffn_act_ready")
        p_in, ple_out, ple_ready, sig_ready = sem("p_in"), sem("ple_out"), sem("ple_ready"), sem("sig_ready")
        y_rows, c_rows = sem("y_rows"), sem("conv_rows")
        vec, sca = sem("vector_steps"), sem("scalar_steps")
        stored, state_stored = sem("stored"), sem("state_rows_stored")
        time_in, samples_ready, finals_ready = sem("time_in"), sem("sample_states_ready"), sem("final_states_ready")
        ple_ready_p, ple_filled = sem("p_transposed"), sem("ple_filled")
        params_in = sem("ssm_params_for_scalar")
        params, pool_steps = sem("ssm_params"), sem("pool_steps")
        act_params = sem("scalar_ssm_params")
        k_filled, k_freed = sem("turn_filled"), [sem("turn_freed_scalar"), sem("turn_freed_vector")]
        pv_done, pv_out = sem("pv_done"), sem("pv_out")
        c_stored, y_stored = [sem(f"conv_rows_stored{s}") for s in range(3)], [sem(f"y_stored{s}") for s in range(2)]
        c_turned, y_turned = sem("conv_rows_turned"), sem("y_turned")
        prompt_o = sem("prompt_attended")

        def fill_wait(pe, m):
            if m >= 4:
                pe.wait_ge(freed[m % 4], m // 4)

        def col(r):
            return cols[:, r:r + 1]

        def rows(tt):
            return P if tt < 2 else TS

        conv_at = [(fw[:, 0:3072], 0, 24), (fg[:, 6144:9216], 24, 24), (fq[:, 0:3072], 48, 24), (fh[:, 0:1792], 72, 14)]
        xn = fg[:, 0:6144].rearrange("p (j n) -> p j n", j=3)
        fo = oT[:].rearrange("p k t -> p (k t)")
        fi = iqT[:].rearrange("p k t -> p (k t)")
        idx_raw = fw[:, 0:4096].rearrange("p (b j n) -> p b j n", b=4, j=8)
        idxT = fg[:, 0:8192].rearrange("p (b n) -> p b n", b=NB)
        qb = fg[:, 8192:9216].rearrange("p (b n) -> p b n", b=NB)
        relu = fo[:, 0:2048].rearrange("p (r n) -> p r n", r=4)
        wheads = wmask[:].rearrange("p (b q) t -> p b (q t)", b=NB)
        nk = sc[:, 0:32].rearrange("p (b t) -> p b t", b=NB)
        m8 = sc[:, 32:40]
        dt_raw = sc[R_DT:R_DT + SPAIR, 0:2]
        bl = fi[:, 0:1024].rearrange("p (q r n) -> p q r n", q=4, r=2)
        cl = fi[:, 1024:2048].rearrange("p (j r c) -> p j r c", j=SPAIR, r=2)
        ini_raw = fi[:, 2048:2304].rearrange("p (r n) -> p r n", r=2)
        bus = fo[:, 0:1024].rearrange("p (r b j t) -> p r b j t", r=2, b=NB, j=SPAIR)
        sst = fo[:, 1024:2048].rearrange("p (r b j t) -> p r b j t", r=2, b=NB, j=SPAIR)
        ini = fo[:, 2048:2304].rearrange("p (r b j) -> p r b j", r=2, b=NB)
        braw = fw[:, 0:512].rearrange("p (r j c) -> p r j c", r=2, j=SPAIR)
        bbd = fw[:, 512:1536].rearrange("p (q r j g c) -> p q r j g c", q=4, r=2, j=4, g=2)
        craw = fw[:, 1536:2560].rearrange("p (q r d n) -> p q r d n", q=4, r=2, d=2)
        btmp = fw[:, 2560:3584].rearrange("p (k j c) -> p k j c", k=4, j=SPAIR)
        angle = fh[:, 0:512]
        rest = [fh[:, 512 + k * 256:768 + k * 256] for k in range(2)]
        trig = [fh[:, 1024 + k * 512:1536 + k * 512] for k in range(2)]
        time = fh[:, 2048:2304]
        dt_ = [fh[:, 2304 + k * 256:2560 + k * 256] for k in range(5)] + [fw[:, 0:256]]
        states = [fh[:, 3584 + k * 512:4096 + k * 512].rearrange("p (r t) -> p r t", r=2) for k in range(2)]
        yt = fh[:, 0:1152].rearrange("p (k t) -> p k t", k=4)
        sg = fh[:, 1152:2304].rearrange("p (k t) -> p k t", k=4)
        rows_out = fw[:, 3712:4096].rearrange("p (r n) -> p r n", r=3)
        psc = [fw[:, 2560 + k * 256:2816 + k * 256] for k in range(2)]
        ppt = [fw[:, 3072 + k * 256:3328 + k * 256].rearrange("p (k t) -> p k t", k=2) for k in range(2)]
        kraw = fh[:, 0:4096].rearrange("p (j n) -> p j n", j=SLOT)
        vraw = [fr[:, k * 4096:(k + 1) * 4096].rearrange("p (j n) -> p j n", j=SLOT) for k in range(2)]
        kT = fr[:, 4096:8192].rearrange("p (g n) -> p g n", g=2)
        qz = fi[:, 0:2048].rearrange("p (b g n) -> p b g n", b=NB, g=2)
        sp_ = fw[:, 0:PAST + TS]
        os_ = fw[0:TS, 2080:2336]
        spT = fq[:, 0:2048].rearrange("p (j n) -> p j n", j=SLOT)
        spN = fq[0:TS, 2048:2176]
        ext = fg[:, 0:1224].rearrange("p (e s n) -> p e s n", e=2, s=2)
        cv = fg[:, 1224:2448].rearrange("p (e s n) -> p e s n", e=2, s=2)
        gl = fg[:, 2448:3060].rearrange("p (e n) -> p e n", e=2)
        taps = fg[:, 3060:3140].rearrange("p (e s n) -> p e s n", e=2, s=2)
        acts = fg[:, 3140:7748].rearrange("p (e k t) -> p e k t", e=2, k=FG)
        pn = fw[:, 0:768].rearrange("p (j n) -> p j n", j=3)
        pT = fw[:, 768:1344].rearrange("p (k t) -> p k t", k=2)
        pl = fg[:, 0:4608].rearrange("p (k t) -> p k t", k=KD)
        sig = fg[:, 4608:5760].rearrange("p (e k t) -> p e k t", e=2, k=2)
        crow = fg[:, 5760:8832].rearrange("p (e n) -> p e n", e=3)
        yrow = fw[:, 0:4096].rearrange("p (e n) -> p e n", e=2)
        C_GLU = 2 + 4 + 8 + 12 + 32
        w_in = a["w_in"][0]
        KC = KD // 2

        def load(sp, st, src, n):
            k = src.shape[0] // P
            if st.off is not None or st.c >= st.SLOTS:
                sp.wait_ge(used, st.count() - st.SLOTS)
            sp.dma_start(ring[:, st.slot(), 0:k * n].rearrange("p (k n) -> p k n", n=n),
                         src.rearrange("(k p) n -> p k n", p=P)).then_inc(landed[st.slot()], 16)
            st.c += 1

        def load_pair(sp, st, w, c0, width=256):
            for kc in range(2):
                load(sp, st, w[kc * KC * P:(kc + 1) * KC * P, bass.ds(c0, width)], width)

        def products(pe, st, pr, rhs, widths, chunks=2, kt=KC):
            if pr.off is not None or pr.n[pr.s] > 0:
                pe.wait_ge(out[pr.s], pr.before())
            for kc in range(chunks):
                pe.wait_ge(landed[st.slot()], st.landed())
                w = ring[:, st.slot(), 0:kt * sum(widths)].rearrange("p (k n) -> p k n", k=kt)
                for n, width in enumerate(widths):
                    for k in range(kt):
                        mm = nc.tensor.matmul(ps[0:width, 2 * pr.s + n, 0:NT], w[:, k, n * P:n * P + width],
                                              rhs[:, kc * kt + k, :], start=(kc == 0 and k == 0),
                                              stop=(kc == chunks - 1 and k == kt - 1))
                mm.then_inc(used, 1)
                st.c += 1
            pr.step()

        def taken(eng, st, pr, chunks=2):
            s = pr.s
            eng.wait_ge(used, st.count(chunks - 1))
            st.c += chunks
            pr.step()
            return ps[:, 2 * s:2 * s + 2, 0:NT], out[s]

        def walk(st, pr, name):
            pairs, chunks = {"ikw": (1, 2), "u": (2, 2), "iq": (4, 2), "qkv": (6, 2), "gates": (16, 2),
                             "glu": (2, 1), "w_o": (8, 2)}[name]
            for _ in range(pairs):
                st.c += chunks
                pr.step()

        block = ctx.enter_context(nc.Block())

        def ffn(eng, st, pr, up, down, more=()):
            counted = ((st, 48),) + (((pr, 16),) if pr else ()) + tuple(more)
            for j in range(FG):
                up(j, 0, j)
            with eng.Fori(0, 2) as i:
                for x, per in counted:
                    x.begin(i, per)
                for gg in range(2):
                    for j in range(FG):
                        up(i * 16 + (FG * (1 + gg) + j), (1 + gg) % 2, j)
                    down(i * 16 + FG * gg, gg, FG)
            for x, _ in counted:
                x.end(2)
            for j in range(FT - 5 * FG):
                up(5 * FG + j, 1, j)
            down(4 * FG, 0, FG)
            down(5 * FG, 1, FT - 5 * FG)

        @block.sync
        def _(sp):
            st = Stream()
            for dst, src in ((mats[:], a["c_mats"]), (ropes[:], a["c_rope"]), (causal[:], a["c_causal"]),
                             (cnew[:], a["c_new"]), (rowsf[:], a["c_rows"]), (headsel[:], a["c_heads"]),
                             (wmask[:], a["c_wmask"]), (csub[:], a["c_sub"])):
                sp.dma_start(dst, src).then_inc(consts_in, 16)
            for j in range(2):
                sp.dma_start(xn[:, j, :], a["x_prompt"][0, j * P:(j + 1) * P, :]).then_inc(x_in, 16)
            sp.dma_start(xn[0:TS, 2, :], a["x_sample"].rearrange("b t d -> (b t) d")).then_inc(x_in, 16)
            for r, n, src in ((R_MIX, 16, "g_mix"), (R_FFN, 16, "g_ffn"), (R_PG, 16, "g_pg"), (R_PLE, 16, "g_ple"),
                              (R_GQ, 1, "g_q"), (R_GK, 1, "g_k"), (R_D, 4, "ssm_d")):
                sp.dma_start(small[r:r + n, :], a[src][0].rearrange("(k p) -> k p", p=P)).then_inc(small_in, 16)
            for r, src in ((R_ARE, "ssm_a_re"), (R_AIM, "ssm_a_im")):
                sp.dma_start(small[r:r + SPAIR, :], a[src][0].rearrange("(j g) n -> j (g n)", g=2)).then_inc(small_in, 16)
            sp.dma_start(dt_raw, a["ssm_log_dt"][0].rearrange("(j g) -> j g", g=2)).then_inc(small_in, 16)
            for dst, t0, n in conv_at:
                w = slice(t0 * P, (t0 + n) * P)
                sp.dma_start(dst[0:16, 0:n * P], a["state_conv"][0].rearrange("b r n -> (b r) n")[:, w]).then_inc(conv_in, 16)
                sp.dma_start(dst[16:19, 0:n * P], a["conv_w"][0][:, w]).then_inc(conv_in, 16)
                sp.dma_start(dst[19:20, 0:n * P], a["conv_b"][:, w]).then_inc(conv_in, 16)
            for kc in range(2):
                load(sp, st, w_in[kc * KC * P:(kc + 1) * KC * P, C_IK:C_U], C_U - C_IK)
            for n in range(2):
                load_pair(sp, st, w_in, C_U + n * 256)
            for c0, times in ((C_IQ, 2), (C_Q, 3), (C_GA, 8)):
                with sp.Fori(0, times) as i:
                    st.begin(i, 4)
                    for n in range(2):
                        load_pair(sp, st, w_in, i * 512 + (c0 + n * 256))
                st.end(times)
                if c0 == C_Q:
                    sp.wait_ge(tok_ready, 6)
                    for tt in range(3):
                        n = rows(tt)
                        g = "prompt" if tt < 2 else "sample"
                        r0 = tt * P if tt < 2 else 0
                        for name, lo, w in (("k", 0, 256), ("v", 256, 256), ("idx_k", 512, 64)):
                            sp.dma_start(o[f"{name}_{g}"][r0:r0 + n, :], tok[0:n, tt, lo:lo + w]).then_inc(stored, 16)
            sp.wait_ge(sb_ready, 1)
            for r, part in enumerate(("re", "im")):
                sp.dma_start(braw[:, r], a[f"ssm_b_{part}"][0].rearrange("(j g) n c -> (g n) j c", g=2)).then_inc(ssm_in, 16)
                for d in range(2):
                    sp.dma_start(craw[:, :, r, d, :], a[f"ssm_c_{part}"][0].rearrange("(q r) c n -> (r c) q n", r=8)).then_inc(ssm_in, 16)
                sp.dma_start(ini_raw[:, r], a[f"state_ssm_{part}"][0].rearrange("b (j g) n -> (b j) (g n)", g=2)).then_inc(ssm_in, 16)
            sp.wait_ge(used, C_GLU)
            sp.dma_start(time, a["c_time"]).then_inc(time_in, 16)
            for n in range(2):
                load(sp, st, a["w_glu"][0][:, n * 256:(n + 1) * 256], 256)
            sp.wait_ge(state_out, 2)
            for r, part in enumerate(("re", "im")):
                sp.dma_start(o[f"ssm_{part}_prompt"], rows_out[r * SPAIR:(r + 1) * SPAIR, 0, :]).then_inc(state_stored, 16)
                sp.dma_start(o[f"ssm_{part}_sample"], rows_out[:, 1 + r, :]).then_inc(state_stored, 16)
            sp.wait_ge(o_ready, 2)
            with sp.Fori(0, 4) as i:
                st.begin(i, 4)
                for n in range(2):
                    c = bass.ds(i * 512 + n * 256, 256)
                    load(sp, st, a["w_att_br"][0][:, c], 256)
                    load(sp, st, a["w_ssm_br"][0][:, c], 256)
            st.end(4)
            with sp.Fori(0, 4) as i:
                st.begin(i, 4)
                for n in range(2):
                    load_pair(sp, st, a["w_o"][0], i * 512 + n * 256)
            st.end(4)

            def load_up(t):
                for half in range(2):
                    load(sp, st, a["w_up"][0][:, bass.ds(t * P + half * FF, P)], P)

            def load_down(t, k):
                for n in range(8):
                    load(sp, st, a["w_down"][0][bass.ds(t * P, k * P), n * 256:(n + 1) * 256], 256)

            ffn(sp, st, None, lambda t, g, j: load_up(t), lambda t, g, k: load_down(t, k))
            sp.wait_ge(act_ready, FT)
            for j in range(3):
                src = a["p_prompt"][0, 0, j * P:(j + 1) * P, :] if j < 2 else a["p_sample"][0].rearrange("b t n -> (b t) n")
                sp.dma_start(pn[0:rows(j), j, :], src).then_inc(p_in, 16)
            for n in range(2):
                load(sp, st, a["w_ple"][0][:, n * 1024:(n + 1) * 1024], 1024)
            with sp.Fori(0, 4) as i:
                st.begin(i, 4)
                for n in range(2):
                    load_pair(sp, st, a["w_pg"][0], i * 512 + n * 256)
            st.end(4)
            for j in range(3):
                sp.wait_ge(y_turned, 4 * (j + 1))
                dst = o["y_prompt"][j * P:(j + 1) * P, :] if j < 2 else o["y_sample"]
                sp.dma_start(dst, yrow[0:rows(j), j % 2, :]).then_inc(y_stored[j % 2], 16)
            sp.wait_ge(stored, 9 * 16)
            sp.wait_ge(state_stored, 4 * 16)
            for s in range(3):
                sp.wait_ge(c_stored[s], 32 * ((11 - s + 2) // 3))
            for s in range(2):
                sp.wait_ge(y_stored[s], 16 * (2 - s))

        @block.gpsimd
        def _(pool):
            for b in range(NB):
                pool.dma_start(pidx[:, b:b + 1], a["page_table"][b].unsqueeze(1).unsqueeze(1).to_broadcast([NPAGE, 8, 1])).then_inc(table_in, 16)
            pool.wait_ge(table_ready, 1)
            rows16 = a["cache_idx_k"][0].rearrange("n (r j) d -> (n r) (j d)", j=SLOT)
            pool.wait_ge(freed[0], 1)
            for b in range(NB):
                if b == 4:
                    pool.wait_ge(filled, UNITS["idx"] + 8)
                nc.gpsimd.indirect_dma_start(fw[:, b % 4 * 1024:(b % 4 + 1) * 1024], None, rows16,
                                             bass.IndirectOffsetOnAxis(ap=pidx[:, b:b + 1], axis=0)
                                             ).then_inc(idx_in[b // 4], 16)

            pl_ = Steps(pool, pool_steps)
            G = nc.gpsimd
            x, r = rest
            pool.wait_ge(params, 1)
            pool.wait_ge(time_in, 16)
            for j in range(SPAIR):
                fa, fb = ssmv[:, 8, j:j + 1], ssmv[:, 9, j:j + 1]
                pl_.link(G.tensor_scalar(x, time, fa, None, ALU.mult))
                pl_.link(G.tensor_scalar(r, x, MAGIC, MAGIC, ALU.add, ALU.subtract))
                pl_.link(G.tensor_tensor(x, x, r, ALU.subtract))
                pl_.link(G.tensor_scalar(r, time, fb, None, ALU.mult))
                pl_.link(G.tensor_tensor(x, x, r, ALU.add))
                if j:
                    pool.wait_ge(trig_out, j)
                for half, shift in ((0, 0.0), (1, 0.25)):
                    y = angle[:, half * 256:half * 256 + 256]
                    if shift:
                        pl_.link(G.tensor_scalar(x, x, shift, None, ALU.add))
                    pl_.link(G.tensor_scalar(r, x, MAGIC, MAGIC, ALU.add, ALU.subtract))
                    pl_.link(G.tensor_tensor(y, x, r, ALU.subtract))
                    ins = G.tensor_scalar(y, y, HALF, -HALF, ALU.min, ALU.max)
                    if shift:
                        ins.then_inc(trig_in, 1)
                    else:
                        pl_.link(ins)
            rows_k = a["cache_k"][0].rearrange("n (r j) g d -> (n r) (j g d)", j=SLOT)
            rows_v = a["cache_v"][0].rearrange("n (r j) g d -> (n r) (j g d)", j=SLOT)
            pool.wait_ge(glu_ready, 1)

            def gather(dst, src, b, done):
                G.indirect_dma_start(dst, None, src, bass.IndirectOffsetOnAxis(ap=pidx[:, b:b + 1], axis=0)).then_inc(done, 16)

            for half in range(2):
                for b in range(4 * half, 4 * half + 4):
                    if b:
                        pool.wait_ge(k_used, b)
                    gather(fh[:, 0:4096], rows_k, b, k_in)
                for b in range(4 * half, 4 * half + 4):
                    if b >= 2:
                        pool.wait_ge(pv_done, b - 1)
                    if b == 4 * half + 1:
                        pool.wait_ge(s_scored, half + 1)
                    gather(fr[:, b % 2 * 4096:(b % 2 + 1) * 4096], rows_v, b, v_in[b % 2])

            for n in range(11):
                pool.wait_ge(c_turned, min(2 * n + 2, 22))
                w = min(1024, 2 * FF - n * 1024)
                pool.dma_start(o["conv_prompt"][:, n * 1024:n * 1024 + w], crow[0:2, n % 3, 0:w]).then_inc(c_stored[n % 3], 16)
                pool.dma_start(o["conv_sample"][:, n * 1024:n * 1024 + w], crow[2:18, n % 3, 0:w]).then_inc(c_stored[n % 3], 16)

        @block.scalar
        def _(act):
            st, pr = Stream(), Pairs()
            sq = fo.rearrange("p (s n) -> p s n", s=2)

            def square_x(base):
                for q in range(4):
                    if q >= 2:
                        act.wait_ge(squares_used, base + q - 1)
                    nc.scalar.activation(sq[:, q % 2, :], xT[:, 4 * q:4 * q + 4, :].rearrange("p k t -> p (k t)"),
                                         ACT.Square).then_inc(squares, 1)

            def root(n, x):
                act.wait_ge(var_ready, n)
                nc.scalar.activation(x, x, ACT.Sqrt).then_inc(rstd_ready, 1)

            act.wait_ge(x_ready, 12)
            square_x(0)
            root(1, rstd[:, 0, :])
            for name in ("ikw", "u", "iq", "qkv"):
                walk(st, pr, name)
            act.wait_ge(a_out, 4)
            for j in range(12):
                if j < 10:
                    if j >= 4:
                        act.wait_ge(squares_used, 4 + j - 3)
                    nc.scalar.activation(oT[:, j % 4, :], qkvT[:, j, :], ACT.Square).then_inc(squares, 1)
                if j >= 2:
                    root(j, oT[:, 4 + (j - 2) % 4, :])
            act.wait_ge(x_ready, 12)
            for n in range(16):
                m = UNITS["idx"] + n
                act.wait_ge(filled, m + 1)
                nc.scalar.copy(idxT[:, n // 2, n % 2 * 512:(n % 2 + 1) * 512], ps[:, bank(m), :]).then_inc(freed[m % 4], 1)
            act.wait_ge(squares_used, 14)
            for n in range(16 + 24):
                m = UNITS["pidx"] + n
                w = 512 if n < 32 else TQ
                act.wait_ge(filled, m + 1)
                if 4 <= n < 20:
                    act.wait_ge(relu_summed, n - 3)
                elif n >= 20:
                    act.wait_ge(relu_weighed, n - 19)
                nc.scalar.activation(relu[:, n % 4, 0:w], ps[:, bank(m), 0:w], ACT.Relu).then_inc(freed[m % 4], 1)
                act.wait_ge(freed[m % 4], m // 4 + 1)
                act.sem_inc(relu_ready, 1)
            with act.Fori(0, 8) as i:
                st.begin(i, 4)
                pr.begin(i, 1)
                for n in range(2):
                    src, free = taken(act, st, pr)
                    nc.scalar.activation(gates[:, bass.ds(i * 4 + 2 * n, 2), :], src, ACT.Sigmoid).then_inc(free, 1)
            st.end(8)
            pr.end(8)


            nc.scalar.activation(ssmv[:, 0, :], cols[:, R_DT:R_DT + SPAIR], ACT.Exp).then_inc(act_params, 1)
            act.wait_ge(params_in, 1)
            nc.scalar.activation(ssmv[:, 3, :], ssmv[:, 1, :], ACT.Exp).then_inc(act_params, 1)
            act.wait_ge(params_in, 2)
            nc.scalar.activation(ssmv[:, 12:14, :], ssmv[:, 10:12, :], ACT.Sin, scale=TURN).then_inc(act_params, 1)
            for j in range(SPAIR):
                act.wait_ge(trig_in, j + 1)
                if j >= 2:
                    act.wait_ge(state_ready, j - 1)
                nc.scalar.activation(trig[j % 2], angle, ACT.Sin, scale=TURN).then_inc(trig_out, 1)
            for q in range(4):
                act.wait_ge(y_ready, q + 1)
                nc.scalar.activation(uT[:, q, :], yt[:, q, :], ACT.Gelu_apprx_tanh).then_inc(z_ready, 1)
            for n in range(2):
                src, free = taken(act, st, pr, 1)
                nc.scalar.activation(sg[:, 2 * n:2 * n + 2, :], src, ACT.Sigmoid).then_inc(free, 1)
            U = UNITS["pa"]
            scale = HD ** -0.5
            for i in range(16):
                act.wait_ge(p_max, i + 1)
                w = P * (i % 2 + 1)
                nc.scalar.activation(psc[i % 2][:, 0:w], psc[i % 2][:, 0:w], ACT.Exp, bias=sc[:, 2 + i % 2:3 + i % 2], scale=scale,
                                     accum_out=sc[:, 4 + i % 2:5 + i % 2]).then_inc(p_exp, 1)
                m = U + 3 * i + 2 - (i == 15)
                act.wait_ge(filled, m + 1)
                if i >= 2:
                    act.wait_ge(filled, U + 3 * (i - 2) + 4)
                nc.scalar.copy(ppt[i % 2][:, 0:w // P, :], ps[:, bank(m), 0:w].rearrange("p (k t) -> p k t", t=P)).then_inc(freed[m % 4], 1)
                act.wait_ge(freed[m % 4], m // 4 + 1)
                act.sem_inc(p_turned, 1)
            kk = Turns()

            def turn(dst, src):
                k = kk.next()
                if k % 2 == 0:
                    act.wait_ge(k_filled, k + 1)
                    nc.scalar.copy(dst, src(k % 2)).then_inc(k_freed[0], 1)

            for half in range(2):
                for b in range(4 * half, 4 * half + 4):
                    if b:
                        act.wait_ge(s_free, b)
                    if b == 4:
                        act.wait_ge(pv_done, 4)
                    for n in range(8):
                        turn(kT[:, n // 4, n % 4 * 512:n % 4 * 512 + 512], lambda s: ps[:, s, :])
                act.wait_ge(s_max, half + 1)
                nc.scalar.activation(sp_[:, 0:PAST], ps[:, 4:8, :].rearrange("p k n -> p (k n)"), ACT.Exp, bias=sc[:, 11:12],
                                     scale=scale, accum_out=sc[:, 12:13]).then_inc(s_exp, 1)
                nc.scalar.activation(sp_[:, PAST:PAST + TS], ps[:, 3, 0:TS], ACT.Exp, bias=sc[:, 11:12],
                                     scale=scale, accum_out=sc[:, 13:14]).then_inc(s_exp, 1)
                for n in range(4):
                    turn(spT[:, 4 * n:4 * n + 4, :], lambda s: ps[:, s, :].rearrange("p (j n) -> p j n", j=4))
                turn(spN, lambda s: ps[0:TS, s, 0:P])
                for b in range(4 * half, 4 * half + 4):
                    t0 = TP + b * TQ
                    for g in range(2):
                        if g:
                            kk.k -= 1
                        k = kk.next()
                        if k % 2 == 0:
                            act.wait_ge(k_filled, k + 1)
                            ins = nc.scalar.copy(oT[:, g * 4:g * 4 + 4, t0:t0 + TQ],
                                                 ps[:, 0, g * 48:g * 48 + 16].rearrange("p (r t) -> p r t", t=TQ))
                            if g:
                                ins.then_inc(k_freed[0], 1)
            act.wait_ge(k_freed[0], (kk.k + 1) // 2)
            act.sem_inc(o_ready, 1)
            st.c += 16
            walk(st, pr, "w_o")
            act.wait_ge(x_step, 1)
            square_x(14)
            root(12, rstd[:, 0, :])

            def up(t, g, j):
                s, e = pr.s, pr.s
                act.wait_ge(used, st.count(1))
                if pr.off is not None or j >= 2 or g:
                    act.wait_ge(conv_ready, t - 1)
                src = ps[:, 2 * s:2 * s + 2, :]
                nc.scalar.copy(ext[:, e, :, 2:2 + TP], src[:, :, 0:TP])
                nc.scalar.copy(ext[:, e, :, EXT_S:EXT].rearrange("p s (b t) -> p s b t", b=NB)[:, :, :, 2:2 + TQ],
                               src[:, :, TP:NT].rearrange("p s (b t) -> p s b t", b=NB)).then_inc(out[s], 1)
                act.wait_ge(out[s], pr.before() + 1)
                act.sem_inc(ext_ready, 1)
                st.c += 2
                pr.step()
                act.wait_ge(conv_ready, t + 1)
                nc.scalar.activation(gl[:, e, 0:CONVN], cv[:, e, 0, 0:CONVN], ACT.Gelu_apprx_tanh).then_inc(gelu_ready, 1)

            def skip_down(t, g, k):
                for _ in range(8):
                    st.c += 1
                    pr.step()

            act.wait_ge(x_step, 1)
            ffn(act, st, pr, up, skip_down)
            act.wait_ge(x_step, 2)
            square_x(18)
            root(13, rstd[:, 0, :])
            act.wait_ge(ple_out, 8)
            for q in range(4):
                if q >= 2:
                    act.wait_ge(squares_used, 22 + q - 1)
                nc.scalar.activation(sq[:, q % 2, :], pl[:, 4 * q:4 * q + 4, :].rearrange("p k t -> p (k t)"),
                                     ACT.Square).then_inc(squares, 1)
            root(14, rstd[:, 1, :])
            for _ in range(8):
                pr.step()
            st.c += 2
            with act.Fori(0, 4) as i:
                st.begin(i, 4)
                pr.begin(i, 1)
                for n in range(2):
                    src, free = taken(act, st, pr)
                    act.wait_ge(ple_ready, i * 2 + (1 + n))
                    nc.scalar.activation(sig[:, n, :, :], src, ACT.Sigmoid).then_inc(free, 1)
                    act.wait_ge(free, pr.n[pr.s ^ 1] + i)
                    act.sem_inc(sig_ready, 1)
            st.end(4)
            pr.end(4)

        @block.vector
        def _(ve):
            st, pr = Stream(), Pairs()
            v = Steps(ve, vec)
            V = nc.vector

            def evac(m, dst, src):
                ve.wait_ge(filled, m + 1)
                V.tensor_copy(dst, src).then_inc(freed[m % 4], 1)

            def norm_x(m, nth, row):
                ve.wait_ge(filled, m + 1)
                V.tensor_scalar(rstd[:, 0, :], ps[:, bank(m), 0:NT], 1.0 / D, EPS, ALU.mult, ALU.add).then_inc(freed[m % 4], 1)
                ve.wait_ge(freed[m % 4], m // 4 + 1)
                ve.sem_inc(var_ready, 1)
                ve.wait_ge(rstd_ready, nth)
                v.link(V.reciprocal(rstd[:, 0, :], rstd[:, 0, :]))
                for k in range(KD):
                    ins = V.scalar_tensor_tensor(hT[:, k, :], xT[:, k, :], col(row + k), rstd[:, 0, :], ALU.mult, ALU.mult)
                ins.then_inc(normed, 1)

            ve.wait_ge(small_in, 160)
            V.tensor_copy(small[R_DT:R_DT + SPAIR, :].rearrange("j (g n) -> j g n", g=2),
                          dt_raw.unsqueeze(2).to_broadcast([SPAIR, 2, N_SSM])).then_inc(small_ready, 1)
            for n, (_, t0, k) in enumerate(conv_at):
                m = UNITS["conv"] + n
                evac(m, convT[:, t0:t0 + k, :], ps[:, bank(m), 0:k * 20].rearrange("p (k r) -> p k r", r=20))
            m = UNITS["small"]
            evac(m, cols[:], ps[:, bank(m), 0:R_ALL])
            for n in range(12):
                m, j, q = UNITS["x"] + n, n // 4, n % 4
                w = rows(j)
                ve.wait_ge(filled, m + 1)
                V.tensor_copy(xT[:, 4 * q:4 * q + 4, j * P:j * P + w],
                              ps[:, bank(m), 0:4 * w].rearrange("p (k t) -> p k t", k=4)).then_inc(freed[m % 4], 1)
                ve.wait_ge(freed[m % 4], m // 4 + 1)
                ve.sem_inc(x_ready, 1)
            norm_x(UNITS["norm0"], 1, R_MIX)
            ve.wait_ge(table_in, 128)
            ve.wait_ge(consts_in, 128)
            v.link(V.tensor_scalar(pidf[:], pidx[:], 8.0, csub[:, 0:1], ALU.mult, ALU.add))
            V.tensor_copy(pidx[:], pidf[:]).then_inc(table_ready, 1)

            ve.wait_ge(used, st.count(1))
            V.tensor_copy(ikT[0:80, :], ps[0:80, 0, 0:NT]).then_inc(out[0], 1)
            st.c += 2
            pr.step()
            for n in range(2):
                src, free = taken(ve, st, pr)
                V.tensor_copy(uT[:, 2 * n:2 * n + 2, :], src).then_inc(free, 1)
            for dst, times in ((iqT, 2), (qkvT, 3)):
                with ve.Fori(0, times) as i:
                    st.begin(i, 4)
                    pr.begin(i, 1)
                    for n in range(2):
                        src, free = taken(ve, st, pr)
                        V.tensor_copy(dst[:, bass.ds(i * 4 + 2 * n, 2), :], src).then_inc(free, 1)
                st.end(times)
                pr.end(times)
            for s in range(2):
                ve.wait_ge(out[s], pr.n[s])
                ve.sem_inc(a_out, 2)

            for j in range(12):
                if j < 10:
                    m = UNITS["qkn"] + j
                    ve.wait_ge(filled, m + 1)
                    if j >= 4:
                        ve.wait_ge(head_normed, j - 3)
                    V.tensor_scalar(oT[:, 4 + j % 4, :], ps[:, bank(m), 0:NT], 1.0 / HD, EPS, ALU.mult,
                                    ALU.add).then_inc(freed[m % 4], 1)
                    ve.wait_ge(freed[m % 4], m // 4 + 1)
                    ve.sem_inc(var_ready, 1)
                if j >= 2:
                    k = j - 2
                    ve.wait_ge(rstd_ready, 2 + k)
                    v.link(V.reciprocal(oT[:, 4 + k % 4, :], oT[:, 4 + k % 4, :]))
                    V.scalar_tensor_tensor(qkvT[:, k, :], qkvT[:, k, :], col(R_GQ if k < 8 else R_GK), oT[:, 4 + k % 4, :],
                                           ALU.mult, ALU.mult).then_inc(head_normed, 1)
            ve.wait_ge(head_normed, 10)

            def rope(m, x, cos, sin, n=P):
                ve.wait_ge(filled, m + 1)
                V.tensor_tensor(rstd[0:n, 0, :], x, ropes[0:n, cos, :], ALU.mult)
                v.link(V.tensor_tensor(rstd[0:n, 1, :], ps[0:n, bank(m), 0:NT], ropes[0:n, sin, :], ALU.mult))
                V.tensor_tensor(x, rstd[0:n, 0, :], rstd[0:n, 1, :], ALU.add).then_inc(freed[m % 4], 1)
                ve.wait_ge(freed[m % 4], m // 4 + 1)
                ve.sem_inc(roped, 1)

            for j in range(10):
                rope(UNITS["ropeq"] + j, qkvT[:, j, :], 0, 1)
            for j in range(8):
                rope(UNITS["ropei"] + j, iqT[:, j, :], 2, 3)
            rope(UNITS["ropei"] + 8, ikT[0:IDIM, :], 2, 3, IDIM)
            V.tensor_copy(ik2[0:IDIM, :], ikT[0:IDIM, :])
            v.link(V.tensor_copy(ik2[IDIM:P, :], ikT[0:IDIM, :]))
            v.mark(V.memset(qb, 0.0))
            v.link(V.memset(nk, 0.0))
            for j2 in range(2):
                for hp in range(2):
                    for b in range(NB):
                        t0 = TP + b * TQ
                        dst = qb[j2 * 64:j2 * 64 + 64, b, j2 * 64:j2 * 64 + 64].rearrange("p (h q t) -> p h q t", q=2, t=TQ)
                        v.mark(V.tensor_copy(dst[:, :, hp, :], iqT[hp * 64:hp * 64 + 64, :, t0:t0 + TQ]))
            v.link(V.tensor_copy(nk[0:IDIM], ikT[0:IDIM, TP:NT].rearrange("p (b t) -> p b t", t=TQ)))
            for n in range(6):
                m, tt = UNITS["tok"] + n, n // 2
                w, lo, hi = rows(tt), (0, 512)[n % 2], (512, 592)[n % 2]
                evac(m, tok[0:w, tt, lo:hi], ps[0:w, bank(m), 0:hi - lo])
                ve.wait_ge(freed[m % 4], m // 4 + 1)
                ve.sem_inc(tok_ready, 1)
            m = UNITS["wb"]
            ve.wait_ge(filled, m + 1)
            V.tensor_tensor(wmask[:], ps[:, bank(m), 0:TS].unsqueeze(1).to_broadcast([P, 2 * NB, TS]), wmask[:],
                            ALU.mult).then_inc(freed[m % 4], 1)
            ve.wait_ge(freed[m % 4], m // 4 + 1)
            ve.sem_inc(wb_ready, 1)

            for tt in range(2):
                s = pscore[:, tt, 0, :]
                for i in range(4):
                    for par in range(2):
                        n = tt * 8 + i * 2 + par
                        ve.wait_ge(relu_ready, n + 1)
                        for k in range(2):
                            h = 2 * (2 * i + k) + par
                            src, wt = relu[:, n % 4, k * 256:k * 256 + 256], tok[:, tt, 576 + h:577 + h]
                            if i == par == k == 0:
                                v.link(V.tensor_scalar(s, src, wt, None, ALU.mult))
                            else:
                                v.link(V.scalar_tensor_tensor(s, src, wt, s, ALU.mult, ALU.add))
                        ve.sem_inc(relu_summed, 1)
                v.link(V.tensor_tensor(s, s, causal[:, tt, :], ALU.add))
            S0, S1 = work[0:TS, 0, :], work[0:TS, 1, :]
            slots = S0[:, 0:PAST].rearrange("r (p j q) -> r q j p", j=8, q=2)
            for blk in range(2):
                ve.wait_ge(blk_scored, blk + 1)
                for q in range(2):
                    V.tensor_copy(slots[:, q, 4 * blk:4 * blk + 4, :],
                                  ps[q * TS:(q + 1) * TS, blk, :].rearrange("r (j p) -> r j p", j=4)).then_inc(blk_out, 1)
            ve.wait_ge(blk_scored, 3)
            V.tensor_tensor(S0[:, PAST:PAST + TQ], ps[0:TS, 2, 0:TQ], cnew[:, 0:TQ], ALU.add).then_inc(blk_out, 1)
            ve.wait_ge(blk_out, 5)

            def top(src, dst, k):
                for r in range(k // 8):
                    v.link(V.max(m8[0:src.shape[0]], src if r == 0 else dst))
                    v.link(V.match_replace(dst, m8[0:src.shape[0]], src if r == 0 else dst, TAKEN))

            for tt in range(2):
                s, left = pscore[:, tt, 0, :], pscore[:, tt, 1, :]
                top(s, left, TOPK_P)
                v.link(V.tensor_scalar(left, left, TAKEN / 1.5, OFF, ALU.is_ge, ALU.mult))
                V.tensor_tensor(left, left, causal[:, tt, :], ALU.add).then_inc(pb_ready, 1)
            top(S0, S1, TOPK_S)
            V.tensor_scalar(selb[:, 0:PAST].rearrange("r (j p) -> r j p", j=SLOT),
                            S1[:, 0:PAST].rearrange("r (p j) -> r j p", j=SLOT), TAKEN / 1.5, OFF, ALU.is_ge, ALU.mult)
            v.link(V.tensor_scalar(sc[0:TS, 40:44], S1[:, PAST:PAST + TQ], TAKEN / 1.5, OFF, ALU.is_ge, ALU.mult))
            V.tensor_tensor(selb[:, PAST:PAST + TS].rearrange("r (b t) -> r b t", t=TQ),
                            sc[0:TS, 40:44].unsqueeze(1).to_broadcast([TS, NB, TQ]),
                            cnew[:, TQ:TQ + TS].rearrange("r (b t) -> r b t", t=TQ), ALU.add).then_inc(sb_ready, 1)

            v.link(V.tensor_copy(rowsb[:], rowsf[:]))
            for name in ("gates",):
                walk(st, pr, name)

            def q_(k):
                return ssmv[:, k, :]

            are, aim = cols[:, R_ARE:R_ARE + SPAIR], cols[:, R_AIM:R_AIM + SPAIR]

            def tt(d, x, y, op):
                v.link(V.tensor_tensor(d, x, y, op))

            ve.wait_ge(act_params, 1)
            v.link(V.tensor_tensor(q_(1), are, q_(0), ALU.mult))
            ve.sem_inc(params_in, 1)
            tt(q_(2), aim, q_(0), ALU.mult)
            v.link(V.tensor_scalar(q_(4), q_(2), 1.0 / TURN, MAGIC, ALU.mult, ALU.add))
            v.link(V.tensor_scalar(q_(4), q_(4), MAGIC, None, ALU.subtract))
            v.link(V.scalar_tensor_tensor(q_(5), q_(4), -TURN_HI, q_(2), ALU.mult, ALU.add))
            v.link(V.scalar_tensor_tensor(q_(5), q_(4), -TURN_LO, q_(5), ALU.mult, ALU.add))
            v.link(V.tensor_scalar(q_(6), q_(5), 1.0 / TURN, None, ALU.mult))
            v.link(V.tensor_scalar(q_(8), q_(6), COARSE, COARSE, ALU.add, ALU.subtract))
            v.link(V.scalar_tensor_tensor(q_(7), q_(8), -TURN_HI, q_(5), ALU.mult, ALU.add))
            v.link(V.scalar_tensor_tensor(q_(7), q_(8), -TURN_LO, q_(7), ALU.mult, ALU.add))
            v.link(V.tensor_scalar(q_(9), q_(7), 1.0 / TURN, None, ALU.mult))
            ve.sem_inc(params, 1)
            for k, shift in ((10, 0.0), (11, 0.25)):
                v.link(V.tensor_scalar(q_(k), q_(6), shift, None, ALU.add))
                v.link(V.tensor_scalar(q_(4), q_(k), MAGIC, MAGIC, ALU.add, ALU.subtract))
                tt(q_(k), q_(k), q_(4), ALU.subtract)
                v.link(V.tensor_scalar(q_(k), q_(k), HALF, -HALF, ALU.min, ALU.max))
            ve.sem_inc(params_in, 1)
            tt(q_(4), are, are, ALU.mult)
            tt(q_(5), aim, aim, ALU.mult)
            tt(q_(4), q_(4), q_(5), ALU.add)
            v.link(V.reciprocal(q_(18), q_(4)))
            ve.wait_ge(act_params, 3)
            tt(q_(14), q_(3), q_(13), ALU.mult)
            tt(q_(15), q_(3), q_(12), ALU.mult)
            v.link(V.tensor_scalar(q_(4), q_(14), -1.0, None, ALU.add))
            tt(q_(5), q_(4), are, ALU.mult)
            tt(q_(6), q_(15), aim, ALU.mult)
            tt(q_(5), q_(5), q_(6), ALU.add)
            tt(q_(16), q_(5), q_(18), ALU.mult)
            tt(q_(5), q_(15), are, ALU.mult)
            tt(q_(6), q_(4), aim, ALU.mult)
            tt(q_(5), q_(5), q_(6), ALU.subtract)
            tt(q_(17), q_(5), q_(18), ALU.mult)
            ve.wait_ge(ssm_in, 16 * 8)
            v.link(V.memset(bbd, 0.0))
            v.mark(V.memset(cl, 0.0))
            f = [q_(k).unsqueeze(2).to_broadcast([P, SPAIR, C_SSM]) for k in (16, 17)]
            for k, (x, y) in enumerate(((0, 0), (1, 1), (0, 1), (1, 0))):
                v.mark(V.tensor_tensor(btmp[:, k], f[x], braw[:, y], ALU.mult))
            v.wait()
            for g in range(2):
                r = slice(64 * g, 64 * g + 64)
                for ri, op in ((0, ALU.subtract), (1, ALU.add)):
                    x, y = (btmp[r, 2 * ri + k].rearrange("p (q j) c -> p q j c", q=4) for k in range(2))
                    ins = V.tensor_tensor(bbd[r, :, ri, :, g, :], x, y, op)
                    v.mark(ins)
            v.wait()
            ve.sem_inc(ssm_tabs, 1)
            for n in range(2):
                m = UNITS["bt"] + n
                evac(m, bl[:, 2 * n:2 * n + 2], ps[:, bank(m), :].rearrange("p (q r n) -> p q r n", q=2, r=2))
            for n in range(2):
                m = UNITS["ct"] + n
                ve.wait_ge(filled, m + 1)
                src = ps[:, bank(m), :].rearrange("p (q r j g c) -> p q r j g c", q=2, r=2, j=4, g=2)
                for g in range(2):
                    p_ = slice(64 * g, 64 * g + 64)
                    for ri in range(2):
                        for q in range(2):
                            j0 = 4 * (2 * n + q)
                            v.mark(V.tensor_scalar(cl[p_, j0:j0 + 4, ri, g * 16:g * 16 + 16], src[p_, q, ri, :, g, :],
                                                   -1.0 if ri else 1.0, None, ALU.mult))
                v.wait()
                ve.sem_inc(freed[m % 4], 1)
            m = UNITS["ini"]
            evac(m, fo[:, 2048:2304], ps[:, bank(m), 0:256])
            ve.wait_ge(freed[m % 4], m // 4 + 1)
            ve.sem_inc(ssm_tabs, 1)

            t1, t2, vr, vi, _x, _y = dt_
            for j in range(SPAIR):
                mr, mi = UNITS["bu"] + 2 * j, UNITS["bu"] + 2 * j + 1
                ve.wait_ge(filled, mi + 1)
                ve.wait_ge(trig_out, j + 1)
                sn, cs = trig[j % 2][:, 0:256], trig[j % 2][:, 256:512]
                br, bi = ps[:, bank(mr), 0:TP], ps[:, bank(mi), 0:TP]
                v.mark(V.tensor_tensor(t1, br, cs, ALU.mult))
                v.mark(V.tensor_tensor(t2, bi, sn, ALU.mult))
                v.mark(V.tensor_tensor(_x, bi, cs, ALU.mult))
                v.link(V.tensor_tensor(_y, br, sn, ALU.mult))
                v.mark(V.tensor_tensor(vr, t1, t2, ALU.add))
                v.mark(V.tensor_tensor(vi, _x, _y, ALU.subtract))
                for r, mm_ in enumerate((mr, mi)):
                    V.tensor_copy(bus[:, r, :, j, :], ps[:, bank(mm_), TP:NT].rearrange("p (b t) -> p b t", b=NB)).then_inc(freed[mm_ % 4], 1)
                v.wait()
                mag = ssmv[:, 3, j:j + 1].to_broadcast([P, TP])
                v.mark(V.tensor_tensor_scan(t1, mag, vr, 0.0, ALU.mult, ALU.add))
                v.link(V.tensor_tensor_scan(t2, mag, vi, 0.0, ALU.mult, ALU.add))
                if j >= 2:
                    ve.wait_ge(state_used, j - 1)
                S = states[j % 2]
                v.mark(V.tensor_tensor(vr, t1, cs, ALU.mult))
                v.mark(V.tensor_tensor(vi, t2, sn, ALU.mult))
                v.mark(V.tensor_tensor(_x, t1, sn, ALU.mult))
                v.link(V.tensor_tensor(_y, t2, cs, ALU.mult))
                v.mark(V.tensor_tensor(S[:, 0], vr, vi, ALU.subtract))
                v.link(V.tensor_tensor(S[:, 1], _x, _y, ALU.add))
                ve.sem_inc(state_ready, 1)
                v.link(V.tensor_copy(ssmv[:, 20:22, j:j + 1], S[:, :, TP - 1:TP]))
            ab = [q_(k).unsqueeze(1).to_broadcast([P, NB, SPAIR]) for k in (14, 15)]
            w_ = [fw[:, 2560 + 128 * k:2688 + 128 * k].rearrange("p (b j) -> p b j", b=NB) for k in range(4)]
            for t in range(TQ):
                prev = [ini[:, r] if t == 0 else sst[:, r, :, :, t - 1] for r in range(2)]
                for k, (x, y) in enumerate(((0, 0), (1, 1), (0, 1), (1, 0))):
                    v.mark(V.tensor_tensor(w_[k], ab[x], prev[y], ALU.mult))
                v.wait()
                v.mark(V.tensor_tensor(w_[0], w_[0], w_[1], ALU.subtract))
                v.link(V.tensor_tensor(w_[2], w_[2], w_[3], ALU.add))
                v.mark(V.tensor_tensor(sst[:, 0, :, :, t], w_[0], bus[:, 0, :, :, t], ALU.add))
                v.link(V.tensor_tensor(sst[:, 1, :, :, t], w_[2], bus[:, 1, :, :, t], ALU.add))
            ve.sem_inc(samples_ready, 1)
            for q in range(4):
                ve.wait_ge(state_used, 16 + 4 * (q + 1))
                if q == 0:
                    ve.wait_ge(trig_out, SPAIR)
                V.scalar_tensor_tensor(yt[:, q, :], uT[:, q, :], col(R_D + q), ps[:, q, 0:NT], ALU.mult, ALU.add).then_inc(y_ready, 1)
            m = UNITS["fin"]
            evac(m, rows_out[0:2 * SPAIR, 0, :], ps[0:2 * SPAIR, bank(m), 0:P])
            ve.wait_ge(freed[m % 4], m // 4 + 1)
            ve.sem_inc(state_out, 1)
            evac(m + 1, rows_out[:, 1:3, :], ps[:, bank(m + 1), 0:256].rearrange("p (r n) -> p r n", r=2))
            ve.wait_ge(freed[(m + 1) % 4], (m + 1) // 4 + 1)
            ve.sem_inc(state_out, 1)
            for n in range(2):
                _, free = pr.s, out[pr.s]
                st.c += 1
                pr.step()
                ve.wait_ge(free, pr.n[pr.s ^ 1])
            v.link(V.tensor_tensor(uT[:], uT[:], sg, ALU.mult))
            ve.sem_inc(glu_ready, 1)

            U = UNITS["pa"]

            def scores(i):
                m = U if i == 0 else U + 3 * i - 2
                w, t, k = P * (i % 2 + 1), i % 2, i % 2
                ve.wait_ge(filled, m + 1)
                if i >= 2:
                    ve.wait_ge(p_turned, i - 1)
                V.tensor_tensor_reduce(psc[k][:, 0:w], ps[:, bank(m), 0:w], pscore[:, t, 1, 0:w], 1.0, -3.0e38, ALU.add, ALU.max,
                                       accum_out=sc[:, k:k + 1]).then_inc(freed[m % 4], 1)
                ve.wait_ge(freed[m % 4], m // 4 + 1)
                V.tensor_scalar(sc[:, 2 + k:3 + k], sc[:, k:k + 1], -(HD ** -0.5), None, ALU.mult).then_inc(p_max, 1)

            def keep(i):
                m = U + 3 * i + 3 - (i == 15)
                evac(m, oT[:, i // 2, i % 2 * P:(i % 2 + 1) * P], ps[:, bank(m), 0:P])

            scores(0)
            for i in range(16):
                if i < 15:
                    scores(i + 1)
                k, w = i % 2, P * (i % 2 + 1)
                ve.wait_ge(p_exp, i + 1)
                v.link(V.reciprocal(sc[:, 6 + k:7 + k], sc[:, 4 + k:5 + k]))
                V.tensor_scalar(psc[k][:, 0:w], psc[k][:, 0:w], sc[:, 6 + k:7 + k], None, ALU.mult).then_inc(p_norm, 1)
                if i:
                    keep(i - 1)
            keep(15)
            v.link(V.memset(fi[:, 0:2048], 0.0))
            for b in range(NB):
                for g in range(2):
                    c0 = b % 4 * 32 + g * 16
                    v.mark(V.tensor_copy(qz[:, b, g, c0:c0 + 16].rearrange("p (r t) -> p r t", t=TQ),
                                         qkvT[:, g * 4:g * 4 + 4, TP + b * TQ:TP + (b + 1) * TQ]))
            v.wait()
            ve.sem_inc(qz_ready, 1)
            kk = Turns()

            def turn(dst, src):
                k = kk.next()
                if k % 2:
                    ve.wait_ge(k_filled, k + 1)
                    V.tensor_copy(dst, src(k % 2)).then_inc(k_freed[1], 1)

            ve.wait_ge(state_stored, 64)
            for half in range(2):
                for b in range(4 * half, 4 * half + 4):
                    if b:
                        ve.wait_ge(s_free, b)
                    if b == 4:
                        ve.wait_ge(pv_done, 4)
                    for n in range(8):
                        turn(kT[:, n // 4, n % 4 * 512:n % 4 * 512 + 512], lambda s: ps[:, s, :])
                ve.wait_ge(s_free, 4 * half + 4)
                v.mark(V.tensor_reduce(sc[:, 8:9], ps[:, 4:8, :].rearrange("p k n -> p (k n)"), AX, ALU.max))
                v.link(V.tensor_reduce(sc[:, 9:10], ps[:, 3, 0:TS], AX, ALU.max))
                v.link(V.tensor_tensor(sc[:, 10:11], sc[:, 8:9], sc[:, 9:10], ALU.max))
                v.link(V.tensor_scalar(sc[:, 11:12], sc[:, 10:11], -(HD ** -0.5), None, ALU.mult))
                ve.sem_inc(s_max, 1)
                ve.wait_ge(s_exp, 2 * half + 2)
                v.link(V.tensor_tensor(sc[:, 14:15], sc[:, 12:13], sc[:, 13:14], ALU.add))
                v.link(V.reciprocal(sc[:, 15:16], sc[:, 14:15]))
                V.tensor_scalar(sp_, sp_, sc[:, 15:16], None, ALU.mult).then_inc(s_norm, 1)
                for n in range(4):
                    turn(spT[:, 4 * n:4 * n + 4, :], lambda s: ps[:, s, :].rearrange("p (j n) -> p j n", j=4))
                turn(spN, lambda s: ps[0:TS, s, 0:P])
                for b in range(4 * half, 4 * half + 4):
                    t0 = TP + b * TQ
                    ve.wait_ge(pv_done, b + 1)
                    if b:
                        ve.wait_ge(os_ready, b)
                        ve.wait_ge(k_filled, kk.k)
                    V.tensor_copy(os_, ps[0:TS, 2 + b % 2, 0:256]).then_inc(os_ready, 1)
                    k = kk.next()
                    if k % 2:
                        ve.wait_ge(k_filled, k + 1)
                        for g in range(2):
                            ins = V.tensor_copy(oT[:, g * 4:g * 4 + 4, t0:t0 + TQ],
                                                ps[:, 1, g * 48:g * 48 + 16].rearrange("p (r t) -> p r t", t=TQ))
                        ins.then_inc(k_freed[1], 1)
            ve.wait_ge(k_freed[1], kk.k // 2)
            ve.sem_inc(o_ready, 1)

            for n in range(8):
                s = n % 2
                ve.wait_ge(used, st.count(1))
                t0, t1_ = gates[:, 2 * n:2 * n + 2, :], gates[:, KD + 2 * n:KD + 2 * n + 2, :]
                v.mark(V.tensor_tensor(t0, t0, ps[:, 4 * s:4 * s + 2, 0:NT], ALU.mult))
                v.link(V.tensor_tensor(t1_, t1_, ps[:, 4 * s + 2:4 * s + 4, 0:NT], ALU.mult))
                V.tensor_tensor(t0, t0, t1_, ALU.add).then_inc(merged, 1)
                st.c += 2
            with ve.Fori(0, 4) as i:
                st.begin(i, 4)
                pr.begin(i, 1)
                for n in range(2):
                    src, free = taken(ve, st, pr)
                    x = xT[:, bass.ds(i * 4 + 2 * n, 2), :]
                    V.tensor_tensor(x, x, src, ALU.add).then_inc(free, 1)
            st.end(4)
            pr.end(4)
            for s in range(2):
                ve.wait_ge(out[s], pr.n[s])
            ve.sem_inc(x_step, 1)
            norm_x(UNITS["norm1"], 12, R_FFN)

            conv_cols = convT[:].rearrange("p (s f) r -> p s f r", s=2)
            v.mark(V.memset(ext[:, :, :, 0:2], 0.0))
            ext_s = ext[:, :, :, EXT_S:EXT].rearrange("p e s (b t) -> p e s b t", b=NB)
            cout_s = cout[:, :, :, 2:18].rearrange("p s f (b t) -> p s f b t", b=NB)
            gl_s = gl[:, :, EXT_S:EXT].rearrange("p e (b t) -> p e b t", b=NB)
            cv_s = cv[:, :, 1, EXT_S:EXT].rearrange("p e (b t) -> p e b t", b=NB)

            def up(t, g, j):
                e = pr.s
                v.link(V.tensor_copy(taps[:, e], conv_cols[:, :, bass.ds(t, 1), :].rearrange("p s o r -> p s (o r)")))
                v.link(V.tensor_copy(ext_s[:, e, :, :, 0:2], taps[:, e, :, 0:16].rearrange("p s (b r) -> p s b r", b=NB)))
                ve.wait_ge(ext_ready, t + 1)
                if pr.off is not None or j >= 2 or g:
                    ve.wait_ge(gelu_ready, t - 1)
                for s in range(2):
                    v.mark(V.tensor_scalar(cv[:, e, s, 0:CONVN], ext[:, e, s, 0:CONVN], taps[:, e, s, 16:17], taps[:, e, s, 19:20],
                                           ALU.mult, ALU.add))
                for k in (1, 2):
                    v.wait()
                    for s in range(2):
                        ins = V.scalar_tensor_tensor(cv[:, e, s, 0:CONVN], ext[:, e, s, k:k + CONVN], taps[:, e, s, 16 + k:17 + k],
                                                     cv[:, e, s, 0:CONVN], ALU.mult, ALU.add)
                        v.mark(ins)
                one = bass.ds(t, 1)
                v.mark(V.tensor_copy(cout[:, :, one, 0:2].rearrange("p s o r -> p s (o r)"), ext[:, e, :, TP:TP + 2]))
                for s in range(2):
                    v.mark(V.tensor_copy(cout_s[:, s, one].rearrange("p o b t -> p (o b) t"), ext_s[:, e, s, :, TQ:TQ + 2]))
                v.wait()
                ve.sem_inc(conv_ready, 1)
                ve.wait_ge(gelu_ready, t + 1)
                v.mark(V.tensor_tensor(acts[:, g, j, 0:TP], gl[:, e, 0:TP], cv[:, e, 1, 0:TP], ALU.mult))
                v.link(V.tensor_tensor(acts[:, g, j, TP:NT].rearrange("p (b t) -> p b t", b=NB), gl_s[:, e, :, 0:TQ],
                                       cv_s[:, e, :, 0:TQ], ALU.mult))
                ve.sem_inc(act_ready, 1)
                st.c += 2
                pr.step()

            def down(t, g, k):
                for n in range(8):
                    src, free = taken(ve, st, pr, 1)
                    x = xT[:, 2 * n:2 * n + 2, :]
                    V.tensor_tensor(x, x, src, ALU.add).then_inc(free, 1)

            ffn(ve, st, pr, up, down, ((v, 2 * FG * UP_STEPS),))
            for s in range(2):
                ve.wait_ge(out[s], pr.n[s])
            ve.sem_inc(x_step, 1)
            for n in range(22):
                m = UNITS["cout"] + n
                w = min(512, 2 * FF - n * 512)
                ve.wait_ge(filled, m + 1)
                if n >= 6:
                    ve.wait_ge(c_stored[n // 2 % 3], 32 * (n // 2 // 3))
                V.tensor_copy(crow[0:18, n // 2 % 3, n % 2 * 512:n % 2 * 512 + w], ps[0:18, bank(m), 0:w]).then_inc(freed[m % 4], 1)
                ve.wait_ge(freed[m % 4], m // 4 + 1)
                ve.sem_inc(c_turned, 1)
            for n in range(2):
                m = UNITS["pt"] + n
                evac(m, pT[:, n, :], ps[:, bank(m), 0:NT])
                ve.wait_ge(freed[m % 4], m // 4 + 1)
                ve.sem_inc(ple_ready_p, 1)
            for n in range(8):
                s = pr.s
                ve.wait_ge(ple_filled, n + 1)
                V.tensor_copy(pl[:, 2 * n:2 * n + 2, :], ps[:, 2 * s:2 * s + 2, 0:NT]).then_inc(out[s], 1)
                pr.step()
                ve.wait_ge(out[s], pr.n[s])
                ve.sem_inc(ple_out, 1)
            st.c += 2
            norm_x(UNITS["norm2"], 13, R_PG)
            m = UNITS["norm3"]
            ve.wait_ge(filled, m + 1)
            V.tensor_scalar(rstd[:, 1, :], ps[:, bank(m), 0:NT], 1.0 / D, EPS, ALU.mult, ALU.add).then_inc(freed[m % 4], 1)
            ve.wait_ge(freed[m % 4], m // 4 + 1)
            ve.sem_inc(var_ready, 1)
            ve.wait_ge(rstd_ready, 14)
            v.link(V.reciprocal(rstd[:, 1, :], rstd[:, 1, :]))
            for k in range(KD):
                v.mark(V.scalar_tensor_tensor(pl[:, k, :], pl[:, k, :], col(R_PLE + k), rstd[:, 1, :], ALU.mult, ALU.mult))
            v.wait()
            ve.sem_inc(ple_ready, 2)
            with ve.Fori(0, 4) as i:
                v.begin(i, 2)
                for n in range(2):
                    ve.wait_ge(sig_ready, i * 2 + (1 + n))
                    k = bass.ds(i * 4 + 2 * n, 2)
                    v.link(V.tensor_tensor(sig[:, n], sig[:, n], pl[:, k, :], ALU.mult))
                    V.tensor_tensor(xT[:, k, :], xT[:, k, :], sig[:, n], ALU.add).then_inc(ple_ready, 1)
            v.end(4)
            for n in range(12):
                m, j, q = UNITS["y"] + n, n // 4, n % 4
                w = rows(j)
                if n == 8:
                    ve.wait_ge(y_stored[0], 16)
                evac(m, yrow[0:w, j % 2, q * 512:(q + 1) * 512], ps[0:w, bank(m), :])
                ve.wait_ge(freed[m % 4], m // 4 + 1)
                ve.sem_inc(y_turned, 1)

        @block.tensor
        def _(pe):
            st, pr = Stream(), Pairs()
            T = nc.tensor

            def square_sum(m, base):
                fill_wait(pe, m)
                for q in range(4):
                    pe.wait_ge(squares, base + q + 1)
                    for k in range(4):
                        mm = T.matmul(ps[:, bank(m), 0:NT], ones, fo[:, (q % 2) * 1152 + k * NT:(q % 2) * 1152 + (k + 1) * NT],
                                      start=(q == k == 0), stop=(q == k == 3))
                    if q < 3:
                        mm.then_inc(squares_used, 1)
                mm.then_inc(filled, 1)
                pe.wait_ge(filled, m + 1)
                pe.sem_inc(squares_used, 1)

            pe.wait_ge(consts_in, 128)
            pe.wait_ge(conv_in, 16 * 12)
            for n, (src, t0, k) in enumerate(conv_at):
                m = UNITS["conv"] + n
                for t in range(k):
                    mm = T.transpose(ps[:, bank(m), t * 20:t * 20 + 20], src[0:20, t * P:(t + 1) * P], ident[0:20, 0:20])
                mm.then_inc(filled, 1)
            m = UNITS["small"]
            fill_wait(pe, m)
            pe.wait_ge(small_in, 160)
            pe.wait_ge(small_ready, 1)
            T.transpose(ps[:, bank(m), 0:R_ALL], small[:], ident[0:R_ALL, 0:R_ALL]).then_inc(filled, 1)
            pe.wait_ge(x_in, 48)
            for n in range(12):
                m, j, q = UNITS["x"] + n, n // 4, n % 4
                w = rows(j)
                fill_wait(pe, m)
                for k in range(4):
                    mm = T.transpose(ps[:, bank(m), k * w:(k + 1) * w], xn[0:w, j, (4 * q + k) * P:(4 * q + k + 1) * P],
                                     ident[0:w, 0:w])
                mm.then_inc(filled, 1)
            square_sum(UNITS["norm0"], 0)
            pe.wait_ge(normed, 1)
            products(pe, st, pr, hT, [C_U - C_IK])
            for n in range(2):
                products(pe, st, pr, hT, [P, P])
            for times in (2, 3):
                with pe.Fori(0, times) as i:
                    st.begin(i, 4)
                    pr.begin(i, 1)
                    for n in range(2):
                        products(pe, st, pr, hT, [P, P])
                st.end(times)
                pr.end(times)
            for j in range(10):
                m = UNITS["qkn"] + j
                fill_wait(pe, m)
                pe.wait_ge(squares, 4 + j + 1)
                T.matmul(ps[:, bank(m), 0:NT], ones, oT[:, j % 4, :], start=True, stop=True).then_inc(filled, 1)
                pe.wait_ge(filled, m + 1)
                pe.sem_inc(squares_used, 1)
            for j in range(19):
                m = UNITS["ropeq"] + j
                fill_wait(pe, m)
                if j < 10:
                    pe.wait_ge(head_normed, j + 1)
                    mm = T.matmul(ps[:, bank(m), 0:NT], turn_q, qkvT[:, j, :], start=True, stop=True)
                elif j < 18:
                    pe.wait_ge(a_out, 4)
                    mm = T.matmul(ps[:, bank(m), 0:NT], turn_i, iqT[:, j - 10, :], start=True, stop=True)
                else:
                    mm = T.matmul(ps[0:IDIM, bank(m), 0:NT], turn_i[0:IDIM, 0:IDIM], ikT[0:IDIM, :], start=True, stop=True)
                mm.then_inc(filled, 1)
            for n in range(6):
                m, tt = UNITS["tok"] + n, n // 2
                w, t0 = rows(tt), tt * P
                fill_wait(pe, m)
                pe.wait_ge(roped, 19)
                if n % 2 == 0:
                    for k in range(4):
                        mm = T.transpose(ps[0:w, bank(m), k * P:(k + 1) * P], qkvT[:, 8 + k, t0:t0 + w], ident)
                else:
                    mm = T.transpose(ps[0:w, bank(m), 0:80], ikT[0:80, t0:t0 + w], ident[0:80, 0:80])
                mm.then_inc(filled, 1)
            m = UNITS["wb"]
            fill_wait(pe, m)
            T.matmul(ps[:, bank(m), 0:TS], headsel[:], ikT[0:80, TP:NT], start=True, stop=True).then_inc(filled, 1)
            for n in range(16):
                m, b, jh = UNITS["idx"] + n, n // 2, n % 2
                fill_wait(pe, m)
                if n % 8 == 0:
                    pe.wait_ge(idx_in[n // 8], 64)
                for k in range(4):
                    mm = T.transpose(ps[:, bank(m), k * P:(k + 1) * P], idx_raw[:, b % 4, 4 * jh + k, :], ident)
                mm.then_inc(filled, 1)
            for n in range(16):
                m, tt, i, par = UNITS["pidx"] + n, n // 8, n // 2 % 4, n % 2
                fill_wait(pe, m)
                r = slice(64 * par, 64 * par + 64)
                for k in range(2):
                    mm = T.matmul(ps[:, bank(m), k * 256:k * 256 + 256], iqT[r, 2 * i + k, tt * P:(tt + 1) * P],
                                  ik2[r, 0:TP], start=True, stop=True)
                mm.then_inc(filled, 1)
            pe.wait_ge(wb_ready, 1)
            for s in range(2):
                pe.wait_ge(out[s], pr.n[s])

            def weigh(n):
                blk, b = n // NB, n % NB
                w = 512 if blk < 2 else TQ
                pe.wait_ge(relu_ready, 16 + n + 1)
                T.matmul(ps[0:2 * TS, blk, 0:w], wheads[:, b, :], relu[:, n % 4, 0:w], start=(b == 0),
                         stop=(b == NB - 1)).then_inc(relu_weighed, 1)
                if b == NB - 1:
                    pe.wait_ge(relu_weighed, n + 1)
                    pe.sem_inc(blk_scored, 1)

            for n in range(24):
                m, blk, b = UNITS["sidx"] + n, n // NB, n % NB
                fill_wait(pe, m)
                w, keys = (512, idxT[:, b, blk * 512:(blk + 1) * 512]) if blk < 2 else (TQ, nk[:, b, :])
                T.matmul(ps[:, bank(m), 0:w], qb[:, b, :], keys, start=True, stop=True).then_inc(filled, 1)
                if n:
                    weigh(n - 1)
            weigh(23)
            pe.wait_ge(blk_out, 5)
            with pe.Fori(0, 8) as i:
                st.begin(i, 4)
                pr.begin(i, 1)
                for n in range(2):
                    products(pe, st, pr, hT, [P, P])
            st.end(8)
            pr.end(8)

            pe.wait_ge(ssm_tabs, 1)
            for n in range(2):
                m = UNITS["bt"] + n
                fill_wait(pe, m)
                for k in range(4):
                    src = bbd[:, 2 * n + k // 2, k % 2].rearrange("p j g c -> p (j g c)")
                    mm = T.transpose(ps[:, bank(m), k * P:(k + 1) * P], src, ident)
                mm.then_inc(filled, 1)
            for n in range(2):
                m = UNITS["ct"] + n
                fill_wait(pe, m)
                for k in range(4):
                    src = craw[:, 2 * n + k // 2, k % 2].rearrange("p d n -> p (d n)")
                    mm = T.transpose(ps[:, bank(m), k * P:(k + 1) * P], src, ident)
                mm.then_inc(filled, 1)
            m = UNITS["ini"]
            fill_wait(pe, m)
            for k in range(2):
                mm = T.transpose(ps[:, bank(m), k * P:(k + 1) * P], ini_raw[:, k], ident)
            mm.then_inc(filled, 1)
            for s in range(2):
                pe.wait_ge(out[s], pr.n[s])
            pe.wait_ge(ssm_tabs, 2)

            def c_states(j, src, t0, n):
                q, g = j // 4, 32 * (j % 4)
                for r in range(2):
                    mm = T.matmul(ps[g:g + 32, q, t0:t0 + n], cl[:, j, r, :], src(r), start=(r == 0), stop=(r == 1))
                mm.then_inc(state_used, 1)

            for j in range(SPAIR + 1):
                if j < SPAIR:
                    q, g = j // 4, slice(32 * (j % 4), 32 * (j % 4) + 32)
                    for r in range(2):
                        m = UNITS["bu"] + 2 * j + r
                        fill_wait(pe, m)
                        T.matmul(ps[:, bank(m), 0:NT], bl[g, q, r, :], uT[g, q, :], start=True, stop=True).then_inc(filled, 1)
                if j:
                    pe.wait_ge(state_ready, j)
                    c_states(j - 1, lambda r: states[(j - 1) % 2][:, r, :], 0, TP)
            pe.wait_ge(samples_ready, 1)
            for j in range(SPAIR):
                c_states(j, lambda r: sst[:, r, :, j, :], TP, TS)
            m = UNITS["fin"]
            fill_wait(pe, m)
            T.transpose(ps[0:32, bank(m), 0:P], ssmv[:, 20:22, :].rearrange("p r j -> p (r j)"), ident).then_inc(filled, 1)
            fill_wait(pe, m + 1)
            for r in range(2):
                src = sst[:, r].rearrange("p b j t -> p (b j) t")[:, :, TQ - 1]
                mm = T.transpose(ps[:, bank(m + 1), r * P:(r + 1) * P], src, ident)
            mm.then_inc(filled, 1)
            pe.wait_ge(z_ready, 4)
            for n in range(2):
                products(pe, st, pr, uT, [P, P], 1, 4)
            U = UNITS["pa"]

            def scores(i):
                m = U if i == 0 else U + 3 * i - 2
                h, t = i // 2, i % 2
                fill_wait(pe, m)
                T.matmul(ps[:, bank(m), 0:P * (t + 1)], qkvT[:, h, t * P:(t + 1) * P], qkvT[:, 8 + h // GRP, 0:P * (t + 1)],
                         start=True, stop=True).then_inc(filled, 1)

            pe.wait_ge(pb_ready, 2)
            scores(0)
            for i in range(16):
                if i < 15:
                    scores(i + 1)
                h, t = i // 2, i % 2
                m = U + 3 * i + 2 - (i == 15)
                fill_wait(pe, m)
                pe.wait_ge(p_norm, i + 1)
                for k in range(t + 1):
                    mm = T.transpose(ps[:, bank(m), k * P:(k + 1) * P], psc[i % 2][:, k * P:(k + 1) * P], ident)
                mm.then_inc(filled, 1)
                m += 1
                fill_wait(pe, m)
                pe.wait_ge(p_turned, i + 1)
                g0 = 256 + h // GRP * HD
                for k in range(t + 1):
                    mm = T.matmul(ps[:, bank(m), 0:P], tok[:, k, g0:g0 + HD], ppt[i % 2][:, k, :], start=(k == 0), stop=(k == t))
                mm.then_inc(filled, 1)
            kk = Turns()

            def turn():
                k = kk.next()
                if k >= 2:
                    pe.wait_ge(k_freed[k % 2], k // 2)
                return k % 2

            pe.wait_ge(qz_ready, 1)
            for m in range(UNITS["norm1"] - 4, UNITS["norm1"]):
                pe.wait_ge(freed[m % 4], m // 4 + 1)
            for half in range(2):
                if half:
                    pe.wait_ge(s_exp, 2)
                for n in range(4):
                    T.matmul(ps[:, 4 + n, :], rowsb[:, half, :], selb[:, n * 512:n * 512 + 512], start=True, stop=False,
                             skip_group_check=True)
                if half:
                    pe.wait_ge(os_ready, 4)
                T.matmul(ps[:, 3, 0:TS], rowsb[:, half, :], selb[:, PAST:PAST + TS], start=True, stop=False,
                         skip_group_check=True)
                for b in range(4 * half, 4 * half + 4):
                    pe.wait_ge(k_in, 16 * (b + 1))
                    for n in range(8):
                        s = turn()
                        g = n // 4
                        for k in range(4):
                            mm = T.transpose(ps[:, s, k * P:(k + 1) * P], kraw[:, n % 4 * 4 + k, g * P:(g + 1) * P], ident)
                        mm.then_inc(k_filled, 1)
                    pe.wait_ge(k_filled, kk.k)
                    pe.sem_inc(k_used, 1)
                    last = b == 4 * half + 3
                    for s in range(2):
                        pe.wait_ge(k_freed[s], (kk.k + 1 - s) // 2)
                    for g in range(2):
                        for n in range(4):
                            T.matmul(ps[:, 4 + n, :], qz[:, b, g, :], kT[:, g, n * 512:n * 512 + 512], start=False,
                                     stop=(last and g == 1), skip_group_check=True)
                        mm = T.matmul(ps[:, 3, 0:TS], qz[:, b, g, :], qkvT[:, 8 + g, TP:NT], start=False,
                                      stop=(last and g == 1), skip_group_check=True)
                    mm.then_inc(s_free, 1)
                pe.wait_ge(s_free, 4 * half + 4)
                pe.sem_inc(s_scored, 1)
                pe.wait_ge(s_norm, half + 1)
                for n in range(5):
                    s = turn()
                    if n < 4:
                        for k in range(4):
                            j = 4 * n + k
                            mm = T.transpose(ps[:, s, k * P:(k + 1) * P], sp_[:, j * P:(j + 1) * P], ident)
                    else:
                        mm = T.transpose(ps[0:TS, s, 0:P], sp_[:, PAST:PAST + TS], ident)
                    mm.then_inc(k_filled, 1)
                for s in range(2):
                    pe.wait_ge(k_freed[s], (kk.k + 1 - s) // 2)
                for b in range(4 * half, 4 * half + 4):
                    c = slice(b % 4 * 32, b % 4 * 32 + 32)
                    pe.wait_ge(v_in[b % 2], 16 * (b // 2 + 1))
                    dst = ps[0:TS, 2 + b % 2, 0:256]
                    for j in range(SLOT):
                        T.matmul(dst, spT[:, j, c], vraw[b % 2][:, j, :], start=(j == 0), stop=False)
                    T.matmul(dst, spN[:, c], tok[0:TS, 2, 256:512], start=False, stop=True).then_inc(pv_done, 1)
                    s = turn()
                    pe.wait_ge(os_ready, b + 1)
                    for g in range(2):
                        mm = T.transpose(ps[:, s, g * 32:g * 32 + 32], os_[:, g * P:(g + 1) * P], ident[0:TS, 0:TS])
                    mm.then_inc(k_filled, 1)
            pe.wait_ge(o_ready, 2)
            pe.wait_ge(glu_ready, 1)
            for n in range(8):
                s = n % 2
                if n >= 2:
                    pe.wait_ge(merged, n - 1)
                for kt, rhs, b0 in ((8, oT, 4 * s), (4, uT, 4 * s + 2)):
                    pe.wait_ge(landed[st.slot()], st.landed())
                    w = ring[:, st.slot(), 0:kt * 256].rearrange("p (k n) -> p k n", k=kt)
                    for c in range(2):
                        for k in range(kt):
                            mm = T.matmul(ps[:, b0 + c, 0:NT], w[:, k, c * P:(c + 1) * P], rhs[:, k, :], start=(k == 0), stop=(k == kt - 1))
                    mm.then_inc(used, 1)
                    st.c += 1
            pe.wait_ge(merged, 8)
            with pe.Fori(0, 4) as i:
                st.begin(i, 4)
                pr.begin(i, 1)
                for n in range(2):
                    products(pe, st, pr, gates, [P, P])
            st.end(4)
            pr.end(4)
            square_sum(UNITS["norm1"], 14)
            pe.wait_ge(normed, 2)

            def up(t, g, j):
                if pr.off is not None or pr.n[pr.s] > 0:
                    pe.wait_ge(out[pr.s], pr.before())
                for half in range(2):
                    pe.wait_ge(landed[st.slot()], st.landed())
                    for k in range(KD):
                        mm = T.matmul(ps[:, 2 * pr.s + half, 0:NT], ring[:, st.slot(), k * P:(k + 1) * P], hT[:, k, :],
                                      start=(k == 0), stop=(k == KD - 1))
                    mm.then_inc(used, 1)
                    st.c += 1
                pr.step()

            def down(t, g, k):
                pe.wait_ge(act_ready, t + k)
                for n in range(8):
                    products(pe, st, pr, acts[:, g], [P, P], 1, k)

            ffn(pe, st, pr, up, down)
            for n in range(22):
                m = UNITS["cout"] + n
                fill_wait(pe, m)
                for k in range(min(4, 2 * FT - 4 * n)):
                    f = 4 * n + k
                    mm = T.transpose(ps[0:18, bank(m), k * P:(k + 1) * P], cout[:, f // FT, f % FT, :], ident)
                mm.then_inc(filled, 1)
            pe.wait_ge(p_in, 48)
            for n in range(2):
                m = UNITS["pt"] + n
                fill_wait(pe, m)
                for j in range(3):
                    w = rows(j)
                    mm = T.transpose(ps[:, bank(m), j * P:j * P + w], pn[0:w, j, n * P:(n + 1) * P], ident[0:w, 0:w])
                mm.then_inc(filled, 1)
            pe.wait_ge(ple_ready_p, 2)
            for n in range(8):
                pe.wait_ge(out[pr.s], pr.before())
                pe.wait_ge(landed[st.slot()], st.landed())
                w = ring[:, st.slot(), :].rearrange("p (k n) -> p k n", k=2)
                for c in range(2):
                    c0 = (n % 4 * 2 + c) * P
                    for k in range(2):
                        mm = T.matmul(ps[:, 2 * pr.s + c, 0:NT], w[:, k, c0:c0 + P], pT[:, k, :], start=(k == 0), stop=(k == 1))
                mm.then_inc(ple_filled, 1)
                pr.step()
                if n % 4 == 3:
                    pe.wait_ge(ple_filled, n + 1)
                    pe.sem_inc(used, 1)
                    st.c += 1
            square_sum(UNITS["norm2"], 18)
            square_sum(UNITS["norm3"], 22)
            pe.wait_ge(normed, 3)
            with pe.Fori(0, 4) as i:
                st.begin(i, 4)
                pr.begin(i, 1)
                for n in range(2):
                    products(pe, st, pr, hT, [P, P])
            st.end(4)
            pr.end(4)
            pe.wait_ge(ple_ready, 10)
            for n in range(12):
                m, j, q = UNITS["y"] + n, n // 4, n % 4
                w = rows(j)
                fill_wait(pe, m)
                for k in range(4):
                    mm = T.transpose(ps[0:w, bank(m), k * P:(k + 1) * P], xT[:, 4 * q + k, j * P:j * P + w], ident)
                mm.then_inc(filled, 1)


INPUTS = ["x_prompt", "x_sample", "cache_k", "cache_v", "cache_idx_k", "state_ssm_re", "state_ssm_im", "state_conv",
          "page_table", "p_prompt", "p_sample", "g_mix", "w_in", "g_q", "g_k", "ssm_a_re", "ssm_a_im", "ssm_log_dt",
          "ssm_b_re", "ssm_b_im", "ssm_c_re", "ssm_c_im", "ssm_d", "w_glu", "w_att_br", "w_ssm_br", "w_o", "g_ffn",
          "w_up", "conv_w", "conv_b", "w_down", "w_ple", "g_ple", "g_pg", "w_pg"]
OUTPUTS = [("y_prompt", (TP, D), (1, TP, D)), ("y_sample", (TS, D), (NB, TQ, D)),
           ("k_prompt", (TP, 256), (1, 1, TP, KVH, HD)), ("v_prompt", (TP, 256), (1, 1, TP, KVH, HD)),
           ("idx_k_prompt", (TP, IDIM), (1, 1, TP, IDIM)),
           ("ssm_re_prompt", (SPAIR, P), (1, 1, G_SSM, N_SSM)), ("ssm_im_prompt", (SPAIR, P), (1, 1, G_SSM, N_SSM)),
           ("conv_prompt", (2, 2 * FF), (1, 1, 2, 2 * FF)),
           ("k_sample", (TS, 256), (1, NB, TQ, KVH, HD)), ("v_sample", (TS, 256), (1, NB, TQ, KVH, HD)),
           ("idx_k_sample", (TS, IDIM), (1, NB, TQ, IDIM)),
           ("ssm_re_sample", (P, P), (1, NB, G_SSM, N_SSM)), ("ssm_im_sample", (P, P), (1, NB, G_SSM, N_SSM)),
           ("conv_sample", (2 * NB, 2 * FF), (1, NB, 2, 2 * FF))]


def kernel(**inputs):
    import concourse.bacc as bacc
    from concourse.bass_utils import run_bass_kernel_spmd

    nc = bacc.Bacc("TRN2", target_bir_lowering=False, num_devices=1)
    arrays, a, o = {}, {}, {}
    for name, x in [(n, np.ascontiguousarray(inputs[n])) for n in INPUTS] + sorted(constants().items()):
        arrays[f"in_{name}"] = x
        a[name] = nc.dram_tensor(f"in_{name}", x.shape, mybir.dt.from_np(x.dtype), kind="ExternalInput").ap()
    for name, shape, _ in OUTPUTS:
        o[name] = nc.dram_tensor(f"out_{name}", shape, F32, kind="ExternalOutput").ap()
    build(nc, a, o)
    r = run_bass_kernel_spmd(nc, [arrays], core_ids=[0])
    return tuple(r.results[0][f"out_{name}"].reshape(shape) for name, _, shape in OUTPUTS)
```

```python
from contextlib import ExitStack

import numpy as np
import concourse.bass as bass
from concourse import mybir
from concourse.alu_op_type import AluOpType as ALU

ACT = mybir.ActivationFunctionType
F32 = mybir.dt.float32
F32R = mybir.dt.float32r
BF16 = mybir.dt.bfloat16
I32 = mybir.dt.int32
AX = mybir.AxisListType.X

P = 128
D = 2048
TP = 256
NB, TQ = 8, 4
TS = NB * TQ
NT = TP + TS
PAST = 2048
PAGE = 128
NPAGE = PAST // PAGE
KD = D // P
HEADS, KVH, HD = 8, 2, 128
GRP = HEADS // KVH
IH, IDIM = 16, 64
TOPK_P = min(256, TP // 4)
TOPK_S = min(256, (PAST + TQ) // 4)
G_SSM, C_SSM, N_SSM = 32, 16, 64
W_SSM = G_SSM * C_SSM
T16 = int(TP ** 0.5)
SPAIR = G_SSM // 2
FF = 5504
FT = FF // P
FG = 8
PLE = 256
EPS = 1e-6
SLOT = PAST // P
MASKED = -1.0e38
TAKEN = -3.0e38
OFF = -1.0e30
MAGIC = 12582912.0
C_Q, C_K, C_V, C_IQ, C_IK, C_U, C_GA = 0, 1024, 1280, 1536, 2560, 2640, 3152
EXT_S = 2 + TP
EXT = EXT_S + NB * (TQ + 2)
CONVN = EXT - 2
R_MIX, R_FFN, R_PG, R_PLE, R_DT, R_ARE, R_AIM, R_GQ, R_GK, R_D = 0, 16, 32, 48, 64, 80, 96, 112, 113, 114
R_ALL = R_D + W_SSM // P


TURN = 2 * np.pi
TURN_HI = 6.28125
TURN_LO = float(TURN - 6.28125)
UP_STEPS = 2 + 2 + 4 + 3 + 3
COARSE = 6144.0
HALF = 0.4999999


def constants():
    f = np.float32
    pos = np.concatenate([np.arange(TP), np.tile(PAST + np.arange(TQ), NB)]).astype(f)

    def rope(width, rot, heads):
        half = rot // 2
        inv = (f(500000.0) ** (-np.arange(half, dtype=f) / f(half))).astype(f)
        ang = (pos[:, None] * inv[None, :]).astype(f).astype(np.float64)
        cos, sin = np.ones((width, NT)), np.zeros((width, NT))
        cos[:half] = cos[half:rot] = np.cos(ang).T
        sin[:half] = sin[half:rot] = np.sin(ang).T
        turn = np.zeros((width, width))
        for i in range(half):
            turn[half + i, i] = -1.0
            turn[i, half + i] = 1.0
        big = np.kron(np.eye(heads), turn)
        return [np.tile(x, (heads, 1)).astype(f) for x in (cos, sin)] + [big.astype(f)]

    cq, sq, pq = rope(HD, HD // 4, 1)
    ci, si, pi = rope(IDIM, IDIM // 4, 2)
    c = {}
    c["c_mats"] = np.stack([np.eye(P), pq, pi, np.ones((P, P))], 1).astype(f)
    c["c_rope"] = np.stack([cq, sq, ci, si], 1)
    t = np.arange(P)
    cm = np.zeros((P, 2, TP), f)
    for a in range(2):
        cm[:, a] = np.where(np.arange(TP)[None] <= (a * P + t)[:, None], 0, MASKED)
    c["c_causal"] = cm
    cs = np.zeros((TS, TQ), f)
    off = np.zeros((TS, NB, TQ), f)
    for b in range(NB):
        for q in range(TQ):
            cs[b * TQ + q, q + 1:] = MASKED
            off[b * TQ + q, [x for x in range(NB) if x != b]] = OFF
            off[b * TQ + q, b, q + 1:] = OFF
    c["c_new"] = np.concatenate([cs, off.reshape(TS, NB * TQ)], 1)
    e = np.zeros((TS, 2, P), f)
    for b in range(NB):
        for x in range(8):
            for q in range(TQ):
                e[b * TQ + q, b // 4, (b % 4) * 32 + x * TQ + q] = 1
    c["c_rows"] = e
    hs = np.zeros((80, P), f)
    wm = np.zeros((P, NB, 2, TS), f)
    for j2 in range(2):
        for h in range(IH):
            for q in range(TQ):
                row = j2 * 64 + h * TQ + q
                hs[64 + h, row] = 1
                for b in range(NB):
                    wm[row, b, j2, b * TQ + q] = (IH ** -0.5) * (IDIM ** -0.5)
    c["c_heads"] = hs
    c["c_wmask"] = wm.reshape(P, 2 * NB, TS)
    c["c_time"] = np.tile(np.concatenate([np.arange(T16) * T16, np.arange(T16) + 1]).astype(f), (P, 1))
    c["c_sub"] = (np.arange(P) % 8).astype(f).reshape(P, 1)
    return c


class Steps:

    def __init__(self, eng, sem):
        self.eng, self.sem, self.n, self.off = eng, sem, 0, None

    def mark(self, ins):
        ins.then_inc(self.sem, 1)
        self.n += 1
        return self.n

    def wait(self):
        self.eng.wait_ge(self.sem, self.n if self.off is None else self.off + self.n)

    def link(self, ins):
        self.mark(ins)
        self.wait()

    def begin(self, i, per):
        self.base, self.per = self.n, per
        self.off = i * per

    def end(self, times):
        assert self.n - self.base == self.per, (self.n - self.base, self.per)
        self.off = None
        self.n = self.base + self.per * times


class Stream:
    SLOTS = 4

    def __init__(self):
        self.c, self.off = 0, None
        self.whole = 0

    def split(self, j=0):
        return self.count(j) - self.whole

    def slot(self, j=0):
        return (self.c + j) % self.SLOTS

    def landed(self, j=0):
        v = 16 * ((self.c + j) // self.SLOTS + 1)
        return v if self.off is None else self.off * (16 // self.SLOTS) + v

    def count(self, j=0):
        v = self.c + j + 1
        return v if self.off is None else self.off + v

    def begin(self, i, per):
        assert per % self.SLOTS == 0
        self.base, self.per, self.off = self.c, per, i * per

    def end(self, times):
        assert self.c - self.base == self.per
        self.off = None
        self.c = self.base + self.per * times


UNITS = {}
_n = 0
for _name, _k in (("conv", 4), ("small", 1), ("x", 12), ("norm0", 1), ("qkn", 10), ("ropeq", 10),
                  ("ropei", 9), ("tok", 6), ("wb", 1), ("idx", 16), ("pidx", 16), ("sidx", 24),
                  ("bt", 2), ("ct", 2), ("ini", 2), ("first", 2), ("step", 96), ("fin", 2),
                  ("norm1", 1), ("cout", 22), ("pt", 2), ("norm2", 1), ("norm3", 1), ("y", 12)):
    UNITS[_name] = _n
    _n += _k
U_ALL = _n


def bank(m):
    return 4 + m % 4


class Turns:

    def __init__(self):
        self.k = 0

    def next(self):
        self.k += 1
        return self.k - 1


class Pairs:

    def __init__(self):
        self.s, self.n, self.off = 0, [0, 0], None

    def before(self):
        v = self.n[self.s]
        return v if self.off is None else self.off + v

    def step(self):
        self.n[self.s] += 1
        self.s ^= 1

    def begin(self, i, per):
        self.base, self.per, self.off, self.s0 = list(self.n), per, i * per, self.s

    def end(self, times):
        assert self.s == self.s0 and all(x - y == self.per for x, y in zip(self.n, self.base))
        self.off, self.n = None, [x + self.per * times for x in self.base]


def build(nc, a, o):
    ctx = ExitStack()
    with ctx:
        def sb(name, shape, dt=F32):
            return ctx.enter_context(nc.sbuf_tensor(name, shape, dt))

        def sem(name):
            return ctx.enter_context(nc.semaphore(name))

        def both(name, n):
            with nc.sbuf_tensor(name, [P, n], F32) as plain:
                pass
            return plain, sb(name + "_r", [P, n], F32R)

        def area(x, lo, shape):
            n = int(np.prod(shape))
            names = "abcd"[:len(shape)]
            return x[:, lo:lo + n].rearrange(f"p ({' '.join(names)}) -> p {' '.join(names)}",
                                             **dict(zip(names, shape)))

        fx, rx = both("x", KD * NT)
        fh, rh = both("h", KD * NT)
        fg, rg = both("g", 2 * KD * NT)
        fq, rq = both("q", 20 * NT)
        fw, rw = both("w", 2 * 2052 + 4 * NT)
        fr, rr = both("ring", Stream.SLOTS * 2048)
        fk, rk = both("highs", 2 * 2048)
        highs = area(rk, 0, (2, 2048))
        xT = area(fx, 0, (KD, NT))
        gates = area(fg, 0, (2 * KD, NT))
        qkvT = area(fq, 0, (12, NT))
        iqT = area(fq, 12 * NT, (8, NT))
        work = area(fw, 0, (2, 2052))
        uT = area(fw, 2 * 2052, (4, NT))
        ring = area(fr, 0, (Stream.SLOTS, 2048))
        lows = area(rr, 0, (Stream.SLOTS, 2048))
        h_hi = area(rh, 0, (KD, NT))
        h_lo0 = area(rx, 0, (KD, NT))
        h_lo = area(rw, 0, (KD, NT))
        ssmv = area(fx, 8 * NT, (28, SPAIR))
        norm_tmp = area(fq, 0, (2, 4 * NT))
        o_hi, o_lo = area(rh, 0, (HEADS, NT)), area(rh, HEADS * NT, (HEADS, NT))
        z_hi, z_lo = area(rx, 0, (4, NT)), area(rx, 4 * NT, (4, NT))
        m_lo, m_hi = area(rg, 0, (KD, NT)), area(rg, KD * NT, (KD, NT))
        acts_hi, acts_lo = area(rg, 3140, (2, FG, NT)), area(rq, 0, (2, FG, NT))
        x_saved = nc.dram_tensor("x_saved", (P, KD * NT), F32).ap()
        oT = sb("oT", [P, HEADS, NT])
        ikT = sb("ikT", [P, NT])
        ik2 = sb("ik2", [P, NT])
        mats = sb("mats", [P, 4, P])
        causal = sb("causal", [P, 2, TP])
        cnew = sb("cnew", [TS, TQ + TS])
        rowsf = sb("rowsf", [TS, 2, P])
        rowsb = sb("rowsb", [TS, 2, P], BF16)
        headsel = sb("headsel", [80, P])
        wmask = sb("wmask", [P, 2 * NB, TS])
        small = sb("small", [R_ALL, P])
        cols = sb("cols", [P, R_ALL])
        convT = sb("convT", [P, 2 * FT, 20])
        tok = sb("tok", [P, 3, 512 + 80])
        sc = sb("sc", [P, 64])
        rstd = sb("rstd", [P, 2, NT])
        pidx = sb("pidx", [P, NB], I32)
        pidf = sb("pidf", [P, NB])
        csub = sb("csub", [P, 1])
        pscore = sb("pscore", [P, 2, 2, TP])
        selb = sb("selb", [TS, PAST + TS], BF16)

        ident, turn_q, turn_i, ones = (mats[:, k, :] for k in range(4))
        ropes = area(fg, 0, (4, NT))
        cout = tok[:].rearrange("p a b -> p (a b)")[:, 0:36 * FT].rearrange("p (s f r) -> p s f r", s=2, f=FT)
        ps = ctx.enter_context(nc.psum_tensor("ps", [P, 8, 512], F32))

        landed = [sem(f"weights_landed{s}") for s in range(Stream.SLOTS)]
        used = sem("weights_used")
        out = [sem(f"products_out{s}") for s in range(2)]
        filled = sem("unit_filled")
        freed = [sem(f"unit_freed{s}") for s in range(4)]
        small_ready, trig_ready = sem("small_ready"), sem("trig_ready")
        consts_in, x_in, conv_in, small_in = sem("consts_in"), sem("x_in"), sem("conv_in"), sem("small_in")
        table_in, table_ready = sem("table_in"), sem("table_ready")
        idx_in = [sem(f"idx_keys_in{s}") for s in range(2)]
        x_ready = sem("x_transposed")
        squares, squares_used = sem("squares_ready"), sem("squares_used")
        var_ready, rstd_ready = sem("variance_ready"), sem("rstd_ready")
        normed = sem("normed")
        a_out = sem("projections_out")
        head_normed, roped, tok_ready = sem("head_normed"), sem("roped"), sem("tok_ready")
        wb_ready = sem("indexer_weights_ready")
        relu_ready, relu_summed, relu_weighed = sem("relu_ready"), sem("relu_summed"), sem("relu_weighed")
        blk_scored, blk_out = sem("block_scored"), sem("block_out")
        pb_ready = sem("prompt_mask_ready")
        sb_ready = sem("sample_mask_ready")
        ssm_in, ssm_tabs = sem("ssm_in"), sem("ssm_tables_ready")
        trig_in, trig_out = sem("angles_ready"), sem("sines_ready")
        state_ready, state_used = sem("states_ready"), sem("states_used")
        y_ready, z_ready, glu_ready = sem("y_ready"), sem("z_ready"), sem("glu_ready")
        ssm_done, state_out = sem("ssm_done"), sem("state_rows_ready")
        p_max, p_exp, p_norm, p_turned = sem("p_max"), sem("p_exp"), sem("p_norm"), sem("p_turned")
        k_in, v_in = [sem(f"k_in{s}") for s in range(2)], [sem(f"v_in{s}") for s in range(2)]
        k_turned, s_scored, s_exp = sem("k_turned"), sem("s_scored"), sem("s_exp")
        s_max, s_norm, s_turned, s_pv = sem("s_max"), sem("s_norm"), sem("s_turned"), sem("s_pv")
        qz_ready, os_ready, o_ready = sem("qz_ready"), sem("os_ready"), sem("o_ready")
        k_used, v_used, s_free = sem("k_used"), sem("v_used"), sem("s_free")
        merged, x_step = sem("merged"), sem("residual_ready")
        ext_ready, conv_ready, gelu_ready = sem("ext_ready"), sem("conv_ready"), sem("gelu_ready")
        act_ready = sem("ffn_act_ready")
        p_in, ple_out, ple_ready, sig_ready = sem("p_in"), sem("ple_out"), sem("ple_ready"), sem("sig_ready")
        y_rows, c_rows = sem("y_rows"), sem("conv_rows")
        vec, sca = sem("vector_steps"), sem("scalar_steps")
        stored, state_stored = sem("stored"), sem("state_rows_stored")
        time_in, samples_ready, finals_ready = sem("time_in"), sem("sample_states_ready"), sem("final_states_ready")
        ple_ready_p, ple_filled = sem("p_transposed"), sem("ple_filled")
        params_in = sem("ssm_params_for_scalar")
        params, pool_steps = sem("ssm_params"), sem("pool_steps")
        act_params = sem("scalar_ssm_params")
        k_filled, k_freed = sem("turn_filled"), [sem("turn_freed_scalar"), sem("turn_freed_vector")]
        pv_done, pv_out = sem("pv_done"), sem("pv_out")
        c_stored, y_stored = [sem(f"conv_rows_stored{s}") for s in range(3)], [sem(f"y_stored{s}") for s in range(2)]
        c_turned, y_turned = sem("conv_rows_turned"), sem("y_turned")
        prompt_o = sem("prompt_attended")

        def fill_wait(pe, m):
            if m >= 4:
                pe.wait_ge(freed[m % 4], m // 4)

        def col(r):
            return cols[:, r:r + 1]

        def rows(tt):
            return P if tt < 2 else TS

        conv_at = [(fw[:, 0:3072], 0, 24), (fg[:, 6144:9216], 24, 24), (fq[:, 0:3072], 48, 24), (fh[:, 0:1792], 72, 14)]
        xn = fg[:, 0:6144].rearrange("p (j n) -> p j n", j=3)
        fo = oT[:].rearrange("p k t -> p (k t)")
        fi = fq[:, 12 * NT:20 * NT]
        idx_raw = fw[:, 0:4096].rearrange("p (b j n) -> p b j n", b=4, j=8)
        idxT = fg[:, 0:8192].rearrange("p (b n) -> p b n", b=NB)
        qb = fg[:, 8192:9216].rearrange("p (b n) -> p b n", b=NB)
        relu = fo[:, 0:2048].rearrange("p (r n) -> p r n", r=4)
        wheads = wmask[:].rearrange("p (b q) t -> p b (q t)", b=NB)
        nk = sc[:, 0:32].rearrange("p (b t) -> p b t", b=NB)
        m8 = sc[:, 32:40]
        dt_raw = sc[R_DT:R_DT + SPAIR, 0:2]
        bl = fi[:, 0:1024].rearrange("p (q r n) -> p q r n", q=4, r=2)
        cl = fi[:, 1024:2048].rearrange("p (j r c) -> p j r c", j=SPAIR, r=2)
        ini_raw = fi[:, 2048:2304].rearrange("p (r n) -> p r n", r=2)
        bus = area(fx, 2752, (2, NB, SPAIR, TQ))
        sst = area(fw, 512, (2, NB, SPAIR, TQ))
        ini = area(fw, 2048, (2, NB, SPAIR))
        braw = fw[:, 0:512].rearrange("p (r j c) -> p r j c", r=2, j=SPAIR)
        bbd = fw[:, 512:1536].rearrange("p (q r j g c) -> p q r j g c", q=4, r=2, j=4, g=2)
        craw = fw[:, 1536:2560].rearrange("p (q r d n) -> p q r d n", q=4, r=2, d=2)
        btmp = fw[:, 2560:3584].rearrange("p (k j c) -> p k j c", k=4, j=SPAIR)
        angle = area(fx, 2752, (2, SPAIR, 2 * T16))
        tables = area(fx, 0, (3, SPAIR, 2 * T16))
        rest = [area(fh, 2 * k * SPAIR * T16, (SPAIR, 2 * T16)) for k in range(2)]
        trig = [area(fh, 1024 + k * 512, (2, TP)) for k in range(2)]
        part = area(fh, 0, (2, TP))
        time = fh[:, 2048:2048 + 2 * T16]
        rot = [area(fh, 2304 + k * 512, (2, TP)) for k in range(2)]
        turned = area(fw, 0, (2, TP))
        states = [fh[:, 3584 + k * 512:4096 + k * 512].rearrange("p (r t) -> p r t", r=2) for k in range(2)]
        yt = fh[:, 0:1152].rearrange("p (k t) -> p k t", k=4)
        sg = fh[:, 1152:2304].rearrange("p (k t) -> p k t", k=4)
        rows_out = fw[:, 3712:4096].rearrange("p (r n) -> p r n", r=3)
        psc = [fw[:, 2560 + k * 256:2816 + k * 256] for k in range(2)]
        ppt = [fw[:, 3072 + k * 256:3328 + k * 256].rearrange("p (k t) -> p k t", k=2) for k in range(2)]
        kraw = [x[:, 0:4096].rearrange("p (j n) -> p j n", j=SLOT) for x in (fk, fh)]
        vraw = [fr[:, k * 4096:(k + 1) * 4096].rearrange("p (j n) -> p j n", j=SLOT) for k in range(2)]
        kT = fr[:, 4096:8192].rearrange("p (g n) -> p g n", g=2)
        qz = fi[:, 0:2048].rearrange("p (b g n) -> p b g n", b=NB, g=2)
        sp_ = fw[:, 0:PAST + TS]
        os_ = [fw[0:TS, 2080 + k * 256:2336 + k * 256] for k in range(2)]
        spT = fq[:, 0:2048].rearrange("p (j n) -> p j n", j=SLOT)
        spN = fq[0:TS, 2048:2176]
        ext = fg[:, 0:1224].rearrange("p (e s n) -> p e s n", e=2, s=2)
        cv = fg[:, 1224:2448].rearrange("p (e s n) -> p e s n", e=2, s=2)
        gl = fg[:, 2448:3060].rearrange("p (e n) -> p e n", e=2)
        taps = fg[:, 3060:3140].rearrange("p (e s n) -> p e s n", e=2, s=2)
        act_tmp = fg[:, 7748:8324].rearrange("p (e t) -> p e t", e=2)
        hi_ready, lo_ready = sem("high_parts_ready"), sem("low_parts_ready")
        h_tmp, h_high = sem("h_ready_to_split"), sem("h_high_ready")
        x_stored, x_back, ropes_in = sem("x_stored"), sem("x_back"), sem("ropes_in")
        o_high, o_split, z_high, z_split = sem("o_high"), sem("o_split"), sem("z_high"), sem("z_split")
        m_sum, m_high, a_high, a_sum = sem("merged_sum"), sem("merged_high"), sem("act_high"), sem("act_product")
        pn = fw[:, 0:768].rearrange("p (j n) -> p j n", j=3)
        pT = fw[:, 768:1344].rearrange("p (k t) -> p k t", k=2)
        pl = fg[:, 0:4608].rearrange("p (k t) -> p k t", k=KD)
        sig = fg[:, 4608:5760].rearrange("p (e k t) -> p e k t", e=2, k=2)
        crow = fg[:, 5760:8832].rearrange("p (e n) -> p e n", e=3)
        yrow = fw[:, 0:4096].rearrange("p (e n) -> p e n", e=2)
        C_GLU = 2 + 4 + 8 + 12 + 32
        w_in = a["w_in"][0]
        KC = KD // 2

        def load(sp, st, src, n):
            k = src.shape[0] // P
            if st.off is not None or st.c >= st.SLOTS:
                sp.wait_ge(used, st.count() - st.SLOTS)
            sp.dma_start(ring[:, st.slot(), 0:k * n].rearrange("p (k n) -> p k n", n=n),
                         src.rearrange("(k p) n -> p k n", p=P)).then_inc(landed[st.slot()], 16)
            st.c += 1

        def load_pair(sp, st, w, c0, width=256):
            for kc in range(2):
                load(sp, st, w[kc * KC * P:(kc + 1) * KC * P, bass.ds(c0, width)], width)

        def products(pe, st, pr, rhs, widths, chunks=2, kt=KC, norm=None):
            if pr.off is not None or pr.n[pr.s] > 0:
                pe.wait_ge(out[pr.s], pr.before())
            for kc in range(chunks):
                chunk(pe, st, [(2 * pr.s + n, width) for n, width in enumerate(widths)], rhs, kc * kt, kt,
                      kc == 0, kc == chunks - 1, norm)
            pr.step()

        def chunk(pe, st, cols_, rhs, k0, kt, first, last, norm=None):
            hi, lo = rhs
            total = sum(width for _, width in cols_)

            def tile(x, k, n, width):
                c = k * total + n * P
                return x[:, c:c + width]

            pe.wait_ge(hi_ready, st.split())
            for n, (b, width) in enumerate(cols_):
                for k in range(kt):
                    if norm is not None and n == 0 and (k0 + k) % 4 == 0:
                        pe.wait_ge(normed, 4 * norm + (k0 + k) // 4 + 1)
                    w = tile(highs[:, st.c % 2], k, n, width)
                    for x in (hi, lo):
                        nc.tensor.matmul(ps[0:width, b, 0:NT], w, x[:, k0 + k, :], start=(first and k == 0 and x is hi),
                                         stop=False, skip_group_check=True)
            pe.wait_ge(lo_ready, st.split())
            for n, (b, width) in enumerate(cols_):
                for k in range(kt):
                    mm = nc.tensor.matmul(ps[0:width, b, 0:NT], tile(lows[:, st.slot()], k, n, width), hi[:, k0 + k, :],
                                          start=False, stop=(last and k == kt - 1), skip_group_check=True)
            mm.then_inc(used, 1)
            st.c += 1

        def split_high(act, st, n=2048):
            act.wait_ge(landed[st.slot()], st.landed())
            if st.off is not None or st.c >= 2:
                act.wait_ge(used, st.count() - 2)
            nc.scalar.copy(highs[:, st.c % 2, 0:n], ring[:, st.slot(), 0:n]).then_inc(hi_ready, 1)
            st.c += 1

        def split_low(pool, st, n=2048):
            pool.wait_ge(hi_ready, st.split())
            nc.gpsimd.tensor_tensor(lows[:, st.slot(), 0:n], ring[:, st.slot(), 0:n], highs[:, st.c % 2, 0:n].bitcast(F32),
                                    ALU.subtract).then_inc(lo_ready, 1)
            st.c += 1

        def taken(eng, st, pr, chunks=2):
            s = pr.s
            eng.wait_ge(used, st.count(chunks - 1))
            st.c += chunks
            pr.step()
            return ps[:, 2 * s:2 * s + 2, 0:NT], out[s]

        def walk(st, pr, name):
            pairs, chunks = {"ikw": (1, 2), "u": (2, 2), "iq": (4, 2), "qkv": (6, 2), "gates": (16, 2),
                             "glu": (2, 1), "w_o": (8, 2)}[name]
            for _ in range(pairs):
                st.c += chunks
                pr.step()

        block = ctx.enter_context(nc.Block())

        def ffn(eng, st, pr, up, down, more=()):
            counted = ((st, 48),) + (((pr, 16),) if pr else ()) + tuple(more)
            for j in range(FG):
                up(j, 0, j)
            with eng.Fori(0, 2) as i:
                for x, per in counted:
                    x.begin(i, per)
                for gg in range(2):
                    for j in range(FG):
                        up(i * 16 + (FG * (1 + gg) + j), (1 + gg) % 2, j)
                    down(i * 16 + FG * gg, gg, FG)
            for x, _ in counted:
                x.end(2)
            for j in range(FT - 5 * FG):
                up(5 * FG + j, 1, j)
            down(4 * FG, 0, FG)
            down(5 * FG, 1, FT - 5 * FG)

        @block.sync
        def _(sp):
            st = Stream()
            for dst, src in ((mats[:], a["c_mats"]), (causal[:], a["c_causal"]),
                             (cnew[:], a["c_new"]), (rowsf[:], a["c_rows"]), (headsel[:], a["c_heads"]),
                             (wmask[:], a["c_wmask"]), (csub[:], a["c_sub"])):
                sp.dma_start(dst, src).then_inc(consts_in, 16)
            for j in range(2):
                sp.dma_start(xn[:, j, :], a["x_prompt"][0, j * P:(j + 1) * P, :]).then_inc(x_in, 16)
            sp.dma_start(xn[0:TS, 2, :], a["x_sample"].rearrange("b t d -> (b t) d")).then_inc(x_in, 16)
            for r, n, src in ((R_MIX, 16, "g_mix"), (R_FFN, 16, "g_ffn"), (R_PG, 16, "g_pg"), (R_PLE, 16, "g_ple"),
                              (R_GQ, 1, "g_q"), (R_GK, 1, "g_k"), (R_D, 4, "ssm_d")):
                sp.dma_start(small[r:r + n, :], a[src][0].rearrange("(k p) -> k p", p=P)).then_inc(small_in, 16)
            for r, src in ((R_ARE, "ssm_a_re"), (R_AIM, "ssm_a_im")):
                sp.dma_start(small[r:r + SPAIR, :], a[src][0].rearrange("(j g) n -> j (g n)", g=2)).then_inc(small_in, 16)
            sp.dma_start(dt_raw, a["ssm_log_dt"][0].rearrange("(j g) -> j g", g=2)).then_inc(small_in, 16)
            for dst, t0, n in conv_at:
                w = slice(t0 * P, (t0 + n) * P)
                sp.dma_start(dst[0:16, 0:n * P], a["state_conv"][0].rearrange("b r n -> (b r) n")[:, w]).then_inc(conv_in, 16)
                sp.dma_start(dst[16:19, 0:n * P], a["conv_w"][0][:, w]).then_inc(conv_in, 16)
                sp.dma_start(dst[19:20, 0:n * P], a["conv_b"][:, w]).then_inc(conv_in, 16)
            for kc in range(2):
                load(sp, st, w_in[kc * KC * P:(kc + 1) * KC * P, C_IK:C_U], C_U - C_IK)
            load_pair(sp, st, w_in, C_U)
            sp.wait_ge(x_ready, 12)
            sp.dma_start(x_saved, fx[:]).then_inc(x_stored, 16)
            sp.dma_start(ropes, a["c_rope"]).then_inc(ropes_in, 16)
            load_pair(sp, st, w_in, C_U + 256)
            for c0, times in ((C_IQ, 2), (C_Q, 3), (C_GA, 8)):
                with sp.Fori(0, times) as i:
                    st.begin(i, 4)
                    for n in range(2):
                        load_pair(sp, st, w_in, i * 512 + (c0 + n * 256))
                st.end(times)
            sp.wait_ge(tok_ready, 6)
            for tt in range(3):
                n = rows(tt)
                g = "prompt" if tt < 2 else "sample"
                r0 = tt * P if tt < 2 else 0
                for name, lo, w in (("k", 0, 256), ("v", 256, 256), ("idx_k", 512, 64)):
                    sp.dma_start(o[f"{name}_{g}"][r0:r0 + n, :], tok[0:n, tt, lo:lo + w]).then_inc(stored, 16)
            sp.wait_ge(sb_ready, 1)
            for r, part in enumerate(("re", "im")):
                sp.dma_start(braw[:, r], a[f"ssm_b_{part}"][0].rearrange("(j g) n c -> (g n) j c", g=2)).then_inc(ssm_in, 16)
                for d in range(2):
                    sp.dma_start(craw[:, :, r, d, :], a[f"ssm_c_{part}"][0].rearrange("(q r) c n -> (r c) q n", r=8)).then_inc(ssm_in, 16)
                sp.dma_start(ini_raw[:, r], a[f"state_ssm_{part}"][0].rearrange("b (j g) n -> (b j) (g n)", g=2)).then_inc(ssm_in, 16)
            sp.wait_ge(used, C_GLU)
            sp.dma_start(time, a["c_time"]).then_inc(time_in, 16)
            for n in range(2):
                load(sp, st, a["w_glu"][0][:, n * 256:(n + 1) * 256], 256)
            sp.wait_ge(state_out, 2)
            for r, part in enumerate(("re", "im")):
                sp.dma_start(o[f"ssm_{part}_prompt"], rows_out[r * SPAIR:(r + 1) * SPAIR, 0, :]).then_inc(state_stored, 16)
                sp.dma_start(o[f"ssm_{part}_sample"], rows_out[:, 1 + r, :]).then_inc(state_stored, 16)
            sp.wait_ge(o_ready, 2)
            with sp.Fori(0, 4) as i:
                st.begin(i, 4)
                for n in range(2):
                    c = bass.ds(i * 512 + n * 256, 256)
                    load(sp, st, a["w_att_br"][0][:, c], 256)
                    load(sp, st, a["w_ssm_br"][0][:, c], 256)
            st.end(4)
            with sp.Fori(0, 4) as i:
                st.begin(i, 4)
                for n in range(2):
                    load_pair(sp, st, a["w_o"][0], i * 512 + n * 256)
            st.end(4)

            def load_up(t):
                for half in range(2):
                    load(sp, st, a["w_up"][0][:, bass.ds(t * P + half * FF, P)], P)

            def load_down(t, k):
                for n in range(8):
                    load(sp, st, a["w_down"][0][bass.ds(t * P, k * P), n * 256:(n + 1) * 256], 256)

            ffn(sp, st, None, lambda t, g, j: load_up(t), lambda t, g, k: load_down(t, k))
            sp.wait_ge(act_ready, FT)
            for j in range(3):
                src = a["p_prompt"][0, 0, j * P:(j + 1) * P, :] if j < 2 else a["p_sample"][0].rearrange("b t n -> (b t) n")
                sp.dma_start(pn[0:rows(j), j, :], src).then_inc(p_in, 16)
            for n in range(2):
                load(sp, st, a["w_ple"][0][:, n * 1024:(n + 1) * 1024], 1024)
            with sp.Fori(0, 4) as i:
                st.begin(i, 4)
                for n in range(2):
                    load_pair(sp, st, a["w_pg"][0], i * 512 + n * 256)
            st.end(4)
            for j in range(3):
                sp.wait_ge(y_turned, 4 * (j + 1))
                dst = o["y_prompt"][j * P:(j + 1) * P, :] if j < 2 else o["y_sample"]
                sp.dma_start(dst, yrow[0:rows(j), j % 2, :]).then_inc(y_stored[j % 2], 16)
            sp.wait_ge(stored, 9 * 16)
            sp.wait_ge(state_stored, 4 * 16)
            for s in range(3):
                sp.wait_ge(c_stored[s], 32 * ((11 - s + 2) // 3))
            for s in range(2):
                sp.wait_ge(y_stored[s], 16 * (2 - s))

        @block.gpsimd
        def _(pool):
            st = Stream()
            for b in range(NB):
                pool.dma_start(pidx[:, b:b + 1], a["page_table"][b].unsqueeze(1).unsqueeze(1).to_broadcast([NPAGE, 8, 1])).then_inc(table_in, 16)
            pool.wait_ge(table_ready, 1)
            rows16 = a["cache_idx_k"][0].rearrange("n (r j) d -> (n r) (j d)", j=SLOT)
            pool.wait_ge(freed[0], 1)
            for b in range(NB):
                if b == 4:
                    for n in (640, 640) + 4 * (2048,):
                        split_low(pool, st, n)
                    with pool.Fori(0, 5) as i:
                        st.begin(i, 4)
                        for _ in range(4):
                            split_low(pool, st)
                    st.end(5)
                    pool.wait_ge(filled, UNITS["idx"] + 8)
                nc.gpsimd.indirect_dma_start(fw[:, b % 4 * 1024:(b % 4 + 1) * 1024], None, rows16,
                                             bass.IndirectOffsetOnAxis(ap=pidx[:, b:b + 1], axis=0)
                                             ).then_inc(idx_in[b // 4], 16)

            with pool.Fori(0, 8) as i:
                st.begin(i, 4)
                for _ in range(4):
                    split_low(pool, st)
            st.end(8)
            st.c += 2
            st.whole += 2

            pl_ = Steps(pool, pool_steps)
            G = nc.gpsimd
            x, r = rest
            pool.wait_ge(params, 1)
            pool.wait_ge(time_in, 16)
            when = time.unsqueeze(1).to_broadcast([P, SPAIR, 2 * T16])
            fa, fb = (ssmv[:, k, :].unsqueeze(2).to_broadcast([P, SPAIR, 2 * T16]) for k in (8, 9))
            pl_.link(G.tensor_tensor(x, when, fa, ALU.mult))
            pl_.link(G.tensor_scalar(r, x, MAGIC, MAGIC, ALU.add, ALU.subtract))
            pl_.link(G.tensor_tensor(x, x, r, ALU.subtract))
            pl_.link(G.tensor_tensor(r, when, fb, ALU.mult))
            pl_.link(G.tensor_tensor(x, x, r, ALU.add))
            for half in range(2):
                y = angle[:, half]
                if half:
                    pl_.link(G.tensor_scalar(x, x, 0.25, None, ALU.add))
                pl_.link(G.tensor_scalar(r, x, MAGIC, MAGIC, ALU.add, ALU.subtract))
                pl_.link(G.tensor_tensor(y, x, r, ALU.subtract))
                pl_.link(G.tensor_scalar(y, y, HALF, -HALF, ALU.min, ALU.max))
            pool.sem_inc(trig_in, 1)
            pool.wait_ge(trig_out, 3)
            for j in range(SPAIR):
                if j >= 2:
                    pool.wait_ge(state_ready, j - 1)
                first = [tables[:, k:k + 2, j, 0:T16].unsqueeze(3).to_broadcast([P, 2, T16, T16]) for k in (1, 0)]
                second = [tables[:, k, j, T16:2 * T16].unsqueeze(1).unsqueeze(1).to_broadcast([P, 2, T16, T16]) for k in (1, 2)]
                out_, tmp = (y.rearrange("p k (a b) -> p k a b", a=T16) for y in (trig[j % 2], part))
                pl_.mark(G.tensor_tensor(out_, first[0], second[0], ALU.mult))
                pl_.link(G.tensor_tensor(tmp, first[1], second[1], ALU.mult))
                pl_.link(G.tensor_tensor(trig[j % 2], trig[j % 2], part, ALU.add))
                pool.sem_inc(trig_ready, 1)
            rows_k = a["cache_k"][0].rearrange("n (r j) g d -> (n r) (j g d)", j=SLOT)
            rows_v = a["cache_v"][0].rearrange("n (r j) g d -> (n r) (j g d)", j=SLOT)
            def gather_k(b):
                if b >= 2:
                    pool.wait_ge(k_used, b - 1)
                G.indirect_dma_start((fk, fh)[b % 2][:, 0:4096], None, rows_k,
                                     bass.IndirectOffsetOnAxis(ap=pidx[:, b:b + 1], axis=0)).then_inc(k_in[b % 2], 16)

            def gather_v(b):
                if b >= 2:
                    pool.wait_ge(pv_done, b - 1)
                if b % 4 == 1:
                    pool.wait_ge(s_scored, b // 4 + 1)
                G.indirect_dma_start(fr[:, b % 2 * 4096:(b % 2 + 1) * 4096], None, rows_v,
                                     bass.IndirectOffsetOnAxis(ap=pidx[:, b:b + 1], axis=0)).then_inc(v_in[b % 2], 16)

            gather_k(0)
            gather_v(0)
            pool.wait_ge(glu_ready, 1)
            for gather, b in ((gather_k, 1), (gather_k, 2), (gather_k, 3), (gather_v, 1), (gather_k, 4), (gather_k, 5),
                              (gather_v, 2), (gather_v, 3), (gather_v, 4), (gather_k, 6), (gather_k, 7), (gather_v, 5),
                              (gather_v, 6), (gather_v, 7)):
                gather(b)

            with pool.Fori(0, 4) as i:
                st.begin(i, 4)
                for n in (2048, 1024, 2048, 1024):
                    split_low(pool, st, n)
            st.end(4)
            with pool.Fori(0, 4 + 31) as i:
                st.begin(i, 4)
                for _ in range(4):
                    split_low(pool, st)
            st.end(4 + 31)
            for n in 2 * (2048,) + 8 * ((FT - 5 * FG) * 256,):
                split_low(pool, st, n)
            st.c += 2
            st.whole += 2
            for n in range(11):
                pool.wait_ge(c_turned, min(2 * n + 2, 22))
                w = min(1024, 2 * FF - n * 1024)
                pool.dma_start(o["conv_prompt"][:, n * 1024:n * 1024 + w], crow[0:2, n % 3, 0:w]).then_inc(c_stored[n % 3], 16)
                pool.dma_start(o["conv_sample"][:, n * 1024:n * 1024 + w], crow[2:18, n % 3, 0:w]).then_inc(c_stored[n % 3], 16)
            with pool.Fori(0, 4) as i:
                st.begin(i, 4)
                for _ in range(4):
                    split_low(pool, st)
            st.end(4)

        @block.scalar
        def _(act):
            st, pr, ahead = Stream(), Pairs(), Stream()
            sq = fo.rearrange("p (s n) -> p s n", s=2)

            def square_x(base):
                for q in range(4):
                    if q >= 2:
                        act.wait_ge(squares_used, base + q - 1)
                    nc.scalar.activation(sq[:, q % 2, :], xT[:, 4 * q:4 * q + 4, :].rearrange("p k t -> p (k t)"),
                                         ACT.Square).then_inc(squares, 1)

            def root(n, x):
                act.wait_ge(var_ready, n)
                nc.scalar.activation(x, x, ACT.Sqrt).then_inc(rstd_ready, 1)

            def h_highs(nth):
                for q in range(4):
                    act.wait_ge(h_tmp, nth * 4 + q + 1)
                    nc.scalar.copy(rh[:, q * 4 * NT:(q + 1) * 4 * NT], norm_tmp[:, q % 2, :]).then_inc(h_high, 1)

            act.wait_ge(x_ready, 12)
            square_x(0)
            root(1, rstd[:, 0, :])
            h_highs(0)
            for n in (640, 640) + 4 * (2048,):
                split_high(act, ahead, n)
            with act.Fori(0, 5) as i:
                ahead.begin(i, 4)
                for _ in range(4):
                    split_high(act, ahead)
            ahead.end(5)
            for _ in range(2):
                split_high(act, ahead)
            for name in ("ikw", "u", "iq", "qkv"):
                walk(st, pr, name)
            act.wait_ge(a_out, 4)
            for j in range(12):
                if j < 10:
                    if j >= 4:
                        act.wait_ge(squares_used, 4 + j - 3)
                    nc.scalar.activation(oT[:, j % 4, :], qkvT[:, j, :], ACT.Square).then_inc(squares, 1)
                if j >= 2:
                    root(j, oT[:, 4 + (j - 2) % 4, :])
            act.wait_ge(x_ready, 12)
            for n in range(16):
                m = UNITS["idx"] + n
                act.wait_ge(filled, m + 1)
                nc.scalar.copy(idxT[:, n // 2, n % 2 * 512:(n % 2 + 1) * 512], ps[:, bank(m), :]).then_inc(freed[m % 4], 1)
            act.wait_ge(squares_used, 14)
            for n in range(16 + 24):
                m = UNITS["pidx"] + n
                w = 512 if n < 32 else TQ
                act.wait_ge(filled, m + 1)
                if 4 <= n < 20:
                    act.wait_ge(relu_summed, n - 3)
                elif n >= 20:
                    act.wait_ge(relu_weighed, n - 19)
                nc.scalar.activation(relu[:, n % 4, 0:w], ps[:, bank(m), 0:w], ACT.Relu).then_inc(freed[m % 4], 1)
                act.wait_ge(freed[m % 4], m // 4 + 1)
                act.sem_inc(relu_ready, 1)
            def gate_pairs(i, last):
                for n in range(2):
                    if not (last and n):
                        for _ in range(2):
                            split_high(act, ahead)
                    src, free = taken(act, st, pr)
                    nc.scalar.activation(gates[:, bass.ds(i * 4 + 2 * n, 2), :], src, ACT.Sigmoid).then_inc(free, 1)

            with act.Fori(0, 7) as i:
                for x, per in ((ahead, 4), (st, 4), (pr, 1)):
                    x.begin(i, per)
                gate_pairs(i, False)
            for x in (ahead, st, pr):
                x.end(7)
            gate_pairs(7, True)
            assert ahead.c == st.c
            ahead.c += 2


            nc.scalar.activation(ssmv[:, 0, :], cols[:, R_DT:R_DT + SPAIR], ACT.Exp).then_inc(act_params, 1)
            act.wait_ge(params_in, 1)
            nc.scalar.activation(ssmv[:, 3, :], ssmv[:, 1, :], ACT.Exp).then_inc(act_params, 1)
            act.wait_ge(params_in, 2)
            nc.scalar.activation(ssmv[:, 12:14, :], ssmv[:, 10:12, :], ACT.Sin, scale=TURN).then_inc(act_params, 1)
            act.wait_ge(trig_in, 1)
            for k, (half, sign) in enumerate(((0, -1), (1, 1), (0, 1))):
                nc.scalar.activation(tables[:, k], angle[:, half], ACT.Sin, scale=sign * TURN).then_inc(trig_out, 1)
            U = UNITS["step"]
            scale = HD ** -0.5
            for i in range(16):
                act.wait_ge(p_max, i + 1)
                w = P * (i % 2 + 1)
                nc.scalar.activation(psc[i % 2][:, 0:w], psc[i % 2][:, 0:w], ACT.Exp, bias=sc[:, 2 + i % 2:3 + i % 2], scale=scale,
                                     accum_out=sc[:, 4 + i % 2:5 + i % 2]).then_inc(p_exp, 1)
                m = U + 6 * i + 3
                act.wait_ge(filled, m + 1)
                if i >= 2:
                    act.wait_ge(filled, U + 6 * (i - 2) + 5)
                nc.scalar.copy(ppt[i % 2][:, 0:w // P, :], ps[:, bank(m), 0:w].rearrange("p (k t) -> p k t", t=P)).then_inc(freed[m % 4], 1)
                act.wait_ge(freed[m % 4], m // 4 + 1)
                act.sem_inc(p_turned, 1)
            for q in range(4):
                act.wait_ge(y_ready, q + 1)
                nc.scalar.activation(uT[:, q, :], yt[:, q, :], ACT.Gelu_apprx_tanh).then_inc(z_ready, 1)
            for n in range(2):
                src, free = taken(act, st, pr, 1)
                nc.scalar.activation(sg[:, 2 * n:2 * n + 2, :], src, ACT.Sigmoid).then_inc(free, 1)
            act.wait_ge(glu_ready, 1)
            nc.scalar.copy(rx[:, 0:4 * NT], fw[:, 4104:4104 + 4 * NT]).then_inc(z_high, 1)
            kk = Turns()

            def turn(dst, src):
                k = kk.next()
                if k % 2 == 0:
                    act.wait_ge(k_filled, k + 1)
                    nc.scalar.copy(dst, src(k % 2)).then_inc(k_freed[0], 1)

            for half in range(2):
                for b in range(4 * half, 4 * half + 4):
                    if b == 4:
                        act.wait_ge(pv_done, 4)
                    for n in range(8):
                        if b and kk.k % 2 == 0:
                            act.wait_ge(s_free, 8 * b + n - 7)
                        turn(kT[:, n // 4, n % 4 * 512:n % 4 * 512 + 512], lambda s: ps[:, s, :])
                act.wait_ge(s_max, half + 1)
                nc.scalar.activation(sp_[:, 0:PAST], ps[:, 4:8, :].rearrange("p k n -> p (k n)"), ACT.Exp, bias=sc[:, 11:12],
                                     scale=scale, accum_out=sc[:, 12:13]).then_inc(s_exp, 1)
                nc.scalar.activation(sp_[:, PAST:PAST + TS], ps[:, 3, 0:TS], ACT.Exp, bias=sc[:, 11:12],
                                     scale=scale, accum_out=sc[:, 13:14]).then_inc(s_exp, 1)
                for n in range(4):
                    turn(spT[:, 4 * n:4 * n + 4, :], lambda s: ps[:, s, :].rearrange("p (j n) -> p j n", j=4))
                turn(spN, lambda s: ps[0:TS, s, 0:P])
                for b in range(4 * half, 4 * half + 4):
                    t0 = TP + b * TQ
                    for g in range(2):
                        if g:
                            kk.k -= 1
                        k = kk.next()
                        if k % 2 == 0:
                            act.wait_ge(k_filled, k + 1)
                            ins = nc.scalar.copy(oT[:, g * 4:g * 4 + 4, t0:t0 + TQ],
                                                 ps[:, 0, g * 48:g * 48 + 16].rearrange("p (r t) -> p r t", t=TQ))
                            if g:
                                ins.then_inc(k_freed[0], 1)
            act.wait_ge(k_freed[0], (kk.k + 1) // 2)
            act.sem_inc(o_ready, 1)
            act.wait_ge(o_ready, 2)
            nc.scalar.copy(rh[:, 0:HEADS * NT], fo).then_inc(o_high, 1)
            for n in (2048, 1024):
                split_high(act, ahead, n)
            for n in range(8):
                for w in (2048, 1024) if n < 7 else (2048, 2048):
                    split_high(act, ahead, w)
                act.wait_ge(m_sum, n + 1)
                nc.scalar.copy(m_hi[:, 2 * n:2 * n + 2, :], gates[:, 2 * n:2 * n + 2, :]).then_inc(m_high, 1)
            act.wait_ge(merged, 8)
            act.dma_start(fx[:], x_saved).then_inc(x_back, 16)
            with act.Fori(0, 4) as i:
                ahead.begin(i, 4)
                for _ in range(4):
                    split_high(act, ahead)
            ahead.end(4)
            st.c += 16
            walk(st, pr, "w_o")
            act.wait_ge(x_step, 1)
            square_x(14)
            root(12, rstd[:, 0, :])
            h_highs(1)

            def up(t, g, j):
                s, e = pr.s, pr.s
                for _ in range(2):
                    split_high(act, ahead)
                act.wait_ge(used, st.count(1))
                if pr.off is not None or j >= 2 or g:
                    act.wait_ge(conv_ready, t - 1)
                src = ps[:, 2 * s:2 * s + 2, :]
                nc.scalar.copy(ext[:, e, :, 2:2 + TP], src[:, :, 0:TP])
                nc.scalar.copy(ext[:, e, :, EXT_S:EXT].rearrange("p s (b t) -> p s b t", b=NB)[:, :, :, 2:2 + TQ],
                               src[:, :, TP:NT].rearrange("p s (b t) -> p s b t", b=NB)).then_inc(out[s], 1)
                act.wait_ge(out[s], pr.before() + 1)
                act.sem_inc(ext_ready, 1)
                st.c += 2
                pr.step()
                act.wait_ge(conv_ready, t + 1)
                nc.scalar.activation(gl[:, e, 0:CONVN], cv[:, e, 0, 0:CONVN], ACT.Gelu_apprx_tanh).then_inc(gelu_ready, 1)
                act.wait_ge(a_sum, t + 1)
                nc.scalar.copy(acts_hi[:, g, j, :], act_tmp[:, e, :]).then_inc(a_high, 1)

            def skip_down(t, g, k):
                last, small = k < FG, (FT - 5 * FG) * 256
                before_last = ahead.off is None and not last
                for n in range(8):
                    if not (last and n >= 6):
                        split_high(act, ahead, small if last or (before_last and n >= 6) else 2048)
                    st.c += 1
                    pr.step()

            ffn(act, st, pr, up, skip_down, ((ahead, 48),))
            assert ahead.c == st.c
            ahead.c += 2
            act.wait_ge(x_step, 2)
            square_x(18)
            root(13, rstd[:, 0, :])
            h_highs(2)
            act.wait_ge(ple_out, 8)
            for q in range(4):
                if q >= 2:
                    act.wait_ge(squares_used, 22 + q - 1)
                nc.scalar.activation(sq[:, q % 2, :], pl[:, 4 * q:4 * q + 4, :].rearrange("p k t -> p (k t)"),
                                     ACT.Square).then_inc(squares, 1)
            for _ in range(2):
                split_high(act, ahead)
            root(14, rstd[:, 1, :])
            for _ in range(8):
                pr.step()
            st.c += 2

            def pg_pairs(i, last):
                for n in range(2):
                    if not (last and n):
                        for _ in range(2):
                            split_high(act, ahead)
                    src, free = taken(act, st, pr)
                    act.wait_ge(ple_ready, i * 2 + (1 + n))
                    nc.scalar.activation(sig[:, n, :, :], src, ACT.Sigmoid).then_inc(free, 1)
                    act.wait_ge(free, pr.n[pr.s ^ 1] + (0 if pr.off is None else i))
                    act.sem_inc(sig_ready, 1)

            with act.Fori(0, 3) as i:
                for x, per in ((ahead, 4), (st, 4), (pr, 1)):
                    x.begin(i, per)
                pg_pairs(i, False)
            for x in (ahead, st, pr):
                x.end(3)
            pg_pairs(3, True)

        @block.vector
        def _(ve):
            st, pr = Stream(), Pairs()
            v = Steps(ve, vec)
            V = nc.vector

            def evac(m, dst, src):
                ve.wait_ge(filled, m + 1)
                V.tensor_copy(dst, src).then_inc(freed[m % 4], 1)

            def norm_x(m, nth, row, turn, low):
                ve.wait_ge(filled, m + 1)
                V.tensor_scalar(rstd[:, 0, :], ps[:, bank(m), 0:NT], 1.0 / D, EPS, ALU.mult, ALU.add).then_inc(freed[m % 4], 1)
                ve.wait_ge(freed[m % 4], m // 4 + 1)
                ve.sem_inc(var_ready, 1)
                ve.wait_ge(rstd_ready, nth)
                v.link(V.reciprocal(rstd[:, 0, :], rstd[:, 0, :]))
                for q in range(5):
                    if q < 4:
                        if q >= 2:
                            ve.wait_ge(normed, 4 * turn + q - 1)
                        for k in range(4 * q, 4 * q + 4):
                            ins = V.scalar_tensor_tensor(norm_tmp[:, q % 2, k % 4 * NT:(k % 4 + 1) * NT], xT[:, k, :], col(row + k),
                                                         rstd[:, 0, :], ALU.mult, ALU.mult)
                        ins.then_inc(h_tmp, 1)
                    if q:
                        w = slice((q - 1) * 4 * NT, q * 4 * NT)
                        ve.wait_ge(h_high, 4 * turn + q)
                        V.tensor_tensor(low[:, w], norm_tmp[:, (q - 1) % 2, :], rh[:, w].bitcast(F32), ALU.subtract).then_inc(normed, 1)

            ve.wait_ge(small_in, 160)
            V.tensor_copy(small[R_DT:R_DT + SPAIR, :].rearrange("j (g n) -> j g n", g=2),
                          dt_raw.unsqueeze(2).to_broadcast([SPAIR, 2, N_SSM])).then_inc(small_ready, 1)
            for n, (_, t0, k) in enumerate(conv_at):
                m = UNITS["conv"] + n
                evac(m, convT[:, t0:t0 + k, :], ps[:, bank(m), 0:k * 20].rearrange("p (k r) -> p k r", r=20))
            m = UNITS["small"]
            evac(m, cols[:], ps[:, bank(m), 0:R_ALL])
            for n in range(12):
                m, j, q = UNITS["x"] + n, n // 4, n % 4
                w = rows(j)
                ve.wait_ge(filled, m + 1)
                V.tensor_copy(xT[:, 4 * q:4 * q + 4, j * P:j * P + w],
                              ps[:, bank(m), 0:4 * w].rearrange("p (k t) -> p k t", k=4)).then_inc(freed[m % 4], 1)
                ve.wait_ge(freed[m % 4], m // 4 + 1)
                ve.sem_inc(x_ready, 1)
            ve.wait_ge(x_stored, 16)
            norm_x(UNITS["norm0"], 1, R_MIX, 0, rx)
            ve.wait_ge(table_in, 128)
            ve.wait_ge(consts_in, 112)
            v.link(V.tensor_scalar(pidf[:], pidx[:], 8.0, csub[:, 0:1], ALU.mult, ALU.add))
            V.tensor_copy(pidx[:], pidf[:]).then_inc(table_ready, 1)

            ve.wait_ge(used, st.count(1))
            V.tensor_copy(ikT[0:80, :], ps[0:80, 0, 0:NT]).then_inc(out[0], 1)
            st.c += 2
            pr.step()
            for n in range(2):
                src, free = taken(ve, st, pr)
                V.tensor_copy(uT[:, 2 * n:2 * n + 2, :], src).then_inc(free, 1)
            for dst, times in ((iqT, 2), (qkvT, 3)):
                with ve.Fori(0, times) as i:
                    st.begin(i, 4)
                    pr.begin(i, 1)
                    for n in range(2):
                        src, free = taken(ve, st, pr)
                        V.tensor_copy(dst[:, bass.ds(i * 4 + 2 * n, 2), :], src).then_inc(free, 1)
                st.end(times)
                pr.end(times)
            for s in range(2):
                ve.wait_ge(out[s], pr.n[s])
                ve.sem_inc(a_out, 2)

            for j in range(12):
                if j < 10:
                    m = UNITS["qkn"] + j
                    ve.wait_ge(filled, m + 1)
                    if j >= 4:
                        ve.wait_ge(head_normed, j - 3)
                    V.tensor_scalar(oT[:, 4 + j % 4, :], ps[:, bank(m), 0:NT], 1.0 / HD, EPS, ALU.mult,
                                    ALU.add).then_inc(freed[m % 4], 1)
                    ve.wait_ge(freed[m % 4], m // 4 + 1)
                    ve.sem_inc(var_ready, 1)
                if j >= 2:
                    k = j - 2
                    ve.wait_ge(rstd_ready, 2 + k)
                    v.link(V.reciprocal(oT[:, 4 + k % 4, :], oT[:, 4 + k % 4, :]))
                    V.scalar_tensor_tensor(qkvT[:, k, :], qkvT[:, k, :], col(R_GQ if k < 8 else R_GK), oT[:, 4 + k % 4, :],
                                           ALU.mult, ALU.mult).then_inc(head_normed, 1)
            ve.wait_ge(head_normed, 10)

            def rope(m, x, cos, sin, n=P):
                ve.wait_ge(filled, m + 1)
                V.tensor_tensor(rstd[0:n, 0, :], x, ropes[0:n, cos, :], ALU.mult)
                v.link(V.tensor_tensor(rstd[0:n, 1, :], ps[0:n, bank(m), 0:NT], ropes[0:n, sin, :], ALU.mult))
                V.tensor_tensor(x, rstd[0:n, 0, :], rstd[0:n, 1, :], ALU.add).then_inc(freed[m % 4], 1)
                ve.wait_ge(freed[m % 4], m // 4 + 1)
                ve.sem_inc(roped, 1)

            ve.wait_ge(ropes_in, 16)
            for j in range(10):
                rope(UNITS["ropeq"] + j, qkvT[:, j, :], 0, 1)
            for j in range(8):
                rope(UNITS["ropei"] + j, iqT[:, j, :], 2, 3)
            rope(UNITS["ropei"] + 8, ikT[0:IDIM, :], 2, 3, IDIM)
            V.tensor_copy(ik2[0:IDIM, :], ikT[0:IDIM, :])
            v.link(V.tensor_copy(ik2[IDIM:P, :], ikT[0:IDIM, :]))
            v.mark(V.memset(qb, 0.0))
            v.link(V.memset(nk, 0.0))
            for j2 in range(2):
                for hp in range(2):
                    for b in range(NB):
                        t0 = TP + b * TQ
                        dst = qb[j2 * 64:j2 * 64 + 64, b, j2 * 64:j2 * 64 + 64].rearrange("p (h q t) -> p h q t", q=2, t=TQ)
                        v.mark(V.tensor_copy(dst[:, :, hp, :], iqT[hp * 64:hp * 64 + 64, :, t0:t0 + TQ]))
            v.link(V.tensor_copy(nk[0:IDIM], ikT[0:IDIM, TP:NT].rearrange("p (b t) -> p b t", t=TQ)))
            for n in range(6):
                m, tt = UNITS["tok"] + n, n // 2
                w, lo, hi = rows(tt), (0, 512)[n % 2], (512, 592)[n % 2]
                evac(m, tok[0:w, tt, lo:hi], ps[0:w, bank(m), 0:hi - lo])
                ve.wait_ge(freed[m % 4], m // 4 + 1)
                ve.sem_inc(tok_ready, 1)
            m = UNITS["wb"]
            ve.wait_ge(filled, m + 1)
            V.tensor_tensor(wmask[:], ps[:, bank(m), 0:TS].unsqueeze(1).to_broadcast([P, 2 * NB, TS]), wmask[:],
                            ALU.mult).then_inc(freed[m % 4], 1)
            ve.wait_ge(freed[m % 4], m // 4 + 1)
            ve.sem_inc(wb_ready, 1)

            for tt in range(2):
                s = pscore[:, tt, 0, :]
                for i in range(4):
                    for par in range(2):
                        n = tt * 8 + i * 2 + par
                        ve.wait_ge(relu_ready, n + 1)
                        for k in range(2):
                            h = 2 * (2 * i + k) + par
                            src, wt = relu[:, n % 4, k * 256:k * 256 + 256], tok[:, tt, 576 + h:577 + h]
                            if i == par == k == 0:
                                v.link(V.tensor_scalar(s, src, wt, None, ALU.mult))
                            else:
                                v.link(V.scalar_tensor_tensor(s, src, wt, s, ALU.mult, ALU.add))
                        ve.sem_inc(relu_summed, 1)
                v.link(V.tensor_tensor(s, s, causal[:, tt, :], ALU.add))
            S0, S1 = work[0:TS, 0, :], work[0:TS, 1, :]
            slots = S0[:, 0:PAST].rearrange("r (p j q) -> r q j p", j=8, q=2)
            for blk in range(2):
                ve.wait_ge(blk_scored, blk + 1)
                for q in range(2):
                    V.tensor_copy(slots[:, q, 4 * blk:4 * blk + 4, :],
                                  ps[q * TS:(q + 1) * TS, blk, :].rearrange("r (j p) -> r j p", j=4)).then_inc(blk_out, 1)
            ve.wait_ge(blk_scored, 3)
            V.tensor_tensor(S0[:, PAST:PAST + TQ], ps[0:TS, 2, 0:TQ], cnew[:, 0:TQ], ALU.add).then_inc(blk_out, 1)
            ve.wait_ge(blk_out, 5)

            def top(src, dst, k):
                for r in range(k // 8):
                    v.link(V.max(m8[0:src.shape[0]], src if r == 0 else dst))
                    v.link(V.match_replace(dst, m8[0:src.shape[0]], src if r == 0 else dst, TAKEN))

            for tt in range(2):
                s, left = pscore[:, tt, 0, :], pscore[:, tt, 1, :]
                top(s, left, TOPK_P)
                v.link(V.tensor_scalar(left, left, TAKEN / 1.5, OFF, ALU.is_ge, ALU.mult))
                V.tensor_tensor(left, left, causal[:, tt, :], ALU.add).then_inc(pb_ready, 1)
            top(S0, S1, TOPK_S)
            V.tensor_scalar(selb[:, 0:PAST].rearrange("r (j p) -> r j p", j=SLOT),
                            S1[:, 0:PAST].rearrange("r (p j) -> r j p", j=SLOT), TAKEN / 1.5, OFF, ALU.is_ge, ALU.mult)
            v.link(V.tensor_scalar(sc[0:TS, 40:44], S1[:, PAST:PAST + TQ], TAKEN / 1.5, OFF, ALU.is_ge, ALU.mult))
            V.tensor_tensor(selb[:, PAST:PAST + TS].rearrange("r (b t) -> r b t", t=TQ),
                            sc[0:TS, 40:44].unsqueeze(1).to_broadcast([TS, NB, TQ]),
                            cnew[:, TQ:TQ + TS].rearrange("r (b t) -> r b t", t=TQ), ALU.add).then_inc(sb_ready, 1)

            v.link(V.tensor_copy(rowsb[:], rowsf[:]))
            for name in ("gates",):
                walk(st, pr, name)

            def q_(k):
                return ssmv[:, k, :]

            are, aim = cols[:, R_ARE:R_ARE + SPAIR], cols[:, R_AIM:R_AIM + SPAIR]

            def tt(d, x, y, op):
                v.link(V.tensor_tensor(d, x, y, op))

            ve.wait_ge(act_params, 1)
            v.link(V.tensor_tensor(q_(1), are, q_(0), ALU.mult))
            ve.sem_inc(params_in, 1)
            tt(q_(2), aim, q_(0), ALU.mult)
            v.link(V.tensor_scalar(q_(4), q_(2), 1.0 / TURN, MAGIC, ALU.mult, ALU.add))
            v.link(V.tensor_scalar(q_(4), q_(4), MAGIC, None, ALU.subtract))
            v.link(V.scalar_tensor_tensor(q_(5), q_(4), -TURN_HI, q_(2), ALU.mult, ALU.add))
            v.link(V.scalar_tensor_tensor(q_(5), q_(4), -TURN_LO, q_(5), ALU.mult, ALU.add))
            v.link(V.tensor_scalar(q_(6), q_(5), 1.0 / TURN, None, ALU.mult))
            v.link(V.tensor_scalar(q_(8), q_(6), COARSE, COARSE, ALU.add, ALU.subtract))
            v.link(V.scalar_tensor_tensor(q_(7), q_(8), -TURN_HI, q_(5), ALU.mult, ALU.add))
            v.link(V.scalar_tensor_tensor(q_(7), q_(8), -TURN_LO, q_(7), ALU.mult, ALU.add))
            v.link(V.tensor_scalar(q_(9), q_(7), 1.0 / TURN, None, ALU.mult))
            ve.sem_inc(params, 1)
            for k, shift in ((10, 0.0), (11, 0.25)):
                v.link(V.tensor_scalar(q_(k), q_(6), shift, None, ALU.add))
                v.link(V.tensor_scalar(q_(4), q_(k), MAGIC, MAGIC, ALU.add, ALU.subtract))
                tt(q_(k), q_(k), q_(4), ALU.subtract)
                v.link(V.tensor_scalar(q_(k), q_(k), HALF, -HALF, ALU.min, ALU.max))
            ve.sem_inc(params_in, 1)
            tt(q_(4), are, are, ALU.mult)
            tt(q_(5), aim, aim, ALU.mult)
            tt(q_(4), q_(4), q_(5), ALU.add)
            v.link(V.reciprocal(q_(18), q_(4)))
            ve.wait_ge(act_params, 3)
            tt(q_(14), q_(3), q_(13), ALU.mult)
            tt(q_(15), q_(3), q_(12), ALU.mult)
            v.link(V.tensor_scalar(q_(4), q_(14), -1.0, None, ALU.add))
            tt(q_(5), q_(4), are, ALU.mult)
            tt(q_(6), q_(15), aim, ALU.mult)
            tt(q_(5), q_(5), q_(6), ALU.add)
            tt(q_(16), q_(5), q_(18), ALU.mult)
            tt(q_(5), q_(15), are, ALU.mult)
            tt(q_(6), q_(4), aim, ALU.mult)
            tt(q_(5), q_(5), q_(6), ALU.subtract)
            tt(q_(17), q_(5), q_(18), ALU.mult)
            ve.wait_ge(ssm_in, 16 * 8)
            v.link(V.memset(bbd, 0.0))
            v.mark(V.memset(cl, 0.0))
            f = [q_(k).unsqueeze(2).to_broadcast([P, SPAIR, C_SSM]) for k in (16, 17)]
            for k, (x, y) in enumerate(((0, 0), (1, 1), (0, 1), (1, 0))):
                v.mark(V.tensor_tensor(btmp[:, k], f[x], braw[:, y], ALU.mult))
            v.wait()
            for g in range(2):
                r = slice(64 * g, 64 * g + 64)
                for ri, op in ((0, ALU.subtract), (1, ALU.add)):
                    x, y = (btmp[r, 2 * ri + k].rearrange("p (q j) c -> p q j c", q=4) for k in range(2))
                    ins = V.tensor_tensor(bbd[r, :, ri, :, g, :], x, y, op)
                    v.mark(ins)
            v.wait()
            ve.sem_inc(ssm_tabs, 1)
            for n in range(2):
                m = UNITS["bt"] + n
                evac(m, bl[:, 2 * n:2 * n + 2], ps[:, bank(m), :].rearrange("p (q r n) -> p q r n", q=2, r=2))
            for n in range(2):
                m = UNITS["ct"] + n
                ve.wait_ge(filled, m + 1)
                src = ps[:, bank(m), :].rearrange("p (q r j g c) -> p q r j g c", q=2, r=2, j=4, g=2)
                for g in range(2):
                    p_ = slice(64 * g, 64 * g + 64)
                    for ri in range(2):
                        for q in range(2):
                            j0 = 4 * (2 * n + q)
                            v.mark(V.tensor_scalar(cl[p_, j0:j0 + 4, ri, g * 16:g * 16 + 16], src[p_, q, ri, :, g, :],
                                                   -1.0 if ri else 1.0, None, ALU.mult))
                v.wait()
                ve.sem_inc(freed[m % 4], 1)
            m = UNITS["ini"]
            for k in range(2):
                evac(m + k, fw[:, 2048 + k * P:2048 + (k + 1) * P], ps[:, bank(m + k), 0:P])
                ve.wait_ge(freed[(m + k) % 4], (m + k) // 4 + 1)
            ve.sem_inc(ssm_tabs, 1)

            U = UNITS["step"]

            def scores(i):
                m = U + 6 * i - 4 if i else UNITS["first"]
                w, t, k = P * (i % 2 + 1), i % 2, i % 2
                ve.wait_ge(filled, m + 1)
                if i >= 2:
                    ve.wait_ge(p_turned, i - 1)
                V.tensor_tensor_reduce(psc[k][:, 0:w], ps[:, bank(m), 0:w], pscore[:, t, 1, 0:w], 1.0, -3.0e38, ALU.add, ALU.max,
                                       accum_out=sc[:, k:k + 1]).then_inc(freed[m % 4], 1)
                ve.wait_ge(freed[m % 4], m // 4 + 1)
                V.tensor_scalar(sc[:, 2 + k:3 + k], sc[:, k:k + 1], -(HD ** -0.5), None, ALU.mult).then_inc(p_max, 1)

            def keep(i):
                m = U + 6 * i + 4
                evac(m, oT[:, i // 2, i % 2 * P:(i % 2 + 1) * P], ps[:, bank(m), 0:P])

            def normalize(i):
                k, w = i % 2, P * (i % 2 + 1)
                ve.wait_ge(p_exp, i + 1)
                v.link(V.reciprocal(sc[:, 6 + k:7 + k], sc[:, 4 + k:5 + k]))
                V.tensor_scalar(psc[k][:, 0:w], psc[k][:, 0:w], sc[:, 6 + k:7 + k], None, ALU.mult).then_inc(p_norm, 1)

            scores(0)
            by_cos, by_sin = rot
            for j in range(SPAIR):
                if j:
                    keep(j - 1)
                normalize(j)
                if j < 15:
                    scores(j + 1)
                mr = UNITS["step"] + 6 * j
                ve.wait_ge(filled, mr + 2)
                ve.wait_ge(trig_ready, j + 1)
                cs, sn = (trig[j % 2][:, k, :].unsqueeze(1).to_broadcast([P, 2, TP]) for k in range(2))
                both_ = ps[:, bank(mr):bank(mr) + 2, :]
                v.mark(V.tensor_tensor(by_cos, both_[:, :, 0:TP], cs, ALU.mult))
                v.mark(V.tensor_tensor(by_sin, both_[:, :, 0:TP], sn, ALU.mult))
                v.mark(V.tensor_copy(bus[:, :, :, j, :], both_[:, :, TP:NT].rearrange("p r (b t) -> p r b t", b=NB)))
                v.wait()
                for m in (mr, mr + 1):
                    ve.sem_inc(freed[m % 4], 1)
                v.mark(V.tensor_tensor(turned[:, 0], by_cos[:, 0], by_sin[:, 1], ALU.add))
                v.link(V.tensor_tensor(turned[:, 1], by_cos[:, 1], by_sin[:, 0], ALU.subtract))
                mag = ssmv[:, 3, j:j + 1].to_broadcast([P, TP])
                for k in range(2):
                    v.mark(V.tensor_tensor_scan(by_cos[:, k], mag, turned[:, k], 0.0, ALU.mult, ALU.add))
                v.wait()
                if j >= 2:
                    ve.wait_ge(state_used, j - 1)
                S = states[j % 2]
                v.mark(V.tensor_tensor(by_sin, by_cos, sn, ALU.mult))
                v.link(V.tensor_tensor(turned, by_cos, cs, ALU.mult))
                v.mark(V.tensor_tensor(S[:, 0], turned[:, 0], by_sin[:, 1], ALU.subtract))
                v.link(V.tensor_tensor(S[:, 1], turned[:, 1], by_sin[:, 0], ALU.add))
                ve.sem_inc(state_ready, 1)
                v.mark(V.tensor_copy(ssmv[:, 20:22, j:j + 1], S[:, :, TP - 1:TP]))
            v.wait()
            keep(15)
            assert UNITS["step"] % 2 == 0
            ab = [q_(k).unsqueeze(1).to_broadcast([P, NB, SPAIR]) for k in (14, 15)]
            w_ = [fw[:, 1536 + 128 * k:1664 + 128 * k].rearrange("p (b j) -> p b j", b=NB) for k in range(4)]
            for t in range(TQ):
                prev = [ini[:, r] if t == 0 else sst[:, r, :, :, t - 1] for r in range(2)]
                for k, (x, y) in enumerate(((0, 0), (1, 1), (0, 1), (1, 0))):
                    v.mark(V.tensor_tensor(w_[k], ab[x], prev[y], ALU.mult))
                v.wait()
                v.mark(V.tensor_tensor(w_[0], w_[0], w_[1], ALU.subtract))
                v.link(V.tensor_tensor(w_[2], w_[2], w_[3], ALU.add))
                v.mark(V.tensor_tensor(sst[:, 0, :, :, t], w_[0], bus[:, 0, :, :, t], ALU.add))
                v.link(V.tensor_tensor(sst[:, 1, :, :, t], w_[2], bus[:, 1, :, :, t], ALU.add))
            ve.sem_inc(samples_ready, 1)
            for q in range(4):
                ve.wait_ge(state_used, 16 + 4 * (q + 1))
                if q == 0:
                    ve.wait_ge(trig_ready, SPAIR)
                V.scalar_tensor_tensor(yt[:, q, :], uT[:, q, :], col(R_D + q), ps[:, q, 0:NT], ALU.mult, ALU.add).then_inc(y_ready, 1)
            m = UNITS["fin"]
            evac(m, rows_out[0:2 * SPAIR, 0, :], ps[0:2 * SPAIR, bank(m), 0:P])
            ve.wait_ge(freed[m % 4], m // 4 + 1)
            ve.sem_inc(state_out, 1)
            evac(m + 1, rows_out[:, 1:3, :], ps[:, bank(m + 1), 0:256].rearrange("p (r n) -> p r n", r=2))
            ve.wait_ge(freed[(m + 1) % 4], (m + 1) // 4 + 1)
            ve.sem_inc(state_out, 1)
            for n in range(2):
                _, free = pr.s, out[pr.s]
                st.c += 1
                pr.step()
                ve.wait_ge(free, pr.n[pr.s ^ 1])
            v.link(V.tensor_tensor(uT, uT, sg, ALU.mult))
            ve.sem_inc(glu_ready, 1)
            ve.wait_ge(z_high, 1)
            V.tensor_tensor(z_lo, uT, z_hi.bitcast(F32), ALU.subtract).then_inc(z_split, 1)

            v.link(V.memset(fi[:, 0:2048], 0.0))
            for b in range(NB):
                for g in range(2):
                    c0 = b % 4 * 32 + g * 16
                    v.mark(V.tensor_copy(qz[:, b, g, c0:c0 + 16].rearrange("p (r t) -> p r t", t=TQ),
                                         qkvT[:, g * 4:g * 4 + 4, TP + b * TQ:TP + (b + 1) * TQ]))
            v.wait()
            ve.sem_inc(qz_ready, 1)
            kk = Turns()

            def turn(dst, src):
                k = kk.next()
                if k % 2:
                    ve.wait_ge(k_filled, k + 1)
                    V.tensor_copy(dst, src(k % 2)).then_inc(k_freed[1], 1)

            ve.wait_ge(state_stored, 64)
            for half in range(2):
                for b in range(4 * half, 4 * half + 4):
                    if b == 4:
                        ve.wait_ge(pv_done, 4)
                    for n in range(8):
                        if b and kk.k % 2:
                            ve.wait_ge(s_free, 8 * b + n - 7)
                        turn(kT[:, n // 4, n % 4 * 512:n % 4 * 512 + 512], lambda s: ps[:, s, :])
                ve.wait_ge(s_free, 32 * (half + 1))
                v.mark(V.tensor_reduce(sc[:, 8:9], ps[:, 4:8, :].rearrange("p k n -> p (k n)"), AX, ALU.max))
                v.link(V.tensor_reduce(sc[:, 9:10], ps[:, 3, 0:TS], AX, ALU.max))
                v.link(V.tensor_tensor(sc[:, 10:11], sc[:, 8:9], sc[:, 9:10], ALU.max))
                v.link(V.tensor_scalar(sc[:, 11:12], sc[:, 10:11], -(HD ** -0.5), None, ALU.mult))
                ve.sem_inc(s_max, 1)
                ve.wait_ge(s_exp, 2 * half + 2)
                v.link(V.tensor_tensor(sc[:, 14:15], sc[:, 12:13], sc[:, 13:14], ALU.add))
                v.link(V.reciprocal(sc[:, 15:16], sc[:, 14:15]))
                V.tensor_scalar(sp_, sp_, sc[:, 15:16], None, ALU.mult).then_inc(s_norm, 1)
                for n in range(4):
                    turn(spT[:, 4 * n:4 * n + 4, :], lambda s: ps[:, s, :].rearrange("p (j n) -> p j n", j=4))
                turn(spN, lambda s: ps[0:TS, s, 0:P])

                def spread(b):
                    t0 = TP + b * TQ
                    k = kk.next()
                    if k % 2:
                        ve.wait_ge(k_filled, k + 1)
                        for g in range(2):
                            ins = V.tensor_copy(oT[:, g * 4:g * 4 + 4, t0:t0 + TQ],
                                                ps[:, 1, g * 48:g * 48 + 16].rearrange("p (r t) -> p r t", t=TQ))
                        ins.then_inc(k_freed[1], 1)

                for b in range(4 * half, 4 * half + 4):
                    ve.wait_ge(pv_done, b + 1)
                    if b % 4 >= 2:
                        ve.wait_ge(k_filled, kk.k)
                    V.tensor_copy(os_[b % 2], ps[0:TS, 2 + b % 2, 0:256]).then_inc(os_ready, 1)
                    if b % 4:
                        spread(b - 1)
                spread(4 * half + 3)
            ve.wait_ge(k_freed[1], kk.k // 2)
            ve.sem_inc(o_ready, 1)

            ve.wait_ge(o_high, 1)
            V.tensor_tensor(o_lo, oT[:], o_hi.bitcast(F32), ALU.subtract).then_inc(o_split, 1)

            for n in range(8):
                s = n % 2
                ve.wait_ge(used, st.count(1))
                t0, t1_ = gates[:, 2 * n:2 * n + 2, :], gates[:, KD + 2 * n:KD + 2 * n + 2, :]
                v.mark(V.tensor_tensor(t0, t0, ps[:, 4 * s:4 * s + 2, 0:NT], ALU.mult))
                v.link(V.tensor_tensor(t1_, t1_, ps[:, 4 * s + 2:4 * s + 4, 0:NT], ALU.mult))
                v.link(V.tensor_tensor(t0, t0, t1_, ALU.add))
                ve.sem_inc(m_sum, 1)
                ve.wait_ge(m_high, n + 1)
                k = slice(2 * n, 2 * n + 2)
                V.tensor_tensor(m_lo[:, k, :], t0, m_hi[:, k, :].bitcast(F32), ALU.subtract).then_inc(merged, 1)
                st.c += 2
            ve.wait_ge(x_back, 16)
            with ve.Fori(0, 4) as i:
                st.begin(i, 4)
                pr.begin(i, 1)
                for n in range(2):
                    src, free = taken(ve, st, pr)
                    x = xT[:, bass.ds(i * 4 + 2 * n, 2), :]
                    V.tensor_tensor(x, x, src, ALU.add).then_inc(free, 1)
            st.end(4)
            pr.end(4)
            for s in range(2):
                ve.wait_ge(out[s], pr.n[s])
            ve.sem_inc(x_step, 1)
            norm_x(UNITS["norm1"], 12, R_FFN, 1, rw)

            ve.wait_ge(stored, 9 * 16)
            conv_cols = convT[:].rearrange("p (s f) r -> p s f r", s=2)
            v.mark(V.memset(ext[:, :, :, 0:2], 0.0))
            ext_s = ext[:, :, :, EXT_S:EXT].rearrange("p e s (b t) -> p e s b t", b=NB)
            cout_s = cout[:, :, :, 2:18].rearrange("p s f (b t) -> p s f b t", b=NB)
            gl_s = gl[:, :, EXT_S:EXT].rearrange("p e (b t) -> p e b t", b=NB)
            cv_s = cv[:, :, 1, EXT_S:EXT].rearrange("p e (b t) -> p e b t", b=NB)

            def up(t, g, j):
                e = pr.s
                v.link(V.tensor_copy(taps[:, e], conv_cols[:, :, bass.ds(t, 1), :].rearrange("p s o r -> p s (o r)")))
                v.link(V.tensor_copy(ext_s[:, e, :, :, 0:2], taps[:, e, :, 0:16].rearrange("p s (b r) -> p s b r", b=NB)))
                ve.wait_ge(ext_ready, t + 1)
                if pr.off is not None or j >= 2 or g:
                    ve.wait_ge(gelu_ready, t - 1)
                for s in range(2):
                    v.mark(V.tensor_scalar(cv[:, e, s, 0:CONVN], ext[:, e, s, 0:CONVN], taps[:, e, s, 16:17], taps[:, e, s, 19:20],
                                           ALU.mult, ALU.add))
                for k in (1, 2):
                    v.wait()
                    for s in range(2):
                        ins = V.scalar_tensor_tensor(cv[:, e, s, 0:CONVN], ext[:, e, s, k:k + CONVN], taps[:, e, s, 16 + k:17 + k],
                                                     cv[:, e, s, 0:CONVN], ALU.mult, ALU.add)
                        v.mark(ins)
                one = bass.ds(t, 1)
                v.mark(V.tensor_copy(cout[:, :, one, 0:2].rearrange("p s o r -> p s (o r)"), ext[:, e, :, TP:TP + 2]))
                for s in range(2):
                    v.mark(V.tensor_copy(cout_s[:, s, one].rearrange("p o b t -> p (o b) t"), ext_s[:, e, s, :, TQ:TQ + 2]))
                v.wait()
                ve.sem_inc(conv_ready, 1)
                ve.wait_ge(gelu_ready, t + 1)
                v.mark(V.tensor_tensor(act_tmp[:, e, 0:TP], gl[:, e, 0:TP], cv[:, e, 1, 0:TP], ALU.mult))
                v.link(V.tensor_tensor(act_tmp[:, e, TP:NT].rearrange("p (b t) -> p b t", b=NB), gl_s[:, e, :, 0:TQ],
                                       cv_s[:, e, :, 0:TQ], ALU.mult))
                ve.sem_inc(a_sum, 1)
                ve.wait_ge(a_high, t + 1)
                v.link(V.tensor_tensor(acts_lo[:, g, j, :], act_tmp[:, e, :], acts_hi[:, g, j, :].bitcast(F32), ALU.subtract))
                ve.sem_inc(act_ready, 1)
                st.c += 2
                pr.step()

            def down(t, g, k):
                for n in range(8):
                    src, free = taken(ve, st, pr, 1)
                    x = xT[:, 2 * n:2 * n + 2, :]
                    V.tensor_tensor(x, x, src, ALU.add).then_inc(free, 1)

            ffn(ve, st, pr, up, down, ((v, 2 * FG * UP_STEPS),))
            for s in range(2):
                ve.wait_ge(out[s], pr.n[s])
            ve.sem_inc(x_step, 1)
            for n in range(22):
                m = UNITS["cout"] + n
                w = min(512, 2 * FF - n * 512)
                ve.wait_ge(filled, m + 1)
                if n >= 6:
                    ve.wait_ge(c_stored[n // 2 % 3], 32 * (n // 2 // 3))
                V.tensor_copy(crow[0:18, n // 2 % 3, n % 2 * 512:n % 2 * 512 + w], ps[0:18, bank(m), 0:w]).then_inc(freed[m % 4], 1)
                ve.wait_ge(freed[m % 4], m // 4 + 1)
                ve.sem_inc(c_turned, 1)
            for n in range(2):
                m = UNITS["pt"] + n
                evac(m, pT[:, n, :], ps[:, bank(m), 0:NT])
                ve.wait_ge(freed[m % 4], m // 4 + 1)
                ve.sem_inc(ple_ready_p, 1)
            for n in range(8):
                s = pr.s
                ve.wait_ge(ple_filled, n + 1)
                V.tensor_copy(pl[:, 2 * n:2 * n + 2, :], ps[:, 2 * s:2 * s + 2, 0:NT]).then_inc(out[s], 1)
                pr.step()
                ve.wait_ge(out[s], pr.n[s])
                ve.sem_inc(ple_out, 1)
            st.c += 2
            norm_x(UNITS["norm2"], 13, R_PG, 2, rw)
            m = UNITS["norm3"]
            ve.wait_ge(filled, m + 1)
            V.tensor_scalar(rstd[:, 1, :], ps[:, bank(m), 0:NT], 1.0 / D, EPS, ALU.mult, ALU.add).then_inc(freed[m % 4], 1)
            ve.wait_ge(freed[m % 4], m // 4 + 1)
            ve.sem_inc(var_ready, 1)
            ve.wait_ge(rstd_ready, 14)
            v.link(V.reciprocal(rstd[:, 1, :], rstd[:, 1, :]))
            for k in range(KD):
                v.mark(V.scalar_tensor_tensor(pl[:, k, :], pl[:, k, :], col(R_PLE + k), rstd[:, 1, :], ALU.mult, ALU.mult))
            v.wait()
            ve.sem_inc(ple_ready, 2)
            with ve.Fori(0, 4) as i:
                v.begin(i, 2)
                for n in range(2):
                    ve.wait_ge(sig_ready, i * 2 + (1 + n))
                    k = bass.ds(i * 4 + 2 * n, 2)
                    v.link(V.tensor_tensor(sig[:, n], sig[:, n], pl[:, k, :], ALU.mult))
                    V.tensor_tensor(xT[:, k, :], xT[:, k, :], sig[:, n], ALU.add).then_inc(ple_ready, 1)
            v.end(4)
            for n in range(12):
                m, j, q = UNITS["y"] + n, n // 4, n % 4
                w = rows(j)
                if n == 8:
                    ve.wait_ge(y_stored[0], 16)
                evac(m, yrow[0:w, j % 2, q * 512:(q + 1) * 512], ps[0:w, bank(m), :])
                ve.wait_ge(freed[m % 4], m // 4 + 1)
                ve.sem_inc(y_turned, 1)

        @block.tensor
        def _(pe):
            st, pr = Stream(), Pairs()
            T = nc.tensor

            def square_sum(m, base):
                fill_wait(pe, m)
                for q in range(4):
                    pe.wait_ge(squares, base + q + 1)
                    for k in range(4):
                        mm = T.matmul(ps[:, bank(m), 0:NT], ones, fo[:, (q % 2) * 1152 + k * NT:(q % 2) * 1152 + (k + 1) * NT],
                                      start=(q == k == 0), stop=(q == k == 3))
                    if q < 3:
                        mm.then_inc(squares_used, 1)
                mm.then_inc(filled, 1)
                pe.wait_ge(filled, m + 1)
                pe.sem_inc(squares_used, 1)

            pe.wait_ge(consts_in, 112)
            pe.wait_ge(conv_in, 16 * 12)
            for n, (src, t0, k) in enumerate(conv_at):
                m = UNITS["conv"] + n
                for t in range(k):
                    mm = T.transpose(ps[:, bank(m), t * 20:t * 20 + 20], src[0:20, t * P:(t + 1) * P], ident[0:20, 0:20])
                mm.then_inc(filled, 1)
            m = UNITS["small"]
            fill_wait(pe, m)
            pe.wait_ge(small_in, 160)
            pe.wait_ge(small_ready, 1)
            T.transpose(ps[:, bank(m), 0:R_ALL], small[:], ident[0:R_ALL, 0:R_ALL]).then_inc(filled, 1)
            pe.wait_ge(x_in, 48)
            for n in range(12):
                m, j, q = UNITS["x"] + n, n // 4, n % 4
                w = rows(j)
                fill_wait(pe, m)
                for k in range(4):
                    mm = T.transpose(ps[:, bank(m), k * w:(k + 1) * w], xn[0:w, j, (4 * q + k) * P:(4 * q + k + 1) * P],
                                     ident[0:w, 0:w])
                mm.then_inc(filled, 1)
            square_sum(UNITS["norm0"], 0)
            products(pe, st, pr, (h_hi, h_lo0), [C_U - C_IK], norm=0)
            for n in range(2):
                products(pe, st, pr, (h_hi, h_lo0), [P, P])
            for times in (2, 3):
                with pe.Fori(0, times) as i:
                    st.begin(i, 4)
                    pr.begin(i, 1)
                    for n in range(2):
                        products(pe, st, pr, (h_hi, h_lo0), [P, P])
                st.end(times)
                pr.end(times)
            for j in range(10):
                m = UNITS["qkn"] + j
                fill_wait(pe, m)
                pe.wait_ge(squares, 4 + j + 1)
                T.matmul(ps[:, bank(m), 0:NT], ones, oT[:, j % 4, :], start=True, stop=True).then_inc(filled, 1)
                pe.wait_ge(filled, m + 1)
                pe.sem_inc(squares_used, 1)
            for j in range(19):
                m = UNITS["ropeq"] + j
                fill_wait(pe, m)
                if j < 10:
                    pe.wait_ge(head_normed, j + 1)
                    mm = T.matmul(ps[:, bank(m), 0:NT], turn_q, qkvT[:, j, :], start=True, stop=True)
                elif j < 18:
                    pe.wait_ge(a_out, 4)
                    mm = T.matmul(ps[:, bank(m), 0:NT], turn_i, iqT[:, j - 10, :], start=True, stop=True)
                else:
                    mm = T.matmul(ps[0:IDIM, bank(m), 0:NT], turn_i[0:IDIM, 0:IDIM], ikT[0:IDIM, :], start=True, stop=True)
                mm.then_inc(filled, 1)
            for n in range(6):
                m, tt = UNITS["tok"] + n, n // 2
                w, t0 = rows(tt), tt * P
                fill_wait(pe, m)
                pe.wait_ge(roped, 19)
                if n % 2 == 0:
                    for k in range(4):
                        mm = T.transpose(ps[0:w, bank(m), k * P:(k + 1) * P], qkvT[:, 8 + k, t0:t0 + w], ident)
                else:
                    mm = T.transpose(ps[0:w, bank(m), 0:80], ikT[0:80, t0:t0 + w], ident[0:80, 0:80])
                mm.then_inc(filled, 1)
            m = UNITS["wb"]
            fill_wait(pe, m)
            T.matmul(ps[:, bank(m), 0:TS], headsel[:], ikT[0:80, TP:NT], start=True, stop=True).then_inc(filled, 1)
            for n in range(16):
                m, b, jh = UNITS["idx"] + n, n // 2, n % 2
                fill_wait(pe, m)
                if n % 8 == 0:
                    pe.wait_ge(idx_in[n // 8], 64)
                for k in range(4):
                    mm = T.transpose(ps[:, bank(m), k * P:(k + 1) * P], idx_raw[:, b % 4, 4 * jh + k, :], ident)
                mm.then_inc(filled, 1)
            for n in range(16):
                m, tt, i, par = UNITS["pidx"] + n, n // 8, n // 2 % 4, n % 2
                fill_wait(pe, m)
                r = slice(64 * par, 64 * par + 64)
                for k in range(2):
                    mm = T.matmul(ps[:, bank(m), k * 256:k * 256 + 256], iqT[r, 2 * i + k, tt * P:(tt + 1) * P],
                                  ik2[r, 0:TP], start=True, stop=True)
                mm.then_inc(filled, 1)
            pe.wait_ge(wb_ready, 1)
            for s in range(2):
                pe.wait_ge(out[s], pr.n[s])

            def weigh(n):
                blk, b = n // NB, n % NB
                w = 512 if blk < 2 else TQ
                pe.wait_ge(relu_ready, 16 + n + 1)
                T.matmul(ps[0:2 * TS, blk, 0:w], wheads[:, b, :], relu[:, n % 4, 0:w], start=(b == 0),
                         stop=(b == NB - 1)).then_inc(relu_weighed, 1)
                if b == NB - 1:
                    pe.wait_ge(relu_weighed, n + 1)
                    pe.sem_inc(blk_scored, 1)

            for n in range(24):
                m, blk, b = UNITS["sidx"] + n, n // NB, n % NB
                fill_wait(pe, m)
                w, keys = (512, idxT[:, b, blk * 512:(blk + 1) * 512]) if blk < 2 else (TQ, nk[:, b, :])
                T.matmul(ps[:, bank(m), 0:w], qb[:, b, :], keys, start=True, stop=True).then_inc(filled, 1)
                if n:
                    weigh(n - 1)
            weigh(23)
            pe.wait_ge(blk_out, 5)
            with pe.Fori(0, 8) as i:
                st.begin(i, 4)
                pr.begin(i, 1)
                for n in range(2):
                    products(pe, st, pr, (h_hi, h_lo0), [P, P])
            st.end(8)
            pr.end(8)

            pe.wait_ge(ssm_tabs, 1)
            for n in range(2):
                m = UNITS["bt"] + n
                fill_wait(pe, m)
                for k in range(4):
                    src = bbd[:, 2 * n + k // 2, k % 2].rearrange("p j g c -> p (j g c)")
                    mm = T.transpose(ps[:, bank(m), k * P:(k + 1) * P], src, ident)
                mm.then_inc(filled, 1)
            for n in range(2):
                m = UNITS["ct"] + n
                fill_wait(pe, m)
                for k in range(4):
                    src = craw[:, 2 * n + k // 2, k % 2].rearrange("p d n -> p (d n)")
                    mm = T.transpose(ps[:, bank(m), k * P:(k + 1) * P], src, ident)
                mm.then_inc(filled, 1)
            m = UNITS["ini"]
            for k in range(2):
                fill_wait(pe, m + k)
                T.transpose(ps[:, bank(m + k), 0:P], ini_raw[:, k], ident).then_inc(filled, 1)
            for s in range(2):
                pe.wait_ge(out[s], pr.n[s])
            pe.wait_ge(ssm_tabs, 2)

            def c_states(j, src, t0, n):
                q, g = j // 4, 32 * (j % 4)
                for r in range(2):
                    mm = T.matmul(ps[g:g + 32, q, t0:t0 + n], cl[:, j, r, :], src(r), start=(r == 0), stop=(r == 1))
                mm.then_inc(state_used, 1)

            U = UNITS["step"]

            def scores(i, m):
                h, t = i // 2, i % 2
                fill_wait(pe, m)
                T.matmul(ps[:, bank(m), 0:P * (t + 1)], qkvT[:, h, t * P:(t + 1) * P], qkvT[:, 8 + h // GRP, 0:P * (t + 1)],
                         start=True, stop=True).then_inc(filled, 1)

            def idle_unit(m):
                fill_wait(pe, m)
                pe.wait_ge(filled, m)
                pe.sem_inc(filled, 1)
                pe.sem_inc(freed[m % 4], 1)

            pe.wait_ge(pb_ready, 2)
            scores(0, UNITS["first"])
            idle_unit(UNITS["first"] + 1)
            for i in range(16):
                m = U + 6 * i
                q, g = i // 4, slice(32 * (i % 4), 32 * (i % 4) + 32)
                for r in range(2):
                    fill_wait(pe, m + r)
                    T.matmul(ps[:, bank(m + r), 0:NT], bl[g, q, r, :], uT[g, q, :], start=True, stop=True).then_inc(filled, 1)
                if i < 15:
                    scores(i + 1, m + 2)
                else:
                    idle_unit(m + 2)
                if i:
                    pe.wait_ge(state_ready, i)
                    c_states(i - 1, lambda r: states[(i - 1) % 2][:, r, :], 0, TP)
                h, t = i // 2, i % 2
                fill_wait(pe, m + 3)
                pe.wait_ge(p_norm, i + 1)
                for k in range(t + 1):
                    mm = T.transpose(ps[:, bank(m + 3), k * P:(k + 1) * P], psc[i % 2][:, k * P:(k + 1) * P], ident)
                mm.then_inc(filled, 1)
                fill_wait(pe, m + 4)
                pe.wait_ge(p_turned, i + 1)
                g0 = 256 + h // GRP * HD
                for k in range(t + 1):
                    mm = T.matmul(ps[:, bank(m + 4), 0:P], tok[:, k, g0:g0 + HD], ppt[i % 2][:, k, :], start=(k == 0), stop=(k == t))
                mm.then_inc(filled, 1)
                idle_unit(m + 5)
            pe.wait_ge(state_ready, 16)
            c_states(15, lambda r: states[1][:, r, :], 0, TP)
            pe.wait_ge(samples_ready, 1)
            for j in range(SPAIR):
                c_states(j, lambda r: sst[:, r, :, j, :], TP, TS)
            m = UNITS["fin"]
            fill_wait(pe, m)
            T.transpose(ps[0:32, bank(m), 0:P], ssmv[:, 20:22, :].rearrange("p r j -> p (r j)"), ident).then_inc(filled, 1)
            fill_wait(pe, m + 1)
            for r in range(2):
                src = sst[:, r].rearrange("p b j t -> p (b j) t")[:, :, TQ - 1]
                mm = T.transpose(ps[:, bank(m + 1), r * P:(r + 1) * P], src, ident)
            mm.then_inc(filled, 1)
            pe.wait_ge(z_ready, 4)
            for n in range(2):
                pe.wait_ge(out[pr.s], pr.before())
                pe.wait_ge(landed[st.slot()], st.landed())
                w = ring[:, st.slot(), 0:1024].rearrange("p (k n) -> p k n", k=4)
                for c in range(2):
                    for k in range(4):
                        mm = T.matmul(ps[:, 2 * pr.s + c, 0:NT], w[:, k, c * P:(c + 1) * P], uT[:, k, :], start=(k == 0),
                                      stop=(k == 3))
                mm.then_inc(used, 1)
                st.c += 1
                pr.step()
            st.whole += 2
            kk = Turns()

            def turn():
                k = kk.next()
                if k >= 2:
                    pe.wait_ge(k_freed[k % 2], k // 2)
                return k % 2

            pe.wait_ge(qz_ready, 1)
            for m in range(UNITS["norm1"] - 4, UNITS["norm1"]):
                pe.wait_ge(freed[m % 4], m // 4 + 1)
            for half in range(2):
                if half:
                    pe.wait_ge(s_exp, 2)
                for n in range(4):
                    T.matmul(ps[:, 4 + n, :], rowsb[:, half, :], selb[:, n * 512:n * 512 + 512], start=True, stop=False,
                             skip_group_check=True)
                if half:
                    pe.wait_ge(os_ready, 4)
                T.matmul(ps[:, 3, 0:TS], rowsb[:, half, :], selb[:, PAST:PAST + TS], start=True, stop=False,
                         skip_group_check=True)

                def score(u):
                    b, g, n = u // 8, u // 4 % 2, u % 4
                    last = u % 32 >= 28
                    s = (turn0 + u % 32) % 2
                    pe.wait_ge(k_freed[s], (turn0 + u % 32) // 2 + 1)
                    mm = T.matmul(ps[:, 4 + n, :], qz[:, b, g, :], kT[:, g, n * 512:n * 512 + 512], start=False,
                                  stop=last, skip_group_check=True)
                    if n == 3:
                        mm = T.matmul(ps[:, 3, 0:TS], qz[:, b, g, :], qkvT[:, 8 + g, TP:NT], start=False,
                                      stop=last, skip_group_check=True)
                    mm.then_inc(s_free, 1)

                turn0 = kk.k
                for u in range(32 * half, 32 * half + 32):
                    b, g, n = u // 8, u // 4 % 2, u % 4
                    if u % 8 == 0:
                        pe.wait_ge(k_in[b % 2], 16 * (b // 2 + 1))
                    s = turn()
                    for k in range(4):
                        mm = T.transpose(ps[:, s, k * P:(k + 1) * P], kraw[b % 2][:, n * 4 + k, g * P:(g + 1) * P], ident)
                    mm.then_inc(k_filled, 1)
                    if u % 32 >= 4:
                        score(u - 4)
                    if u % 8 == 7:
                        pe.wait_ge(k_filled, kk.k)
                        pe.sem_inc(k_used, 1)
                for u in range(32 * half + 28, 32 * half + 32):
                    score(u)
                pe.wait_ge(s_free, 32 * (half + 1))
                pe.sem_inc(s_scored, 1)
                pe.wait_ge(s_norm, half + 1)
                for n in range(5):
                    s = turn()
                    if n < 4:
                        for k in range(4):
                            j = 4 * n + k
                            mm = T.transpose(ps[:, s, k * P:(k + 1) * P], sp_[:, j * P:(j + 1) * P], ident)
                    else:
                        mm = T.transpose(ps[0:TS, s, 0:P], sp_[:, PAST:PAST + TS], ident)
                    mm.then_inc(k_filled, 1)
                for s in range(2):
                    pe.wait_ge(k_freed[s], (kk.k + 1 - s) // 2)

                def turn_rows(b):
                    s = turn()
                    pe.wait_ge(os_ready, b + 1)
                    for g in range(2):
                        mm = T.transpose(ps[:, s, g * 32:g * 32 + 32], os_[b % 2][:, g * P:(g + 1) * P], ident[0:TS, 0:TS])
                    mm.then_inc(k_filled, 1)

                for b in range(4 * half, 4 * half + 4):
                    c = slice(b % 4 * 32, b % 4 * 32 + 32)
                    pe.wait_ge(v_in[b % 2], 16 * (b // 2 + 1))
                    if b % 4 >= 2:
                        pe.wait_ge(os_ready, b - 1)
                    dst = ps[0:TS, 2 + b % 2, 0:256]
                    for j in range(SLOT):
                        T.matmul(dst, spT[:, j, c], vraw[b % 2][:, j, :], start=(j == 0), stop=False)
                    T.matmul(dst, spN[:, c], tok[0:TS, 2, 256:512], start=False, stop=True).then_inc(pv_done, 1)
                    if b % 4:
                        turn_rows(b - 1)
                turn_rows(4 * half + 3)
            pe.wait_ge(o_ready, 2)
            pe.wait_ge(o_split, 1)
            pe.wait_ge(z_split, 1)
            for n in range(8):
                s = n % 2
                if n >= 2:
                    pe.wait_ge(merged, n - 1)
                for kt, rhs, b0 in ((8, (o_hi, o_lo), 4 * s), (4, (z_hi, z_lo), 4 * s + 2)):
                    chunk(pe, st, [(b0, P), (b0 + 1, P)], rhs, 0, kt, True, True)
            pe.wait_ge(merged, 8)
            with pe.Fori(0, 4) as i:
                st.begin(i, 4)
                pr.begin(i, 1)
                for n in range(2):
                    products(pe, st, pr, (m_hi, m_lo), [P, P])
            st.end(4)
            pr.end(4)
            square_sum(UNITS["norm1"], 14)

            def up(t, g, j):
                if pr.off is not None or pr.n[pr.s] > 0:
                    pe.wait_ge(out[pr.s], pr.before())
                for half in range(2):
                    chunk(pe, st, [(2 * pr.s + half, P)], (h_hi, h_lo), 0, KD, True, True,
                          1 if pr.off is None and g == j == half == 0 else None)
                pr.step()

            def down(t, g, k):
                pe.wait_ge(act_ready, t + k)
                for n in range(8):
                    products(pe, st, pr, (acts_hi[:, g], acts_lo[:, g]), [P, P], 1, k)

            ffn(pe, st, pr, up, down)
            for n in range(22):
                m = UNITS["cout"] + n
                fill_wait(pe, m)
                for k in range(min(4, 2 * FT - 4 * n)):
                    f = 4 * n + k
                    mm = T.transpose(ps[0:18, bank(m), k * P:(k + 1) * P], cout[:, f // FT, f % FT, :], ident)
                mm.then_inc(filled, 1)
            pe.wait_ge(p_in, 48)
            for n in range(2):
                m = UNITS["pt"] + n
                fill_wait(pe, m)
                for j in range(3):
                    w = rows(j)
                    mm = T.transpose(ps[:, bank(m), j * P:j * P + w], pn[0:w, j, n * P:(n + 1) * P], ident[0:w, 0:w])
                mm.then_inc(filled, 1)
            pe.wait_ge(ple_ready_p, 2)
            for n in range(8):
                pe.wait_ge(out[pr.s], pr.before())
                pe.wait_ge(landed[st.slot()], st.landed())
                w = ring[:, st.slot(), :].rearrange("p (k n) -> p k n", k=2)
                for c in range(2):
                    c0 = (n % 4 * 2 + c) * P
                    for k in range(2):
                        mm = T.matmul(ps[:, 2 * pr.s + c, 0:NT], w[:, k, c0:c0 + P], pT[:, k, :], start=(k == 0), stop=(k == 1))
                mm.then_inc(ple_filled, 1)
                pr.step()
                if n % 4 == 3:
                    pe.wait_ge(ple_filled, n + 1)
                    pe.sem_inc(used, 1)
                    st.c += 1
            st.whole += 2
            square_sum(UNITS["norm2"], 18)
            square_sum(UNITS["norm3"], 22)
            for n in range(2):
                products(pe, st, pr, (h_hi, h_lo), [P, P], norm=(None if n else 2))
            with pe.Fori(0, 3) as i:
                st.begin(i, 4)
                pr.begin(i, 1)
                for n in range(2):
                    products(pe, st, pr, (h_hi, h_lo), [P, P])
            st.end(3)
            pr.end(3)
            pe.wait_ge(ple_ready, 10)
            for n in range(12):
                m, j, q = UNITS["y"] + n, n // 4, n % 4
                w = rows(j)
                fill_wait(pe, m)
                for k in range(4):
                    mm = T.transpose(ps[0:w, bank(m), k * P:(k + 1) * P], xT[:, 4 * q + k, j * P:j * P + w], ident)
                mm.then_inc(filled, 1)


INPUTS = ["x_prompt", "x_sample", "cache_k", "cache_v", "cache_idx_k", "state_ssm_re", "state_ssm_im", "state_conv",
          "page_table", "p_prompt", "p_sample", "g_mix", "w_in", "g_q", "g_k", "ssm_a_re", "ssm_a_im", "ssm_log_dt",
          "ssm_b_re", "ssm_b_im", "ssm_c_re", "ssm_c_im", "ssm_d", "w_glu", "w_att_br", "w_ssm_br", "w_o", "g_ffn",
          "w_up", "conv_w", "conv_b", "w_down", "w_ple", "g_ple", "g_pg", "w_pg"]
OUTPUTS = [("y_prompt", (TP, D), (1, TP, D)), ("y_sample", (TS, D), (NB, TQ, D)),
           ("k_prompt", (TP, 256), (1, 1, TP, KVH, HD)), ("v_prompt", (TP, 256), (1, 1, TP, KVH, HD)),
           ("idx_k_prompt", (TP, IDIM), (1, 1, TP, IDIM)),
           ("ssm_re_prompt", (SPAIR, P), (1, 1, G_SSM, N_SSM)), ("ssm_im_prompt", (SPAIR, P), (1, 1, G_SSM, N_SSM)),
           ("conv_prompt", (2, 2 * FF), (1, 1, 2, 2 * FF)),
           ("k_sample", (TS, 256), (1, NB, TQ, KVH, HD)), ("v_sample", (TS, 256), (1, NB, TQ, KVH, HD)),
           ("idx_k_sample", (TS, IDIM), (1, NB, TQ, IDIM)),
           ("ssm_re_sample", (P, P), (1, NB, G_SSM, N_SSM)), ("ssm_im_sample", (P, P), (1, NB, G_SSM, N_SSM)),
           ("conv_sample", (2 * NB, 2 * FF), (1, NB, 2, 2 * FF))]


def kernel(**inputs):
    import concourse.bacc as bacc
    from concourse.bass_utils import run_bass_kernel_spmd

    nc = bacc.Bacc("TRN2", target_bir_lowering=False, num_devices=1)
    arrays, a, o = {}, {}, {}
    for name, x in [(n, np.ascontiguousarray(inputs[n])) for n in INPUTS] + sorted(constants().items()):
        arrays[f"in_{name}"] = x
        a[name] = nc.dram_tensor(f"in_{name}", x.shape, mybir.dt.from_np(x.dtype), kind="ExternalInput").ap()
    for name, shape, _ in OUTPUTS:
        o[name] = nc.dram_tensor(f"out_{name}", shape, F32, kind="ExternalOutput").ap()
    build(nc, a, o)
    r = run_bass_kernel_spmd(nc, [arrays], core_ids=[0])
    return tuple(r.results[0][f"out_{name}"].reshape(shape) for name, _, shape in OUTPUTS)
```

```python
from contextlib import ExitStack

import numpy as np
import concourse.bass as bass
from concourse import mybir
from concourse.alu_op_type import AluOpType as ALU

ACT = mybir.ActivationFunctionType
F32 = mybir.dt.float32
F32R = mybir.dt.float32r
BF16 = mybir.dt.bfloat16
I32 = mybir.dt.int32
AX = mybir.AxisListType.X

P = 128
D = 2048
TP = 256
NB, TQ = 8, 4
TS = NB * TQ
NT = TP + TS
PAST = 2048
PAGE = 128
NPAGE = PAST // PAGE
KD = D // P
HEADS, KVH, HD = 8, 2, 128
GRP = HEADS // KVH
IH, IDIM = 16, 64
TOPK_P = min(256, TP // 4)
TOPK_S = min(256, (PAST + TQ) // 4)
G_SSM, C_SSM, N_SSM = 32, 16, 64
W_SSM = G_SSM * C_SSM
T16 = int(TP ** 0.5)
SPAIR = G_SSM // 2
FF = 5504
FT = FF // P
FG = 8
PLE = 256
EPS = 1e-6
SLOT = PAST // P
MASKED = -1.0e38
TAKEN = -3.0e38
OFF = -1.0e30
MAGIC = 12582912.0
C_Q, C_K, C_V, C_IQ, C_IK, C_U, C_GA = 0, 1024, 1280, 1536, 2560, 2640, 3152
EXT_S = 2 + TP
EXT = EXT_S + NB * (TQ + 2)
CONVN = EXT - 2
R_MIX, R_FFN, R_PG, R_PLE, R_DT, R_ARE, R_AIM, R_GQ, R_GK, R_D = 0, 16, 32, 48, 64, 80, 96, 112, 113, 114
R_ALL = R_D + W_SSM // P


TURN = 2 * np.pi
TURN_HI = 6.28125
TURN_LO = float(TURN - 6.28125)
UP_STEPS = 2 + 2 + 4 + 3 + 3
COARSE = 6144.0
HALF = 0.4999999


def constants():
    f = np.float32
    pos = np.concatenate([np.arange(TP), np.tile(PAST + np.arange(TQ), NB)]).astype(f)

    def rope(width, rot, heads):
        half = rot // 2
        inv = (f(500000.0) ** (-np.arange(half, dtype=f) / f(half))).astype(f)
        ang = (pos[:, None] * inv[None, :]).astype(f).astype(np.float64)
        cos, sin = np.ones((width, NT)), np.zeros((width, NT))
        cos[:half] = cos[half:rot] = np.cos(ang).T
        sin[:half] = sin[half:rot] = np.sin(ang).T
        turn = np.zeros((width, width))
        for i in range(half):
            turn[half + i, i] = -1.0
            turn[i, half + i] = 1.0
        big = np.kron(np.eye(heads), turn)
        return [np.tile(x, (heads, 1)).astype(f) for x in (cos, sin)] + [big.astype(f)]

    cq, sq, pq = rope(HD, HD // 4, 1)
    ci, si, pi = rope(IDIM, IDIM // 4, 2)
    c = {}
    c["c_mats"] = np.stack([np.eye(P), pq, pi, np.ones((P, P))], 1).astype(f)
    c["c_rope"] = np.stack([cq, sq, ci, si], 1)
    t = np.arange(P)
    cm = np.zeros((P, 2, TP), f)
    for a in range(2):
        cm[:, a] = np.where(np.arange(TP)[None] <= (a * P + t)[:, None], 0, MASKED)
    c["c_causal"] = cm
    cs = np.zeros((TS, TQ), f)
    off = np.zeros((TS, NB, TQ), f)
    for b in range(NB):
        for q in range(TQ):
            cs[b * TQ + q, q + 1:] = MASKED
            off[b * TQ + q, [x for x in range(NB) if x != b]] = OFF
            off[b * TQ + q, b, q + 1:] = OFF
    c["c_new"] = np.concatenate([cs, off.reshape(TS, NB * TQ)], 1)
    e = np.zeros((TS, 2, P), f)
    for b in range(NB):
        for x in range(8):
            for q in range(TQ):
                e[b * TQ + q, b // 4, (b % 4) * 32 + x * TQ + q] = 1
    c["c_rows"] = e
    hs = np.zeros((80, P), f)
    wm = np.zeros((P, NB, 2, TS), f)
    for j2 in range(2):
        for h in range(IH):
            for q in range(TQ):
                row = j2 * 64 + h * TQ + q
                hs[64 + h, row] = 1
                for b in range(NB):
                    wm[row, b, j2, b * TQ + q] = (IH ** -0.5) * (IDIM ** -0.5)
    c["c_heads"] = hs
    c["c_wmask"] = wm.reshape(P, 2 * NB, TS)
    times = np.tile(np.concatenate([np.arange(T16) * T16, np.arange(T16) + 1]), (P, 1))
    c["c_cols"] = np.concatenate([(np.arange(P) % 8)[:, None], np.full((P, 1), EPS), times], 1).astype(f)
    return c


class Steps:

    def __init__(self, eng, sem):
        self.eng, self.sem, self.n, self.off = eng, sem, 0, None

    def mark(self, ins):
        ins.then_inc(self.sem, 1)
        self.n += 1
        return self.n

    def wait(self):
        self.eng.wait_ge(self.sem, self.n if self.off is None else self.off + self.n)

    def upto(self, n):
        assert self.off is None
        self.eng.wait_ge(self.sem, n)

    def link(self, ins):
        self.mark(ins)
        self.wait()

    def begin(self, i, per):
        self.base, self.per = self.n, per
        self.off = i * per

    def end(self, times):
        assert self.n - self.base == self.per, (self.n - self.base, self.per)
        self.off = None
        self.n = self.base + self.per * times


class Stream:
    SLOTS = 4

    def __init__(self):
        self.c, self.off = 0, None
        self.whole = 0

    def split(self, j=0):
        return self.count(j) - self.whole

    def slot(self, j=0):
        return (self.c + j) % self.SLOTS

    def landed(self, j=0):
        v = 16 * ((self.c + j) // self.SLOTS + 1)
        return v if self.off is None else self.off * (16 // self.SLOTS) + v

    def count(self, j=0):
        v = self.c + j + 1
        return v if self.off is None else self.off + v

    def begin(self, i, per):
        assert per % self.SLOTS == 0
        self.base, self.per, self.off = self.c, per, i * per

    def end(self, times):
        assert self.c - self.base == self.per
        self.off = None
        self.c = self.base + self.per * times


UNITS = {}
_n = 0
for _name, _k in (("small", 1), ("x", 12), ("norm0", 1), ("conv", 4), ("qkn", 10), ("ropeq", 10),
                  ("ropei", 9), ("tok", 6), ("wb", 1), ("idx", 8), ("pidx", 16), ("idx2", 8), ("sidx", 24),
                  ("bt", 2), ("ct", 2), ("ini", 2), ("first", 2), ("step", 96), ("fin", 2),
                  ("norm1", 1), ("cout", 22), ("pt", 2), ("norm2", 1), ("norm3", 1), ("y", 12)):
    UNITS[_name] = _n
    _n += _k
U_ALL = _n


def bank(m):
    return 4 + m % 4


class Turns:

    def __init__(self):
        self.k = 0

    def next(self):
        self.k += 1
        return self.k - 1


class Pairs:

    def __init__(self):
        self.s, self.n, self.off = 0, [0, 0], None

    def before(self):
        v = self.n[self.s]
        return v if self.off is None else self.off + v

    def step(self):
        self.n[self.s] += 1
        self.s ^= 1

    def begin(self, i, per):
        self.base, self.per, self.off, self.s0 = list(self.n), per, i * per, self.s

    def end(self, times):
        assert self.s == self.s0 and all(x - y == self.per for x, y in zip(self.n, self.base))
        self.off, self.n = None, [x + self.per * times for x in self.base]


def build(nc, a, o):
    ctx = ExitStack()
    with ctx:
        def sb(name, shape, dt=F32):
            return ctx.enter_context(nc.sbuf_tensor(name, shape, dt))

        def sem(name):
            return ctx.enter_context(nc.semaphore(name))

        def both(name, n):
            with nc.sbuf_tensor(name, [P, n], F32) as plain:
                pass
            return plain, sb(name + "_r", [P, n], F32R)

        def area(x, lo, shape):
            n = int(np.prod(shape))
            names = "abcd"[:len(shape)]
            return x[:, lo:lo + n].rearrange(f"p ({' '.join(names)}) -> p {' '.join(names)}",
                                             **dict(zip(names, shape)))

        fx, rx = both("x", KD * NT)
        fh, rh = both("h", KD * NT)
        fg, rg = both("g", 2 * KD * NT)
        fq, rq = both("q", 20 * NT)
        fw, rw = both("w", 2 * 2052 + 4 * NT)
        fr, rr = both("ring", Stream.SLOTS * 2048)
        fk, rk = both("highs", 2 * 2048)
        highs = area(rk, 0, (2, 2048))
        xT = area(fx, 0, (KD, NT))
        gates = area(fg, 0, (2 * KD, NT))
        qkvT = area(fq, 0, (12, NT))
        iqT = area(fq, 12 * NT, (8, NT))
        work = area(fw, 0, (2, 2052))
        uT = area(fw, 2 * 2052, (4, NT))
        ring = area(fr, 0, (Stream.SLOTS, 2048))
        lows = area(rr, 0, (Stream.SLOTS, 2048))
        h_hi = area(rh, 0, (KD, NT))
        h_lo0 = area(rx, 0, (KD, NT))
        h_lo = area(rw, 0, (KD, NT))
        ssmv = area(fx, 8 * NT, (28, SPAIR))
        norm_tmp = area(fq, 0, (2, 4 * NT))
        o_hi, o_lo = area(rh, 0, (HEADS, NT)), area(rh, HEADS * NT, (HEADS, NT))
        z_hi, z_lo = area(rx, 8 * NT, (4, NT)), area(rx, 12 * NT, (4, NT))
        m_lo, m_hi = area(rg, 0, (KD, NT)), area(rg, KD * NT, (KD, NT))
        acts_hi, acts_lo = area(rg, 3140, (2, FG, NT)), area(rq, 0, (2, FG, NT))
        x_saved = nc.dram_tensor("x_saved", (P, KD * NT), F32).ap()
        oT = sb("oT", [P, HEADS, NT])
        ikT = sb("ikT", [P, NT])
        ik2 = sb("ik2", [P, NT])
        mats = sb("mats", [P, 4, P])
        causal = sb("causal", [P, 2, TP])
        cnew = sb("cnew", [TS, TQ + TS])
        rowsf = sb("rowsf", [TS, 2, P])
        rowsb = sb("rowsb", [TS, 2, P], BF16)
        headsel = sb("headsel", [80, P])
        wmask = sb("wmask", [P, 2 * NB, TS])
        small = sb("small", [R_ALL, P])
        cols = sb("cols", [P, R_ALL])
        convT = sb("convT", [P, 2 * FT, 20])
        tok = sb("tok", [P, 3, 512 + 80])
        sc = sb("sc", [P, 80])
        rstd = sb("rstd", [P, 2, NT])
        pidx = sb("pidx", [P, NB], I32)
        pidf = sb("pidf", [P, NB])
        pscore = sb("pscore", [P, 2, 2, TP])
        selb = sb("selb", [TS, PAST + TS], BF16)

        ident, turn_q, turn_i, ones = (mats[:, k, :] for k in range(4))
        ropes = area(fg, 0, (4, NT))
        cout = tok[:].rearrange("p a b -> p (a b)")[:, 0:36 * FT].rearrange("p (s f r) -> p s f r", s=2, f=FT)
        ps = ctx.enter_context(nc.psum_tensor("ps", [P, 8, 512], F32))

        landed = [sem(f"weights_landed{s}") for s in range(Stream.SLOTS)]
        used = sem("weights_used")
        out = [sem(f"products_out{s}") for s in range(2)]
        filled = sem("unit_filled")
        freed = [sem(f"unit_freed{s}") for s in range(4)]
        bus_out, rotated = sem("samples_input_taken"), sem("input_rotated")
        first_in = sem("first_constants_in")
        sined = sem("rotary_sine_part_ready")
        small_ready, trig_ready = sem("small_ready"), sem("trig_ready")
        consts_in, x_in, conv_in, small_in = sem("consts_in"), sem("x_in"), sem("conv_in"), sem("small_in")
        table_in, table_ready = sem("table_in"), sem("table_ready")
        idx_in = [sem(f"idx_keys_in{s}") for s in range(2)]
        x_ready = sem("x_transposed")
        squares, squares_used = sem("squares_ready"), sem("squares_used")
        rstd_ready = sem("root_ready")
        normed = sem("normed")
        a_out = sem("projections_out")
        head_normed, roped, tok_ready = sem("head_normed"), sem("roped"), sem("tok_ready")
        wb_ready = sem("indexer_weights_ready")
        relu_ready, relu_summed, relu_weighed = sem("relu_ready"), sem("relu_summed"), sem("relu_weighed")
        blk_scored, blk_out = sem("block_scored"), sem("block_out")
        pb_ready = sem("prompt_mask_ready")
        sb_ready = sem("sample_mask_ready")
        ssm_in, ssm_tabs = sem("ssm_in"), sem("ssm_tables_ready")
        trig_in, trig_out = sem("angles_ready"), sem("sines_ready")
        state_ready, state_used = sem("states_ready"), sem("states_used")
        y_ready, z_ready, glu_ready = sem("y_ready"), sem("z_ready"), sem("glu_ready")
        ssm_done, state_out = sem("ssm_done"), sem("state_rows_ready")
        p_max, p_exp, p_norm, p_turned = sem("p_max"), sem("p_exp"), sem("p_norm"), sem("p_turned")
        k_in, v_in = [sem(f"k_in{s}") for s in range(2)], [sem(f"v_in{s}") for s in range(2)]
        k_turned, s_scored, s_exp = sem("k_turned"), sem("s_scored"), sem("s_exp")
        s_max, s_norm, s_turned, s_pv = sem("s_max"), sem("s_norm"), sem("s_turned"), sem("s_pv")
        qz_ready, os_ready, o_ready = sem("qz_ready"), sem("os_ready"), sem("o_ready")
        k_used, v_used, s_free = sem("k_used"), sem("v_used"), sem("s_free")
        merged, x_step = sem("merged"), sem("residual_ready")
        ext_ready, conv_ready, gelu_ready = sem("ext_ready"), sem("conv_ready"), sem("gelu_ready")
        act_ready = sem("ffn_act_ready")
        p_in, ple_out, ple_ready, sig_ready = sem("p_in"), sem("ple_out"), sem("ple_ready"), sem("sig_ready")
        y_rows, c_rows = sem("y_rows"), sem("conv_rows")
        vec, sca = sem("vector_steps"), sem("scalar_steps")
        stored, state_stored = sem("stored"), sem("state_rows_stored")
        samples_ready = sem("sample_states_ready")
        ple_ready_p, ple_filled = sem("p_transposed"), sem("ple_filled")
        params_in = sem("ssm_params_for_scalar")
        params, pool_steps = sem("ssm_params"), sem("pool_steps")
        act_params = sem("scalar_ssm_params")
        k_filled, k_freed = sem("turn_filled"), [sem("turn_freed_scalar"), sem("turn_freed_vector")]
        pv_done, pv_out = sem("pv_done"), sem("pv_out")
        c_stored, y_stored = [sem(f"conv_rows_stored{s}") for s in range(6)], [sem(f"y_stored{s}") for s in range(2)]
        c_turned = [sem(f"conv_rows_turned{s}") for s in range(2)]
        y_turned = [sem(f"y_turned{s}") for s in range(2)]
        prompt_o = sem("prompt_attended")

        def fill_wait(pe, m):
            if m >= 4:
                pe.wait_ge(freed[m % 4], m // 4)

        def col(r):
            return cols[:, r:r + 1]

        def rows(tt):
            return P if tt < 2 else TS

        conv_at = [[(fg[:, 6144:9216], 0, 24)], [(fw[:, 0:2560], 24, 20)], [(fw[:, 2560:5248], 44, 21)],
                   [(tok[:].rearrange("p a b -> p (a b)")[:, 0:1664], 65, 13),
                    (pscore[:].rearrange("p a b t -> p (a b t)"), 78, 8)]]
        xn = fg[:, 0:6144].rearrange("p (j n) -> p j n", j=3)
        fo = oT[:].rearrange("p k t -> p (k t)")
        fi = fq[:, 12 * NT:20 * NT]
        idx_raw = fw[:, 0:4096].rearrange("p (b j n) -> p b j n", b=4, j=8)
        idxT = fg[:, 0:8192].rearrange("p (b n) -> p b n", b=NB)
        qb = fg[:, 8192:9216].rearrange("p (b n) -> p b n", b=NB)
        relu = fo[:, 0:2048].rearrange("p (r n) -> p r n", r=4)
        wheads = wmask[:].rearrange("p (b q) t -> p b (q t)", b=NB)
        nk = sc[:, 0:32].rearrange("p (b t) -> p b t", b=NB)
        m8 = sc[:, 32:40]
        dt_raw = sc[R_DT:R_DT + SPAIR, 0:2]
        by_cosine, by_sine = area(fg, 4 * NT, (19, NT)), area(fg, 23 * NT, (8, NT))
        bl = fi[:, 0:1024].rearrange("p (q r n) -> p q r n", q=4, r=2)
        cl = fi[:, 1024:2048].rearrange("p (j r c) -> p j r c", j=SPAIR, r=2)
        ini_raw = fi[:, 2048:2304].rearrange("p (r n) -> p r n", r=2)
        bus = area(fx, 2752, (2, NB, SPAIR, TQ))
        sst = area(fw, 512, (2, NB, SPAIR, TQ))
        ini = area(fw, 2048, (2, NB, SPAIR))
        braw = fw[:, 0:512].rearrange("p (r j c) -> p r j c", r=2, j=SPAIR)
        bbd = fw[:, 512:1536].rearrange("p (q r j g c) -> p q r j g c", q=4, r=2, j=4, g=2)
        craw = fw[:, 1536:2560].rearrange("p (q r d n) -> p q r d n", q=4, r=2, d=2)
        btmp = fw[:, 2560:3584].rearrange("p (k j c) -> p k j c", k=4, j=SPAIR)
        ssm0 = area(fo, 0, (28, SPAIR))
        angle = area(fo, 448, (2, SPAIR, 2 * T16))
        tables = area(fx, 0, (3, SPAIR, 2 * T16))
        turns = area(fo, 1472, (SPAIR, 2 * T16))
        trig = [area(fh, 1024 + k * 512, (2, TP)) for k in range(2)]
        part = area(fh, 0, (2, TP))
        eps, time = sc[:, 45:46], sc[:, 46:46 + 2 * T16]
        rot = [area(fh, 2304 + k * 512, (2, TP)) for k in range(2)]
        turned = area(fw, 0, (2, TP))
        states = [fh[:, 3584 + k * 512:4096 + k * 512].rearrange("p (r t) -> p r t", r=2) for k in range(2)]
        yt = fh[:, 0:1152].rearrange("p (k t) -> p k t", k=4)
        sg = fh[:, 1152:2304].rearrange("p (k t) -> p k t", k=4)
        rows_out = fw[:, 3712:4096].rearrange("p (r n) -> p r n", r=3)
        psc = [fw[:, 2560 + k * 256:2816 + k * 256] for k in range(2)]
        ppt = [fw[:, 3072 + k * 256:3328 + k * 256].rearrange("p (k t) -> p k t", k=2) for k in range(2)]
        kraw = [x[:, 0:4096].rearrange("p (j n) -> p j n", j=SLOT) for x in (fk, fh)]
        vraw = [fr[:, k * 4096:(k + 1) * 4096].rearrange("p (j n) -> p j n", j=SLOT) for k in range(2)]
        kT = fr[:, 4096:8192].rearrange("p (g n) -> p g n", g=2)
        qz = fi[:, 0:2048].rearrange("p (b g n) -> p b g n", b=NB, g=2)
        sp_ = fw[:, 0:PAST + TS]
        os_ = [fw[0:TS, 2080 + k * 256:2336 + k * 256] for k in range(2)]
        spT = fq[:, 0:2048].rearrange("p (j n) -> p j n", j=SLOT)
        spN = fq[0:TS, 2048:2176]
        ext = fg[:, 0:1224].rearrange("p (e s n) -> p e s n", e=2, s=2)
        cv = fg[:, 1224:2448].rearrange("p (e s n) -> p e s n", e=2, s=2)
        gl = fg[:, 2448:3060].rearrange("p (e n) -> p e n", e=2)
        taps = fg[:, 3060:3140].rearrange("p (e s n) -> p e s n", e=2, s=2)
        act_tmp = fg[:, 7748:8324].rearrange("p (e t) -> p e t", e=2)
        hi_ready, lo_ready = sem("high_parts_ready"), sem("low_parts_ready")
        h_tmp, h_high = sem("h_ready_to_split"), sem("h_high_ready")
        x_stored, x_back, ropes_in = sem("x_stored"), [sem("x_back0"), sem("x_back1")], sem("ropes_in")
        o_high, o_split, z_high, z_split = sem("o_high"), sem("o_split"), sem("z_high"), sem("z_split")
        m_sum, m_high, a_high, a_sum = sem("merged_sum"), sem("merged_high"), sem("act_high"), sem("act_product")
        pn = fw[:, 0:768].rearrange("p (j n) -> p j n", j=3)
        pT = fw[:, KD * NT:KD * NT + 2 * NT].rearrange("p (k t) -> p k t", k=2)
        pl = fg[:, 0:4608].rearrange("p (k t) -> p k t", k=KD)
        sig = fg[:, 4608:5760].rearrange("p (e k t) -> p e k t", e=2, k=2)
        crow = [x[:, lo + 1024 * k:lo + 1024 * (k + 1)] for x, lo in ((fg, 5760), (fq, 8 * NT)) for k in range(3)]
        yrow = fw[:, 0:4096].rearrange("p (e n) -> p e n", e=2)
        C_GLU = 2 + 4 + 8 + 12 + 32
        w_in = a["w_in"][0]
        KC = KD // 2

        def load(sp, st, src, n):
            k = src.shape[0] // P
            if st.off is not None or st.c >= st.SLOTS:
                sp.wait_ge(used, st.count() - st.SLOTS)
            sp.dma_start(ring[:, st.slot(), 0:k * n].rearrange("p (k n) -> p k n", n=n),
                         src.rearrange("(k p) n -> p k n", p=P)).then_inc(landed[st.slot()], 16)
            st.c += 1

        def load_pair(sp, st, w, c0, width=256):
            for kc in range(2):
                load(sp, st, w[kc * KC * P:(kc + 1) * KC * P, bass.ds(c0, width)], width)

        def products(pe, st, pr, rhs, widths, chunks=2, kt=KC, norm=None):
            if pr.off is not None or pr.n[pr.s] > 0:
                pe.wait_ge(out[pr.s], pr.before())
            for kc in range(chunks):
                chunk(pe, st, [(2 * pr.s + n, width) for n, width in enumerate(widths)], rhs, kc * kt, kt,
                      kc == 0, kc == chunks - 1, norm)
            pr.step()

        def chunk(pe, st, cols_, rhs, k0, kt, first, last, norm=None):
            hi, lo = rhs
            total = sum(width for _, width in cols_)

            def tile(x, k, n, width):
                c = k * total + n * P
                return x[:, c:c + width]

            pe.wait_ge(hi_ready, st.split())
            for n, (b, width) in enumerate(cols_):
                for k in range(kt):
                    if norm is not None and n == 0 and (k0 + k) % 4 == 0:
                        pe.wait_ge(normed, 4 * norm + (k0 + k) // 4 + 1)
                    w = tile(highs[:, st.c % 2], k, n, width)
                    for x in (hi, lo):
                        nc.tensor.matmul(ps[0:width, b, 0:NT], w, x[:, k0 + k, :], start=(first and k == 0 and x is hi),
                                         stop=False, skip_group_check=True)
            pe.wait_ge(lo_ready, st.split())
            for n, (b, width) in enumerate(cols_):
                for k in range(kt):
                    mm = nc.tensor.matmul(ps[0:width, b, 0:NT], tile(lows[:, st.slot()], k, n, width), hi[:, k0 + k, :],
                                          start=False, stop=(last and k == kt - 1), skip_group_check=True)
            mm.then_inc(used, 1)
            st.c += 1

        def split_high(act, st, n=2048):
            act.wait_ge(landed[st.slot()], st.landed())
            if st.off is not None or st.c >= 2:
                act.wait_ge(used, st.count() - 2)
            nc.scalar.copy(highs[:, st.c % 2, 0:n], ring[:, st.slot(), 0:n]).then_inc(hi_ready, 1)
            st.c += 1

        def split_low(pool, st, n=2048):
            pool.wait_ge(hi_ready, st.split())
            nc.gpsimd.tensor_tensor(lows[:, st.slot(), 0:n], ring[:, st.slot(), 0:n], highs[:, st.c % 2, 0:n].bitcast(F32),
                                    ALU.subtract).then_inc(lo_ready, 1)
            st.c += 1

        def taken(eng, st, pr, chunks=2):
            s = pr.s
            eng.wait_ge(used, st.count(chunks - 1))
            st.c += chunks
            pr.step()
            return ps[:, 2 * s:2 * s + 2, 0:NT], out[s]

        def walk(st, pr, name):
            pairs, chunks = {"ikw": (1, 2), "u": (2, 2), "iq": (4, 2), "qkv": (6, 2), "gates": (16, 2),
                             "glu": (2, 1), "w_o": (8, 2)}[name]
            for _ in range(pairs):
                st.c += chunks
                pr.step()

        def conv_rows_out(eng, copy, n):
            m = UNITS["cout"] + n
            w = min(512, 2 * FF - n * 512)
            eng.wait_ge(filled, m + 1)
            if n >= 12:
                eng.wait_ge(c_stored[n // 2 % 6], 32 * (n // 2 // 6))
            copy(crow[n // 2 % 6][0:18, n % 2 * 512:n % 2 * 512 + w], ps[0:18, bank(m), 0:w]).then_inc(freed[m % 4], 1)
            eng.wait_ge(freed[m % 4], m // 4 + 1)
            eng.sem_inc(c_turned[n % 2], 1)

        def y_rows_out(eng, copy, n):
            m, j, q = UNITS["y"] + n, n // 4, n % 4
            w = rows(j)
            eng.wait_ge(filled, m + 1)
            if j == 2:
                eng.wait_ge(y_stored[0], 16)
            copy(yrow[0:w, j % 2, q * 512:(q + 1) * 512], ps[0:w, bank(m), :]).then_inc(freed[m % 4], 1)
            eng.wait_ge(freed[m % 4], m // 4 + 1)
            eng.sem_inc(y_turned[n % 2], 1)

        block = ctx.enter_context(nc.Block())

        def ffn(eng, st, pr, up, down, more=()):
            counted = ((st, 48),) + (((pr, 16),) if pr else ()) + tuple(more)
            for j in range(FG):
                up(j, 0, j)
            with eng.Fori(0, 2) as i:
                for x, per in counted:
                    x.begin(i, per)
                for gg in range(2):
                    for j in range(FG):
                        up(i * 16 + (FG * (1 + gg) + j), (1 + gg) % 2, j)
                    down(i * 16 + FG * gg, gg, FG)
            for x, _ in counted:
                x.end(2)
            for j in range(FT - 5 * FG):
                up(5 * FG + j, 1, j)
            down(4 * FG, 0, FG)
            down(5 * FG, 1, FT - 5 * FG)

        @block.sync
        def _(sp):
            st = Stream()
            for dst, src in ((mats[:], a["c_mats"]), (sc[:, 44:46 + 2 * T16], a["c_cols"])):
                sp.dma_start(dst, src).then_inc(first_in, 16)
            for j in range(2):
                sp.dma_start(xn[:, j, :], a["x_prompt"][0, j * P:(j + 1) * P, :]).then_inc(x_in, 16)
            sp.dma_start(xn[0:TS, 2, :], a["x_sample"].rearrange("b t d -> (b t) d")).then_inc(x_in, 16)
            for r, n, src in ((R_MIX, 16, "g_mix"), (R_FFN, 16, "g_ffn"), (R_PG, 16, "g_pg"), (R_PLE, 16, "g_ple"),
                              (R_GQ, 1, "g_q"), (R_GK, 1, "g_k"), (R_D, 4, "ssm_d")):
                sp.dma_start(small[r:r + n, :], a[src][0].rearrange("(k p) -> k p", p=P)).then_inc(small_in, 16)
            for r, src in ((R_ARE, "ssm_a_re"), (R_AIM, "ssm_a_im")):
                sp.dma_start(small[r:r + SPAIR, :], a[src][0].rearrange("(j g) n -> j (g n)", g=2)).then_inc(small_in, 16)
            sp.dma_start(dt_raw, a["ssm_log_dt"][0].rearrange("(j g) -> j g", g=2)).then_inc(small_in, 16)
            for kc in range(2):
                load(sp, st, w_in[kc * KC * P:(kc + 1) * KC * P, C_IK:C_U], C_U - C_IK)
            load_pair(sp, st, w_in, C_U)
            for unit in conv_at:
                for dst, t0, n in unit:
                    w = slice(t0 * P, (t0 + n) * P)
                    sp.dma_start(dst[0:16, 0:n * P], a["state_conv"][0].rearrange("b r n -> (b r) n")[:, w]).then_inc(conv_in, 16)
                    sp.dma_start(dst[16:19, 0:n * P], a["conv_w"][0][:, w]).then_inc(conv_in, 16)
                    sp.dma_start(dst[19:20, 0:n * P], a["conv_b"][:, w]).then_inc(conv_in, 16)
            for dst, src in ((causal[:], a["c_causal"]), (cnew[:], a["c_new"]), (rowsf[:], a["c_rows"]),
                             (headsel[:], a["c_heads"]), (wmask[:], a["c_wmask"])):
                sp.dma_start(dst, src).then_inc(consts_in, 16)
            sp.wait_ge(x_ready, 12)
            sp.dma_start(x_saved, fx[:]).then_inc(x_stored, 16)
            sp.dma_start(ropes, a["c_rope"]).then_inc(ropes_in, 16)
            load_pair(sp, st, w_in, C_U + 256)
            for c0, times in ((C_IQ, 2), (C_Q, 3), (C_GA, 8)):
                with sp.Fori(0, times) as i:
                    st.begin(i, 4)
                    for n in range(2):
                        load_pair(sp, st, w_in, i * 512 + (c0 + n * 256))
                st.end(times)
            sp.wait_ge(tok_ready, 6)
            for tt in range(3):
                n = rows(tt)
                g = "prompt" if tt < 2 else "sample"
                r0 = tt * P if tt < 2 else 0
                for name, lo, w in (("k", 0, 256), ("v", 256, 256), ("idx_k", 512, 64)):
                    sp.dma_start(o[f"{name}_{g}"][r0:r0 + n, :], tok[0:n, tt, lo:lo + w]).then_inc(stored, 16)
            sp.wait_ge(sb_ready, 1)
            for r, part in enumerate(("re", "im")):
                sp.dma_start(braw[:, r], a[f"ssm_b_{part}"][0].rearrange("(j g) n c -> (g n) j c", g=2)).then_inc(ssm_in, 16)
                for d in range(2):
                    sp.dma_start(craw[:, :, r, d, :], a[f"ssm_c_{part}"][0].rearrange("(q r) c n -> (r c) q n", r=8)).then_inc(ssm_in, 16)
                sp.dma_start(ini_raw[:, r], a[f"state_ssm_{part}"][0].rearrange("b (j g) n -> (b j) (g n)", g=2)).then_inc(ssm_in, 16)
            sp.wait_ge(used, C_GLU)
            for n in range(2):
                load(sp, st, a["w_glu"][0][:, n * 256:(n + 1) * 256], 256)
            sp.wait_ge(state_out, 2)
            for r, part in enumerate(("re", "im")):
                sp.dma_start(o[f"ssm_{part}_prompt"], rows_out[r * SPAIR:(r + 1) * SPAIR, 0, :]).then_inc(state_stored, 16)
                sp.dma_start(o[f"ssm_{part}_sample"], rows_out[:, 1 + r, :]).then_inc(state_stored, 16)
            def load_branches(c0):
                c = bass.ds(c0, 256)
                load(sp, st, a["w_att_br"][0][:, c], 256)
                load(sp, st, a["w_ssm_br"][0][:, c], 256)

            for n in range(2):
                sp.wait_ge(pv_done, 7 + n)
                load_branches(n * 256)
            with sp.Fori(0, 3) as i:
                st.begin(i, 4)
                for n in range(2):
                    load_branches(i * 512 + (512 + n * 256))
            st.end(3)
            with sp.Fori(0, 4) as i:
                st.begin(i, 4)
                for n in range(2):
                    load_pair(sp, st, a["w_o"][0], i * 512 + n * 256)
            st.end(4)

            def load_up(t):
                for half in range(2):
                    load(sp, st, a["w_up"][0][:, bass.ds(t * P + half * FF, P)], P)

            def load_down(t, k):
                for n in range(8):
                    load(sp, st, a["w_down"][0][bass.ds(t * P, k * P), n * 256:(n + 1) * 256], 256)

            ffn(sp, st, None, lambda t, g, j: load_up(t), lambda t, g, k: load_down(t, k))
            sp.wait_ge(act_ready, FT)
            for j in range(3):
                src = a["p_prompt"][0, 0, j * P:(j + 1) * P, :] if j < 2 else a["p_sample"][0].rearrange("b t n -> (b t) n")
                sp.dma_start(pn[0:rows(j), j, :], src).then_inc(p_in, 16)
            for n in range(2):
                load(sp, st, a["w_ple"][0][:, n * 1024:(n + 1) * 1024], 1024)
            with sp.Fori(0, 4) as i:
                st.begin(i, 4)
                for n in range(2):
                    load_pair(sp, st, a["w_pg"][0], i * 512 + n * 256)
            st.end(4)
            for j in range(3):
                for s in range(2):
                    sp.wait_ge(y_turned[s], 2 * (j + 1))
                dst = o["y_prompt"][j * P:(j + 1) * P, :] if j < 2 else o["y_sample"]
                sp.dma_start(dst, yrow[0:rows(j), j % 2, :]).then_inc(y_stored[j % 2], 16)
            sp.wait_ge(stored, 9 * 16)
            sp.wait_ge(state_stored, 4 * 16)
            for s in range(6):
                sp.wait_ge(c_stored[s], 32 * ((11 - s + 5) // 6))
            for s in range(2):
                sp.wait_ge(y_stored[s], 16 * (2 - s))

        @block.gpsimd
        def _(pool):
            st, pl_, G = Stream(), Steps(pool, pool_steps), nc.gpsimd
            for b in range(NB):
                pool.dma_start(pidx[:, b:b + 1], a["page_table"][b].unsqueeze(1).unsqueeze(1).to_broadcast([NPAGE, 8, 1])).then_inc(table_in, 16)
            pool.wait_ge(table_ready, 1)
            rows16 = a["cache_idx_k"][0].rearrange("n (r j) d -> (n r) (j d)", j=SLOT)
            pool.wait_ge(filled, UNITS["conv"] + 4)

            def gather_idx(b):
                nc.gpsimd.indirect_dma_start(fw[:, b % 4 * 1024:(b % 4 + 1) * 1024], None, rows16,
                                             bass.IndirectOffsetOnAxis(ap=pidx[:, b:b + 1], axis=0)
                                             ).then_inc(idx_in[b // 4], 16)

            for n in (640, 640) + 4 * (2048,):
                split_low(pool, st, n)
                if n == 2048:
                    gather_idx(st.c - 3)
            with pool.Fori(0, 5) as i:
                st.begin(i, 4)
                for _ in range(4):
                    split_low(pool, st)
            st.end(5)
            pool.wait_ge(ropes_in, 16)
            pool.wait_ge(a_out, 4)
            cos = ropes[:, 2, :].unsqueeze(1).to_broadcast([P, 8, NT])
            pl_.mark(G.tensor_tensor(by_cosine[:, 10:18, :], iqT, cos, ALU.mult))
            pl_.mark(G.tensor_tensor(by_cosine[0:IDIM, 18, :], ikT[0:IDIM, :], ropes[0:IDIM, 2, :], ALU.mult))
            for j in range(10):
                pool.wait_ge(head_normed, j + 1)
                pl_.mark(G.tensor_tensor(by_cosine[:, j, :], qkvT[:, j, :], ropes[:, 0, :], ALU.mult))
            pl_.wait()
            for j in range(19):
                n = P if j < 18 else IDIM
                x = qkvT[:, j, :] if j < 10 else iqT[:, j - 10, :] if j < 18 else ikT[0:IDIM, :]
                pool.wait_ge(sined, j + 1)
                G.tensor_tensor(x, by_cosine[0:n, j, :], by_sine[0:n, j % 8, :], ALU.add).then_inc(roped, 1)
            pool.wait_ge(filled, UNITS["idx"] + 8)
            for b in range(4, NB):
                gather_idx(b)

            def lows(n):
                for _ in range(n):
                    split_low(pool, st)

            lows(2)
            pool.wait_ge(params, 1)
            when = time.unsqueeze(1).to_broadcast([P, SPAIR, 2 * T16])
            fa, fb = (ssm0[:, k, :].unsqueeze(2).to_broadcast([P, SPAIR, 2 * T16]) for k in (8, 9))
            x, r = turns, angle[:, 1]
            pl_.link(G.tensor_tensor(x, when, fa, ALU.mult))
            lows(2)
            pl_.link(G.tensor_scalar(r, x, MAGIC, MAGIC, ALU.add, ALU.subtract))
            lows(2)
            pl_.link(G.tensor_tensor(x, x, r, ALU.subtract))
            lows(2)
            pl_.link(G.tensor_tensor(r, when, fb, ALU.mult))
            lows(2)
            pl_.link(G.tensor_tensor(x, x, r, ALU.add))
            for half in range(2):
                y = angle[:, half]
                if half:
                    lows(2)
                    pl_.link(G.tensor_scalar(x, x, 0.25, None, ALU.add))
                lows(2)
                pl_.link(G.tensor_scalar(r, x, MAGIC, MAGIC, ALU.add, ALU.subtract))
                lows(2)
                pl_.link(G.tensor_tensor(y, x, r, ALU.subtract))
                lows(2)
                pl_.link(G.tensor_scalar(y, y, HALF, -HALF, ALU.min, ALU.max))
            pool.sem_inc(trig_in, 1)
            lows(8)
            st.c += 2
            st.whole += 2
            pool.wait_ge(trig_out, 3)
            for j in range(SPAIR):
                if j >= 2:
                    pool.wait_ge(state_ready, j - 1)
                first = [tables[:, k:k + 2, j, 0:T16].unsqueeze(3).to_broadcast([P, 2, T16, T16]) for k in (1, 0)]
                second = [tables[:, k, j, T16:2 * T16].unsqueeze(1).unsqueeze(1).to_broadcast([P, 2, T16, T16]) for k in (1, 2)]
                out_, tmp = (y.rearrange("p k (a b) -> p k a b", a=T16) for y in (trig[j % 2], part))
                pl_.mark(G.tensor_tensor(out_, first[0], second[0], ALU.mult))
                pl_.link(G.tensor_tensor(tmp, first[1], second[1], ALU.mult))
                pl_.link(G.tensor_tensor(trig[j % 2], trig[j % 2], part, ALU.add))
                pool.sem_inc(trig_ready, 1)
            rows_k = a["cache_k"][0].rearrange("n (r j) g d -> (n r) (j g d)", j=SLOT)
            rows_v = a["cache_v"][0].rearrange("n (r j) g d -> (n r) (j g d)", j=SLOT)
            def gather_k(b):
                if b >= 2:
                    pool.wait_ge(k_used, b - 1)
                G.indirect_dma_start((fk, fh)[b % 2][:, 0:4096], None, rows_k,
                                     bass.IndirectOffsetOnAxis(ap=pidx[:, b:b + 1], axis=0)).then_inc(k_in[b % 2], 16)

            def gather_v(b):
                if b >= 2:
                    pool.wait_ge(pv_done, b - 1)
                if b % 4 == 1:
                    pool.wait_ge(s_scored, b // 4 + 1)
                G.indirect_dma_start(fr[:, b % 2 * 4096:(b % 2 + 1) * 4096], None, rows_v,
                                     bass.IndirectOffsetOnAxis(ap=pidx[:, b:b + 1], axis=0)).then_inc(v_in[b % 2], 16)

            gather_k(0)
            gather_v(0)
            pool.wait_ge(glu_ready, 1)
            for gather, b in ((gather_k, 1), (gather_k, 2), (gather_k, 3), (gather_v, 1), (gather_k, 4), (gather_k, 5),
                              (gather_v, 2), (gather_v, 3), (gather_v, 4), (gather_k, 6), (gather_k, 7), (gather_v, 5),
                              (gather_v, 6), (gather_v, 7)):
                gather(b)

            with pool.Fori(0, 4) as i:
                st.begin(i, 4)
                for n in (2048, 1024, 2048, 1024):
                    split_low(pool, st, n)
            st.end(4)
            with pool.Fori(0, 4 + 31) as i:
                st.begin(i, 4)
                for _ in range(4):
                    split_low(pool, st)
            st.end(4 + 31)
            for n in 2 * (2048,) + 8 * ((FT - 5 * FG) * 256,):
                split_low(pool, st, n)
            st.c += 2
            st.whole += 2
            with pool.Fori(0, 4) as i:
                st.begin(i, 4)
                for _ in range(4):
                    split_low(pool, st)
            st.end(4)

        @block.scalar
        def _(act):
            st, pr, ahead = Stream(), Pairs(), Stream()
            sq = fo.rearrange("p (s n) -> p s n", s=2)

            def square_x(base, quarters=range(4)):
                for q in quarters:
                    if q >= 2:
                        act.wait_ge(squares_used, base + q - 1)
                    nc.scalar.activation(sq[:, q % 2, :], xT[:, 4 * q:4 * q + 4, :].rearrange("p k t -> p (k t)"),
                                         ACT.Square).then_inc(squares, 1)

            def root(m, x, width):
                act.wait_ge(filled, m + 1)
                nc.scalar.activation(x, ps[:, bank(m), 0:NT], ACT.Sqrt, bias=eps, scale=1.0 / width).then_inc(freed[m % 4], 1)
                act.wait_ge(freed[m % 4], m // 4 + 1)
                act.sem_inc(rstd_ready, 1)

            act.wait_ge(first_in, 32)
            def h_highs(nth, groups=range(4)):
                for q in groups:
                    act.wait_ge(h_tmp, nth * 4 + q + 1)
                    nc.scalar.copy(rh[:, q * 4 * NT:(q + 1) * 4 * NT], norm_tmp[:, q % 2, :]).then_inc(h_high, 1)

            act.wait_ge(x_ready, 12)
            square_x(0)
            root(UNITS["norm0"], rstd[:, 0, :], D)
            h_highs(0)
            for n in (640, 640) + 4 * (2048,):
                split_high(act, ahead, n)
            with act.Fori(0, 5) as i:
                ahead.begin(i, 4)
                for _ in range(4):
                    split_high(act, ahead)
            ahead.end(5)
            for _ in range(2):
                split_high(act, ahead)
            for name in ("ikw", "u", "iq", "qkv"):
                walk(st, pr, name)
            act.wait_ge(a_out, 4)
            for j in range(12):
                if j < 10:
                    if j >= 4:
                        act.wait_ge(squares_used, 4 + j - 3)
                    nc.scalar.activation(oT[:, j % 4, :], qkvT[:, j, :], ACT.Square).then_inc(squares, 1)
                if j >= 2:
                    if j >= 6:
                        act.wait_ge(head_normed, j - 5)
                    root(UNITS["qkn"] + j - 2, oT[:, 4 + (j - 2) % 4, :], HD)
            def idx_keys(unit, b0):
                for n in range(8):
                    m = UNITS[unit] + n
                    act.wait_ge(filled, m + 1)
                    nc.scalar.copy(idxT[:, b0 + n // 2, n % 2 * 512:(n % 2 + 1) * 512], ps[:, bank(m), :]).then_inc(freed[m % 4], 1)

            idx_keys("idx", 0)
            act.wait_ge(squares_used, 14)
            for n in range(16 + 24):
                if n == 16:
                    idx_keys("idx2", 4)
                m = UNITS["pidx"] + n if n < 16 else UNITS["sidx"] + n - 16
                w = 512 if n < 32 else TQ
                act.wait_ge(filled, m + 1)
                if 4 <= n < 20:
                    act.wait_ge(relu_summed, n - 3)
                elif n >= 20:
                    act.wait_ge(relu_weighed, n - 19)
                nc.scalar.activation(relu[:, n % 4, 0:w], ps[:, bank(m), 0:w], ACT.Relu).then_inc(freed[m % 4], 1)
                act.wait_ge(freed[m % 4], m // 4 + 1)
                act.sem_inc(relu_ready, 1)
            act.wait_ge(relu_weighed, 24)
            nc.scalar.activation(ssm0[:, 0, :], cols[:, R_DT:R_DT + SPAIR], ACT.Exp).then_inc(act_params, 1)
            act.wait_ge(params_in, 1)
            nc.scalar.activation(ssm0[:, 3, :], ssm0[:, 1, :], ACT.Exp).then_inc(act_params, 1)
            act.wait_ge(params_in, 2)
            nc.scalar.activation(ssm0[:, 12:14, :], ssm0[:, 10:12, :], ACT.Sin, scale=TURN).then_inc(act_params, 1)
            def gate_pairs(i, last):
                for n in range(2):
                    if not (last and n):
                        for _ in range(2):
                            split_high(act, ahead)
                    src, free = taken(act, st, pr)
                    nc.scalar.activation(gates[:, bass.ds(i * 4 + 2 * n, 2), :], src, ACT.Sigmoid).then_inc(free, 1)

            with act.Fori(0, 7) as i:
                for x, per in ((ahead, 4), (st, 4), (pr, 1)):
                    x.begin(i, per)
                gate_pairs(i, False)
            for x in (ahead, st, pr):
                x.end(7)
            gate_pairs(7, True)
            assert ahead.c == st.c
            ahead.c += 2


            act.wait_ge(trig_in, 1)
            for k, (half, sign) in enumerate(((0, -1), (1, 1), (0, 1))):
                nc.scalar.activation(tables[:, k], angle[:, half], ACT.Sin, scale=sign * TURN).then_inc(trig_out, 1)
            U = UNITS["step"]
            scale = HD ** -0.5

            def keep(i):
                m = U + 6 * i + 4
                act.wait_ge(filled, m + 1)
                nc.scalar.copy(oT[:, i // 2, i % 2 * P:(i % 2 + 1) * P], ps[:, bank(m), 0:P]).then_inc(freed[m % 4], 1)

            for i in range(16):
                act.wait_ge(p_max, i + 1)
                w = P * (i % 2 + 1)
                nc.scalar.activation(psc[i % 2][:, 0:w], psc[i % 2][:, 0:w], ACT.Exp, bias=sc[:, 2 + i % 2:3 + i % 2], scale=scale,
                                     accum_out=sc[:, 4 + i % 2:5 + i % 2]).then_inc(p_exp, 1)
                if i:
                    keep(i - 1)
                m = U + 6 * i
                act.wait_ge(rotated, i + 1)
                nc.scalar.copy(bus[:, :, :, i, :], ps[:, bank(m):bank(m) + 2, TP:NT].rearrange("p r (b t) -> p r b t", b=NB)
                               ).then_inc(bus_out, 1)
                act.wait_ge(bus_out, i + 1)
                for x in (m, m + 1):
                    act.sem_inc(freed[x % 4], 1)
                m = U + 6 * i + 3
                act.wait_ge(filled, m + 1)
                if i >= 2:
                    act.wait_ge(filled, U + 6 * (i - 2) + 5)
                nc.scalar.copy(ppt[i % 2][:, 0:w // P, :], ps[:, bank(m), 0:w].rearrange("p (k t) -> p k t", t=P)).then_inc(freed[m % 4], 1)
                act.wait_ge(freed[m % 4], m // 4 + 1)
                act.sem_inc(p_turned, 1)
            keep(15)
            for q in range(4):
                act.wait_ge(y_ready, q + 1)
                nc.scalar.activation(uT[:, q, :], yt[:, q, :], ACT.Gelu_apprx_tanh).then_inc(z_ready, 1)
            for n in range(2):
                src, free = taken(act, st, pr, 1)
                nc.scalar.activation(sg[:, 2 * n:2 * n + 2, :], src, ACT.Sigmoid).then_inc(free, 1)
            act.wait_ge(glu_ready, 1)
            nc.scalar.copy(z_hi, uT).then_inc(z_high, 1)
            act.dma_start(fx[:, 0:8 * NT], x_saved[:, 0:8 * NT]).then_inc(x_back[0], 16)
            kk = Turns()

            def turn(dst, src):
                k = kk.next()
                if k % 2 == 0:
                    act.wait_ge(k_filled, k + 1)
                    nc.scalar.copy(dst, src(k % 2)).then_inc(k_freed[0], 1)

            for half in range(2):
                for b in range(4 * half, 4 * half + 4):
                    if b == 4:
                        act.wait_ge(pv_done, 4)
                    for n in range(8):
                        if b and kk.k % 2 == 0:
                            act.wait_ge(s_free, 8 * b + n - 7)
                        turn(kT[:, n // 4, n % 4 * 512:n % 4 * 512 + 512], lambda s: ps[:, s, :])
                act.wait_ge(s_max, half + 1)
                nc.scalar.activation(sp_[:, 0:PAST], ps[:, 4:8, :].rearrange("p k n -> p (k n)"), ACT.Exp, bias=sc[:, 11:12],
                                     scale=scale, accum_out=sc[:, 12:13]).then_inc(s_exp, 1)
                nc.scalar.activation(sp_[:, PAST:PAST + TS], ps[:, 3, 0:TS], ACT.Exp, bias=sc[:, 11:12],
                                     scale=scale, accum_out=sc[:, 13:14]).then_inc(s_exp, 1)
                for n in range(4):
                    turn(spT[:, 4 * n:4 * n + 4, :], lambda s: ps[:, s, :].rearrange("p (j n) -> p j n", j=4))
                turn(spN, lambda s: ps[0:TS, s, 0:P])
                for b in range(4 * half, 4 * half + 4):
                    t0 = TP + b * TQ
                    for g in range(2):
                        if g:
                            kk.k -= 1
                        k = kk.next()
                        if k % 2 == 0:
                            act.wait_ge(k_filled, k + 1)
                            ins = nc.scalar.copy(oT[:, g * 4:g * 4 + 4, t0:t0 + TQ],
                                                 ps[:, 0, g * 48:g * 48 + 16].rearrange("p (r t) -> p r t", t=TQ))
                            if g:
                                ins.then_inc(k_freed[0], 1)
            act.wait_ge(k_freed[0], (kk.k + 1) // 2)
            act.sem_inc(o_ready, 1)
            for n in (2048, 1024):
                split_high(act, ahead, n)
            act.wait_ge(o_ready, 2)
            nc.scalar.copy(rh[:, 0:HEADS * NT], fo).then_inc(o_high, 1)
            for n in range(8):
                for w in (2048, 1024) if n < 7 else (2048, 2048):
                    split_high(act, ahead, w)
                act.wait_ge(m_sum, n + 1)
                nc.scalar.copy(m_hi[:, 2 * n:2 * n + 2, :], gates[:, 2 * n:2 * n + 2, :]).then_inc(m_high, 1)
            act.wait_ge(merged, 8)
            act.dma_start(fx[:, 8 * NT:], x_saved[:, 8 * NT:]).then_inc(x_back[1], 16)
            with act.Fori(0, 4) as i:
                ahead.begin(i, 4)
                for _ in range(4):
                    split_high(act, ahead)
            ahead.end(4)
            st.c += 16
            walk(st, pr, "w_o")
            act.wait_ge(x_step, 1)
            square_x(14)
            root(UNITS["norm1"], rstd[:, 0, :], D)
            h_highs(1)

            def up(t, g, j):
                s, e = pr.s, pr.s
                for _ in range(2):
                    split_high(act, ahead)
                act.wait_ge(used, st.count(1))
                if pr.off is not None or j >= 2 or g:
                    act.wait_ge(conv_ready, t - 1)
                src = ps[:, 2 * s:2 * s + 2, :]
                nc.scalar.copy(ext[:, e, :, 2:2 + TP], src[:, :, 0:TP])
                nc.scalar.copy(ext[:, e, :, EXT_S:EXT].rearrange("p s (b t) -> p s b t", b=NB)[:, :, :, 2:2 + TQ],
                               src[:, :, TP:NT].rearrange("p s (b t) -> p s b t", b=NB)).then_inc(out[s], 1)
                act.wait_ge(out[s], pr.before() + 1)
                act.sem_inc(ext_ready, 1)
                st.c += 2
                pr.step()
                act.wait_ge(conv_ready, t + 1)
                nc.scalar.activation(gl[:, e, 0:CONVN], cv[:, e, 0, 0:CONVN], ACT.Gelu_apprx_tanh).then_inc(gelu_ready, 1)
                act.wait_ge(a_sum, t + 1)
                nc.scalar.copy(acts_hi[:, g, j, :], act_tmp[:, e, :]).then_inc(a_high, 1)

            def skip_down(t, g, k):
                last, small = k < FG, (FT - 5 * FG) * 256
                before_last = ahead.off is None and not last
                for n in range(8):
                    if not (last and n >= 6):
                        split_high(act, ahead, small if last or (before_last and n >= 6) else 2048)
                    st.c += 1
                    pr.step()

            ffn(act, st, pr, up, skip_down, ((ahead, 48),))
            assert ahead.c == st.c
            ahead.c += 2
            act.wait_ge(x_step, 2)
            square_x(18, (0, 1))
            for n in range(1, 22, 2):
                conv_rows_out(act, nc.scalar.copy, n)
                k = n // 2
                for s in range(2):
                    act.wait_ge(c_turned[s], k + 1)
                w = min(1024, 2 * FF - k * 1024)
                act.dma_start(o["conv_prompt"][:, k * 1024:k * 1024 + w], crow[k % 6][0:2, 0:w]).then_inc(c_stored[k % 6], 16)
                act.dma_start(o["conv_sample"][:, k * 1024:k * 1024 + w], crow[k % 6][2:18, 0:w]).then_inc(c_stored[k % 6], 16)
            square_x(18, (2, 3))
            root(UNITS["norm2"], rstd[:, 0, :], D)
            for q in range(4):
                h_highs(2, (q,))
                for n in (2 * q, 2 * q + 1):
                    s = pr.s
                    act.wait_ge(ple_filled, n + 1)
                    nc.scalar.copy(pl[:, 2 * n:2 * n + 2, :], ps[:, 2 * s:2 * s + 2, 0:NT]).then_inc(out[s], 1)
                    pr.step()
            for s in range(2):
                act.wait_ge(out[s], pr.n[s])
            st.c += 2
            for _ in range(2):
                split_high(act, ahead)
            for q in range(4):
                if q >= 2:
                    act.wait_ge(squares_used, 22 + q - 1)
                nc.scalar.activation(sq[:, q % 2, :], pl[:, 4 * q:4 * q + 4, :].rearrange("p k t -> p (k t)"),
                                     ACT.Square).then_inc(squares, 1)
            root(UNITS["norm3"], rstd[:, 1, :], D)

            def pg_pairs(i, last):
                for n in range(2):
                    if not (last and n):
                        for _ in range(2):
                            split_high(act, ahead)
                    src, free = taken(act, st, pr)
                    act.wait_ge(ple_ready, i * 2 + (1 + n))
                    nc.scalar.activation(sig[:, n, :, :], src, ACT.Sigmoid).then_inc(free, 1)
                    act.wait_ge(free, pr.n[pr.s ^ 1] + (0 if pr.off is None else i))
                    act.sem_inc(sig_ready, 1)

            with act.Fori(0, 3) as i:
                for x, per in ((ahead, 4), (st, 4), (pr, 1)):
                    x.begin(i, per)
                pg_pairs(i, False)
            for x in (ahead, st, pr):
                x.end(3)
            pg_pairs(3, True)
            for n in range(1, 12, 2):
                y_rows_out(act, nc.scalar.copy, n)

        @block.vector
        def _(ve):
            st, pr = Stream(), Pairs()
            v = Steps(ve, vec)
            V = nc.vector

            def evac(m, dst, src):
                ve.wait_ge(filled, m + 1)
                V.tensor_copy(dst, src).then_inc(freed[m % 4], 1)

            def norm_x(nth, row, turn, low):
                ve.wait_ge(rstd_ready, nth)
                v.link(V.reciprocal(rstd[:, 0, :], rstd[:, 0, :]))
                for q in range(5):
                    if q < 4:
                        if q >= 2:
                            ve.wait_ge(normed, 4 * turn + q - 1)
                        for k in range(4 * q, 4 * q + 4):
                            ins = V.scalar_tensor_tensor(norm_tmp[:, q % 2, k % 4 * NT:(k % 4 + 1) * NT], xT[:, k, :], col(row + k),
                                                         rstd[:, 0, :], ALU.mult, ALU.mult)
                        ins.then_inc(h_tmp, 1)
                    if q:
                        w = slice((q - 1) * 4 * NT, q * 4 * NT)
                        ve.wait_ge(h_high, 4 * turn + q)
                        V.tensor_tensor(low[:, w], norm_tmp[:, (q - 1) % 2, :], rh[:, w].bitcast(F32), ALU.subtract).then_inc(normed, 1)

            ve.wait_ge(small_in, 160)
            V.tensor_copy(small[R_DT:R_DT + SPAIR, :].rearrange("j (g n) -> j g n", g=2),
                          dt_raw.unsqueeze(2).to_broadcast([SPAIR, 2, N_SSM])).then_inc(small_ready, 1)
            m = UNITS["small"]
            evac(m, cols[:], ps[:, bank(m), 0:R_ALL])
            for n in range(12):
                m, j, q = UNITS["x"] + n, n // 4, n % 4
                w = rows(j)
                ve.wait_ge(filled, m + 1)
                V.tensor_copy(xT[:, 4 * q:4 * q + 4, j * P:j * P + w],
                              ps[:, bank(m), 0:4 * w].rearrange("p (k t) -> p k t", k=4)).then_inc(freed[m % 4], 1)
                ve.wait_ge(freed[m % 4], m // 4 + 1)
                ve.sem_inc(x_ready, 1)
            ve.wait_ge(x_stored, 16)
            norm_x(1, R_MIX, 0, rx)
            for n, unit in enumerate(conv_at):
                m, t0, k = UNITS["conv"] + n, unit[0][1], sum(x[2] for x in unit)
                evac(m, convT[:, t0:t0 + k, :], ps[:, bank(m), 0:k * 20].rearrange("p (k r) -> p k r", r=20))
            ve.wait_ge(table_in, 128)
            ve.wait_ge(first_in, 32)
            ve.wait_ge(consts_in, 80)
            v.link(V.tensor_scalar(pidf[:], pidx[:], 8.0, sc[:, 44:45], ALU.mult, ALU.add))
            V.tensor_copy(pidx[:], pidf[:]).then_inc(table_ready, 1)

            ve.wait_ge(used, st.count(1))
            V.tensor_copy(ikT[0:80, :], ps[0:80, 0, 0:NT]).then_inc(out[0], 1)
            st.c += 2
            pr.step()
            for n in range(2):
                src, free = taken(ve, st, pr)
                V.tensor_copy(uT[:, 2 * n:2 * n + 2, :], src).then_inc(free, 1)
            for dst, times in ((iqT, 2), (qkvT, 3)):
                with ve.Fori(0, times) as i:
                    st.begin(i, 4)
                    pr.begin(i, 1)
                    for n in range(2):
                        src, free = taken(ve, st, pr)
                        V.tensor_copy(dst[:, bass.ds(i * 4 + 2 * n, 2), :], src).then_inc(free, 1)
                st.end(times)
                pr.end(times)
            for s in range(2):
                ve.wait_ge(out[s], pr.n[s])
                ve.sem_inc(a_out, 2)

            for k in range(10):
                ve.wait_ge(rstd_ready, 2 + k)
                v.link(V.reciprocal(oT[:, 4 + k % 4, :], oT[:, 4 + k % 4, :]))
                V.scalar_tensor_tensor(qkvT[:, k, :], qkvT[:, k, :], col(R_GQ if k < 8 else R_GK), oT[:, 4 + k % 4, :],
                                       ALU.mult, ALU.mult).then_inc(head_normed, 1)
            ve.wait_ge(ropes_in, 16)
            for j in range(19):
                m, n, sin = UNITS["ropeq"] + j, P if j < 18 else IDIM, 1 if j < 10 else 3
                ve.wait_ge(filled, m + 1)
                if j >= 8:
                    ve.wait_ge(roped, j - 7)
                V.tensor_tensor(by_sine[0:n, j % 8, :], ps[0:n, bank(m), 0:NT], ropes[0:n, sin, :], ALU.mult).then_inc(freed[m % 4], 1)
                ve.wait_ge(freed[m % 4], m // 4 + 1)
                ve.sem_inc(sined, 1)
            ve.wait_ge(roped, 19)
            v.mark(V.tensor_copy(ik2[0:IDIM, :], ikT[0:IDIM, :]))
            v.link(V.tensor_copy(ik2[IDIM:P, :], ikT[0:IDIM, :]))
            v.mark(V.memset(qb, 0.0))
            v.link(V.memset(nk, 0.0))
            for j2 in range(2):
                for hp in range(2):
                    for b in range(NB):
                        t0 = TP + b * TQ
                        dst = qb[j2 * 64:j2 * 64 + 64, b, j2 * 64:j2 * 64 + 64].rearrange("p (h q t) -> p h q t", q=2, t=TQ)
                        v.mark(V.tensor_copy(dst[:, :, hp, :], iqT[hp * 64:hp * 64 + 64, :, t0:t0 + TQ]))
            v.link(V.tensor_copy(nk[0:IDIM], ikT[0:IDIM, TP:NT].rearrange("p (b t) -> p b t", t=TQ)))
            for n in range(6):
                m, tt = UNITS["tok"] + n, n // 2
                w, lo, hi = rows(tt), (0, 512)[n % 2], (512, 592)[n % 2]
                evac(m, tok[0:w, tt, lo:hi], ps[0:w, bank(m), 0:hi - lo])
                ve.wait_ge(freed[m % 4], m // 4 + 1)
                ve.sem_inc(tok_ready, 1)
            m = UNITS["wb"]
            ve.wait_ge(filled, m + 1)
            V.tensor_tensor(wmask[:], ps[:, bank(m), 0:TS].unsqueeze(1).to_broadcast([P, 2 * NB, TS]), wmask[:],
                            ALU.mult).then_inc(freed[m % 4], 1)
            ve.wait_ge(freed[m % 4], m // 4 + 1)
            ve.sem_inc(wb_ready, 1)

            for tt in range(2):
                s = pscore[:, tt, 0, :]
                for i in range(4):
                    for par in range(2):
                        n = tt * 8 + i * 2 + par
                        ve.wait_ge(relu_ready, n + 1)
                        for k in range(2):
                            h = 2 * (2 * i + k) + par
                            src, wt = relu[:, n % 4, k * 256:k * 256 + 256], tok[:, tt, 576 + h:577 + h]
                            if i == par == k == 0:
                                v.link(V.tensor_scalar(s, src, wt, None, ALU.mult))
                            else:
                                v.link(V.scalar_tensor_tensor(s, src, wt, s, ALU.mult, ALU.add))
                        ve.sem_inc(relu_summed, 1)
                v.link(V.tensor_tensor(s, s, causal[:, tt, :], ALU.add))
            S0, S1 = work[0:TS, 0, :], work[0:TS, 1, :]
            slots = S0[:, 0:PAST].rearrange("r (p j q) -> r q j p", j=8, q=2)
            for blk in range(2):
                ve.wait_ge(blk_scored, blk + 1)
                for q in range(2):
                    V.tensor_copy(slots[:, q, 4 * blk:4 * blk + 4, :],
                                  ps[q * TS:(q + 1) * TS, blk, :].rearrange("r (j p) -> r j p", j=4)).then_inc(blk_out, 1)
            ve.wait_ge(blk_scored, 3)
            V.tensor_tensor(S0[:, PAST:PAST + TQ], ps[0:TS, 2, 0:TQ], cnew[:, 0:TQ], ALU.add).then_inc(blk_out, 1)
            ve.wait_ge(blk_out, 5)

            def q_(k):
                return ssm0[:, k, :]

            are, aim = cols[:, R_ARE:R_ARE + SPAIR], cols[:, R_AIM:R_AIM + SPAIR]

            def tt(d, x, y, op):
                v.link(V.tensor_tensor(d, x, y, op))

            ve.wait_ge(act_params, 1)
            v.link(V.tensor_tensor(q_(1), are, q_(0), ALU.mult))
            ve.sem_inc(params_in, 1)
            tt(q_(2), aim, q_(0), ALU.mult)
            v.link(V.tensor_scalar(q_(4), q_(2), 1.0 / TURN, MAGIC, ALU.mult, ALU.add))
            v.link(V.tensor_scalar(q_(4), q_(4), MAGIC, None, ALU.subtract))
            v.link(V.scalar_tensor_tensor(q_(5), q_(4), -TURN_HI, q_(2), ALU.mult, ALU.add))
            v.link(V.scalar_tensor_tensor(q_(5), q_(4), -TURN_LO, q_(5), ALU.mult, ALU.add))
            v.link(V.tensor_scalar(q_(6), q_(5), 1.0 / TURN, None, ALU.mult))
            v.link(V.tensor_scalar(q_(8), q_(6), COARSE, COARSE, ALU.add, ALU.subtract))
            v.link(V.scalar_tensor_tensor(q_(7), q_(8), -TURN_HI, q_(5), ALU.mult, ALU.add))
            v.link(V.scalar_tensor_tensor(q_(7), q_(8), -TURN_LO, q_(7), ALU.mult, ALU.add))
            v.link(V.tensor_scalar(q_(9), q_(7), 1.0 / TURN, None, ALU.mult))
            ve.sem_inc(params, 1)
            for k, shift in ((10, 0.0), (11, 0.25)):
                v.link(V.tensor_scalar(q_(k), q_(6), shift, None, ALU.add))
                v.link(V.tensor_scalar(q_(4), q_(k), MAGIC, MAGIC, ALU.add, ALU.subtract))
                tt(q_(k), q_(k), q_(4), ALU.subtract)
                v.link(V.tensor_scalar(q_(k), q_(k), HALF, -HALF, ALU.min, ALU.max))
            ve.sem_inc(params_in, 1)
            tt(q_(4), are, are, ALU.mult)
            tt(q_(5), aim, aim, ALU.mult)
            tt(q_(4), q_(4), q_(5), ALU.add)
            v.link(V.reciprocal(q_(18), q_(4)))
            ve.wait_ge(act_params, 3)
            tt(q_(14), q_(3), q_(13), ALU.mult)
            tt(q_(15), q_(3), q_(12), ALU.mult)
            v.link(V.tensor_scalar(q_(4), q_(14), -1.0, None, ALU.add))
            tt(q_(5), q_(4), are, ALU.mult)
            tt(q_(6), q_(15), aim, ALU.mult)
            tt(q_(5), q_(5), q_(6), ALU.add)
            tt(q_(16), q_(5), q_(18), ALU.mult)
            tt(q_(5), q_(15), are, ALU.mult)
            tt(q_(6), q_(4), aim, ALU.mult)
            tt(q_(5), q_(5), q_(6), ALU.subtract)
            tt(q_(17), q_(5), q_(18), ALU.mult)
            def top(src, dst, k):
                for r in range(k // 8):
                    v.link(V.max(m8[0:src.shape[0]], src if r == 0 else dst))
                    v.link(V.match_replace(dst, m8[0:src.shape[0]], src if r == 0 else dst, TAKEN))

            for tt in range(2):
                s, left = pscore[:, tt, 0, :], pscore[:, tt, 1, :]
                top(s, left, TOPK_P)
                v.link(V.tensor_scalar(left, left, TAKEN / 1.5, OFF, ALU.is_ge, ALU.mult))
                V.tensor_tensor(left, left, causal[:, tt, :], ALU.add).then_inc(pb_ready, 1)
            top(S0, S1, TOPK_S)
            V.tensor_scalar(selb[:, 0:PAST].rearrange("r (j p) -> r j p", j=SLOT),
                            S1[:, 0:PAST].rearrange("r (p j) -> r j p", j=SLOT), TAKEN / 1.5, OFF, ALU.is_ge, ALU.mult)
            v.link(V.tensor_scalar(sc[0:TS, 40:44], S1[:, PAST:PAST + TQ], TAKEN / 1.5, OFF, ALU.is_ge, ALU.mult))
            V.tensor_tensor(selb[:, PAST:PAST + TS].rearrange("r (b t) -> r b t", t=TQ),
                            sc[0:TS, 40:44].unsqueeze(1).to_broadcast([TS, NB, TQ]),
                            cnew[:, TQ:TQ + TS].rearrange("r (b t) -> r b t", t=TQ), ALU.add).then_inc(sb_ready, 1)

            v.link(V.tensor_copy(rowsb[:], rowsf[:]))
            ve.wait_ge(ssm_in, 16 * 8)
            v.link(V.memset(bbd, 0.0))
            v.mark(V.memset(cl, 0.0))
            f = [q_(k).unsqueeze(2).to_broadcast([P, SPAIR, C_SSM]) for k in (16, 17)]
            for k, (x, y) in enumerate(((0, 0), (1, 1), (0, 1), (1, 0))):
                v.mark(V.tensor_tensor(btmp[:, k], f[x], braw[:, y], ALU.mult))
            v.wait()
            for g in range(2):
                r = slice(64 * g, 64 * g + 64)
                for ri, op in ((0, ALU.subtract), (1, ALU.add)):
                    x, y = (btmp[r, 2 * ri + k].rearrange("p (q j) c -> p q j c", q=4) for k in range(2))
                    ins = V.tensor_tensor(bbd[r, :, ri, :, g, :], x, y, op)
                    v.mark(ins)
            v.wait()
            ve.sem_inc(ssm_tabs, 1)
            walk(st, pr, "gates")
            ve.wait_ge(used, C_GLU)
            v.link(V.tensor_copy(ssmv, ssm0))
            for n in range(2):
                m = UNITS["bt"] + n
                evac(m, bl[:, 2 * n:2 * n + 2], ps[:, bank(m), :].rearrange("p (q r n) -> p q r n", q=2, r=2))
            for n in range(2):
                m = UNITS["ct"] + n
                ve.wait_ge(filled, m + 1)
                src = ps[:, bank(m), :].rearrange("p (q r j g c) -> p q r j g c", q=2, r=2, j=4, g=2)
                for g in range(2):
                    p_ = slice(64 * g, 64 * g + 64)
                    for ri in range(2):
                        for q in range(2):
                            j0 = 4 * (2 * n + q)
                            v.mark(V.tensor_scalar(cl[p_, j0:j0 + 4, ri, g * 16:g * 16 + 16], src[p_, q, ri, :, g, :],
                                                   -1.0 if ri else 1.0, None, ALU.mult))
                v.wait()
                ve.sem_inc(freed[m % 4], 1)
            m = UNITS["ini"]
            for k in range(2):
                evac(m + k, fw[:, 2048 + k * P:2048 + (k + 1) * P], ps[:, bank(m + k), 0:P])
                ve.wait_ge(freed[(m + k) % 4], (m + k) // 4 + 1)
            ve.sem_inc(ssm_tabs, 1)

            U = UNITS["step"]

            def scores(i):
                m = U + 6 * i - 4 if i else UNITS["first"]
                w, t, k = P * (i % 2 + 1), i % 2, i % 2
                ve.wait_ge(filled, m + 1)
                if i >= 2:
                    ve.wait_ge(p_turned, i - 1)
                V.tensor_tensor_reduce(psc[k][:, 0:w], ps[:, bank(m), 0:w], pscore[:, t, 1, 0:w], 1.0, -3.0e38, ALU.add, ALU.max,
                                       accum_out=sc[:, k:k + 1]).then_inc(freed[m % 4], 1)
                return m

            def limit(m, k):
                ve.wait_ge(freed[m % 4], m // 4 + 1)
                V.tensor_scalar(sc[:, 2 + k:3 + k], sc[:, k:k + 1], -(HD ** -0.5), None, ALU.mult).then_inc(p_max, 1)

            limit(scores(0), 0)
            by_cos, by_sin = rot
            for j in range(SPAIR):
                mr = UNITS["step"] + 6 * j
                k, w = j % 2, P * (j % 2 + 1)
                cs, sn = (trig[k][:, x, :].unsqueeze(1).to_broadcast([P, 2, TP]) for x in range(2))
                both_ = ps[:, bank(mr):bank(mr) + 2, 0:TP]
                ve.wait_ge(p_exp, j + 1)
                inverse = v.mark(V.reciprocal(sc[:, 6 + k:7 + k], sc[:, 4 + k:5 + k]))
                ve.wait_ge(filled, mr + 2)
                ve.wait_ge(trig_ready, j + 1)
                v.mark(V.tensor_tensor(by_cos, both_, cs, ALU.mult))
                v.upto(inverse)
                V.tensor_scalar(psc[k][:, 0:w], psc[k][:, 0:w], sc[:, 6 + k:7 + k], None, ALU.mult).then_inc(p_norm, 1)
                products_ = v.mark(V.tensor_tensor(by_sin, both_, sn, ALU.mult))
                m = scores(j + 1) if j < 15 else None
                v.upto(products_)
                ve.sem_inc(rotated, 1)
                v.mark(V.tensor_tensor(turned[:, 0], by_cos[:, 0], by_sin[:, 1], ALU.add))
                v.mark(V.tensor_tensor(turned[:, 1], by_cos[:, 1], by_sin[:, 0], ALU.subtract))
                if j < 15:
                    limit(m, (j + 1) % 2)
                v.wait()
                mag = ssmv[:, 3, j:j + 1].to_broadcast([P, TP])
                for k in range(2):
                    v.mark(V.tensor_tensor_scan(by_cos[:, k], mag, turned[:, k], 0.0, ALU.mult, ALU.add))
                v.wait()
                if j >= 2:
                    ve.wait_ge(state_used, j - 1)
                S = states[j % 2]
                v.mark(V.tensor_tensor(by_sin, by_cos, sn, ALU.mult))
                v.link(V.tensor_tensor(turned, by_cos, cs, ALU.mult))
                v.mark(V.tensor_tensor(S[:, 0], turned[:, 0], by_sin[:, 1], ALU.subtract))
                v.link(V.tensor_tensor(S[:, 1], turned[:, 1], by_sin[:, 0], ALU.add))
                ve.sem_inc(state_ready, 1)
                v.mark(V.tensor_copy(ssmv[:, 20:22, j:j + 1], S[:, :, TP - 1:TP]))
            v.wait()
            assert UNITS["step"] % 2 == 0
            by_re, by_im = area(fw, 1536, (2, NB, SPAIR)), area(fw, 1792, (2, NB, SPAIR))
            both_ab = [x.unsqueeze(1).to_broadcast([P, 2, NB, SPAIR]) for x in (ssmv[:, 14, :].unsqueeze(1), ssmv[:, 15, :].unsqueeze(1))]
            ve.wait_ge(bus_out, 16)
            for t in range(TQ):
                prev = ini if t == 0 else sst[:, :, :, :, t - 1]
                v.mark(V.tensor_tensor(by_re, both_ab[0], prev, ALU.mult))
                v.link(V.tensor_tensor(by_im, both_ab[1], prev, ALU.mult))
                v.mark(V.tensor_tensor(by_re[:, 0], by_re[:, 0], by_im[:, 1], ALU.subtract))
                v.link(V.tensor_tensor(by_re[:, 1], by_re[:, 1], by_im[:, 0], ALU.add))
                v.link(V.tensor_tensor(sst[:, :, :, :, t], by_re, bus[:, :, :, :, t], ALU.add))
            ve.sem_inc(samples_ready, 1)
            for q in range(4):
                ve.wait_ge(state_used, 16 + 4 * (q + 1))
                if q == 0:
                    ve.wait_ge(trig_ready, SPAIR)
                V.scalar_tensor_tensor(yt[:, q, :], uT[:, q, :], col(R_D + q), ps[:, q, 0:NT], ALU.mult, ALU.add).then_inc(y_ready, 1)
            m = UNITS["fin"]
            evac(m, rows_out[0:2 * SPAIR, 0, :], ps[0:2 * SPAIR, bank(m), 0:P])
            ve.wait_ge(freed[m % 4], m // 4 + 1)
            ve.sem_inc(state_out, 1)
            evac(m + 1, rows_out[:, 1:3, :], ps[:, bank(m + 1), 0:256].rearrange("p (r n) -> p r n", r=2))
            ve.wait_ge(freed[(m + 1) % 4], (m + 1) // 4 + 1)
            ve.sem_inc(state_out, 1)
            v.link(V.memset(fi[:, 0:2048], 0.0))
            for b in range(NB):
                for g in range(2):
                    c0 = b % 4 * 32 + g * 16
                    v.mark(V.tensor_copy(qz[:, b, g, c0:c0 + 16].rearrange("p (r t) -> p r t", t=TQ),
                                         qkvT[:, g * 4:g * 4 + 4, TP + b * TQ:TP + (b + 1) * TQ]))
            v.wait()
            ve.sem_inc(qz_ready, 1)
            for n in range(2):
                _, free = pr.s, out[pr.s]
                st.c += 1
                pr.step()
                ve.wait_ge(free, pr.n[pr.s ^ 1])
            v.link(V.tensor_tensor(uT, uT, sg, ALU.mult))
            ve.sem_inc(glu_ready, 1)
            ve.wait_ge(z_high, 1)
            V.tensor_tensor(z_lo, uT, z_hi.bitcast(F32), ALU.subtract).then_inc(z_split, 1)

            kk = Turns()

            def turn(dst, src):
                k = kk.next()
                if k % 2:
                    ve.wait_ge(k_filled, k + 1)
                    V.tensor_copy(dst, src(k % 2)).then_inc(k_freed[1], 1)

            ve.wait_ge(state_stored, 64)
            for half in range(2):
                for b in range(4 * half, 4 * half + 4):
                    if b == 4:
                        ve.wait_ge(pv_done, 4)
                    for n in range(8):
                        if b and kk.k % 2:
                            ve.wait_ge(s_free, 8 * b + n - 7)
                        turn(kT[:, n // 4, n % 4 * 512:n % 4 * 512 + 512], lambda s: ps[:, s, :])
                ve.wait_ge(s_free, 32 * (half + 1))
                v.mark(V.tensor_reduce(sc[:, 8:9], ps[:, 4:8, :].rearrange("p k n -> p (k n)"), AX, ALU.max))
                v.link(V.tensor_reduce(sc[:, 9:10], ps[:, 3, 0:TS], AX, ALU.max))
                v.link(V.tensor_tensor(sc[:, 10:11], sc[:, 8:9], sc[:, 9:10], ALU.max))
                v.link(V.tensor_scalar(sc[:, 11:12], sc[:, 10:11], -(HD ** -0.5), None, ALU.mult))
                ve.sem_inc(s_max, 1)
                ve.wait_ge(s_exp, 2 * half + 2)
                v.link(V.tensor_tensor(sc[:, 14:15], sc[:, 12:13], sc[:, 13:14], ALU.add))
                v.link(V.reciprocal(sc[:, 15:16], sc[:, 14:15]))
                for n in range(4):
                    w = slice(512 * n, 512 * n + 512 if n < 3 else PAST + TS)
                    V.tensor_scalar(sp_[:, w], sp_[:, w], sc[:, 15:16], None, ALU.mult).then_inc(s_norm, 1)
                for n in range(4):
                    turn(spT[:, 4 * n:4 * n + 4, :], lambda s: ps[:, s, :].rearrange("p (j n) -> p j n", j=4))
                turn(spN, lambda s: ps[0:TS, s, 0:P])

                def spread(b):
                    t0 = TP + b * TQ
                    k = kk.next()
                    if k % 2:
                        ve.wait_ge(k_filled, k + 1)
                        for g in range(2):
                            ins = V.tensor_copy(oT[:, g * 4:g * 4 + 4, t0:t0 + TQ],
                                                ps[:, 1, g * 48:g * 48 + 16].rearrange("p (r t) -> p r t", t=TQ))
                        ins.then_inc(k_freed[1], 1)

                for b in range(4 * half, 4 * half + 4):
                    ve.wait_ge(pv_done, b + 1)
                    if b % 4 >= 2:
                        ve.wait_ge(k_filled, kk.k)
                    V.tensor_copy(os_[b % 2], ps[0:TS, 2 + b % 2, 0:256]).then_inc(os_ready, 1)
                    if b % 4:
                        spread(b - 1)
                spread(4 * half + 3)
            ve.wait_ge(k_freed[1], kk.k // 2)
            ve.sem_inc(o_ready, 1)

            ve.wait_ge(o_high, 1)
            V.tensor_tensor(o_lo, oT[:], o_hi.bitcast(F32), ALU.subtract).then_inc(o_split, 1)

            for n in range(8):
                s = n % 2
                ve.wait_ge(used, st.count(1))
                t0, t1_ = gates[:, 2 * n:2 * n + 2, :], gates[:, KD + 2 * n:KD + 2 * n + 2, :]
                v.mark(V.tensor_tensor(t0, t0, ps[:, 4 * s:4 * s + 2, 0:NT], ALU.mult))
                v.link(V.tensor_tensor(t1_, t1_, ps[:, 4 * s + 2:4 * s + 4, 0:NT], ALU.mult))
                v.link(V.tensor_tensor(t0, t0, t1_, ALU.add))
                ve.sem_inc(m_sum, 1)
                ve.wait_ge(m_high, n + 1)
                k = slice(2 * n, 2 * n + 2)
                V.tensor_tensor(m_lo[:, k, :], t0, m_hi[:, k, :].bitcast(F32), ALU.subtract).then_inc(merged, 1)
                st.c += 2
            for half in range(2):
                ve.wait_ge(x_back[half], 16)
                with ve.Fori(0, 2) as i:
                    st.begin(i, 4)
                    pr.begin(i, 1)
                    for n in range(2):
                        src, free = taken(ve, st, pr)
                        x = xT[:, bass.ds(i * 4 + (8 * half + 2 * n), 2), :]
                        V.tensor_tensor(x, x, src, ALU.add).then_inc(free, 1)
                st.end(2)
                pr.end(2)
            for s in range(2):
                ve.wait_ge(out[s], pr.n[s])
            ve.sem_inc(x_step, 1)
            norm_x(12, R_FFN, 1, rw)

            ve.wait_ge(stored, 9 * 16)
            conv_cols = convT[:].rearrange("p (s f) r -> p s f r", s=2)
            v.mark(V.memset(ext[:, :, :, 0:2], 0.0))
            ext_s = ext[:, :, :, EXT_S:EXT].rearrange("p e s (b t) -> p e s b t", b=NB)
            cout_s = cout[:, :, :, 2:18].rearrange("p s f (b t) -> p s f b t", b=NB)
            gl_s = gl[:, :, EXT_S:EXT].rearrange("p e (b t) -> p e b t", b=NB)
            cv_s = cv[:, :, 1, EXT_S:EXT].rearrange("p e (b t) -> p e b t", b=NB)

            def up(t, g, j):
                e = pr.s
                v.link(V.tensor_copy(taps[:, e], conv_cols[:, :, bass.ds(t, 1), :].rearrange("p s o r -> p s (o r)")))
                v.link(V.tensor_copy(ext_s[:, e, :, :, 0:2], taps[:, e, :, 0:16].rearrange("p s (b r) -> p s b r", b=NB)))
                ve.wait_ge(ext_ready, t + 1)
                if pr.off is not None or j >= 2 or g:
                    ve.wait_ge(gelu_ready, t - 1)
                for s in range(2):
                    v.mark(V.tensor_scalar(cv[:, e, s, 0:CONVN], ext[:, e, s, 0:CONVN], taps[:, e, s, 16:17], taps[:, e, s, 19:20],
                                           ALU.mult, ALU.add))
                for k in (1, 2):
                    v.wait()
                    for s in range(2):
                        ins = V.scalar_tensor_tensor(cv[:, e, s, 0:CONVN], ext[:, e, s, k:k + CONVN], taps[:, e, s, 16 + k:17 + k],
                                                     cv[:, e, s, 0:CONVN], ALU.mult, ALU.add)
                        v.mark(ins)
                one = bass.ds(t, 1)
                v.mark(V.tensor_copy(cout[:, :, one, 0:2].rearrange("p s o r -> p s (o r)"), ext[:, e, :, TP:TP + 2]))
                for s in range(2):
                    v.mark(V.tensor_copy(cout_s[:, s, one].rearrange("p o b t -> p (o b) t"), ext_s[:, e, s, :, TQ:TQ + 2]))
                v.wait()
                ve.sem_inc(conv_ready, 1)
                ve.wait_ge(gelu_ready, t + 1)
                v.mark(V.tensor_tensor(act_tmp[:, e, 0:TP], gl[:, e, 0:TP], cv[:, e, 1, 0:TP], ALU.mult))
                v.link(V.tensor_tensor(act_tmp[:, e, TP:NT].rearrange("p (b t) -> p b t", b=NB), gl_s[:, e, :, 0:TQ],
                                       cv_s[:, e, :, 0:TQ], ALU.mult))
                ve.sem_inc(a_sum, 1)
                ve.wait_ge(a_high, t + 1)
                v.link(V.tensor_tensor(acts_lo[:, g, j, :], act_tmp[:, e, :], acts_hi[:, g, j, :].bitcast(F32), ALU.subtract))
                ve.sem_inc(act_ready, 1)
                st.c += 2
                pr.step()

            def down(t, g, k):
                for n in range(8):
                    src, free = taken(ve, st, pr, 1)
                    x = xT[:, 2 * n:2 * n + 2, :]
                    V.tensor_tensor(x, x, src, ALU.add).then_inc(free, 1)

            ffn(ve, st, pr, up, down, ((v, 2 * FG * UP_STEPS),))
            for s in range(2):
                ve.wait_ge(out[s], pr.n[s])
            ve.sem_inc(x_step, 1)
            for n in range(0, 22, 2):
                conv_rows_out(ve, V.tensor_copy, n)
            for n in range(2):
                m = UNITS["pt"] + n
                evac(m, pT[:, n, :], ps[:, bank(m), 0:NT])
                ve.wait_ge(freed[m % 4], m // 4 + 1)
                ve.sem_inc(ple_ready_p, 1)
            st.c += 2
            for _ in range(8):
                pr.step()
            norm_x(13, R_PG, 2, rw)
            ve.wait_ge(rstd_ready, 14)
            v.link(V.reciprocal(rstd[:, 1, :], rstd[:, 1, :]))
            for k in range(KD):
                v.mark(V.scalar_tensor_tensor(pl[:, k, :], pl[:, k, :], col(R_PLE + k), rstd[:, 1, :], ALU.mult, ALU.mult))
            v.wait()
            ve.sem_inc(ple_ready, 2)
            with ve.Fori(0, 4) as i:
                v.begin(i, 2)
                for n in range(2):
                    ve.wait_ge(sig_ready, i * 2 + (1 + n))
                    k = bass.ds(i * 4 + 2 * n, 2)
                    v.link(V.tensor_tensor(sig[:, n], sig[:, n], pl[:, k, :], ALU.mult))
                    V.tensor_tensor(xT[:, k, :], xT[:, k, :], sig[:, n], ALU.add).then_inc(ple_ready, 1)
            v.end(4)
            for n in range(0, 12, 2):
                y_rows_out(ve, V.tensor_copy, n)

        @block.tensor
        def _(pe):
            st, pr = Stream(), Pairs()
            T = nc.tensor

            def square_sum(m, base):
                fill_wait(pe, m)
                for q in range(4):
                    pe.wait_ge(squares, base + q + 1)
                    for k in range(4):
                        mm = T.matmul(ps[:, bank(m), 0:NT], ones, fo[:, (q % 2) * 1152 + k * NT:(q % 2) * 1152 + (k + 1) * NT],
                                      start=(q == k == 0), stop=(q == k == 3))
                    if q < 3:
                        mm.then_inc(squares_used, 1)
                mm.then_inc(filled, 1)
                pe.wait_ge(filled, m + 1)
                pe.sem_inc(squares_used, 1)

            pe.wait_ge(first_in, 32)
            m = UNITS["small"]
            fill_wait(pe, m)
            pe.wait_ge(small_in, 160)
            pe.wait_ge(small_ready, 1)
            T.transpose(ps[:, bank(m), 0:R_ALL], small[:], ident[0:R_ALL, 0:R_ALL]).then_inc(filled, 1)
            pe.wait_ge(x_in, 48)
            for n in range(12):
                m, j, q = UNITS["x"] + n, n // 4, n % 4
                w = rows(j)
                fill_wait(pe, m)
                for k in range(4):
                    mm = T.transpose(ps[:, bank(m), k * w:(k + 1) * w], xn[0:w, j, (4 * q + k) * P:(4 * q + k + 1) * P],
                                     ident[0:w, 0:w])
                mm.then_inc(filled, 1)
            square_sum(UNITS["norm0"], 0)
            pe.wait_ge(conv_in, 16 * 3 * sum(len(unit) for unit in conv_at))
            for n, unit in enumerate(conv_at):
                m = UNITS["conv"] + n
                fill_wait(pe, m)
                c = 0
                for src, _, k in unit:
                    for t in range(k):
                        mm = T.transpose(ps[:, bank(m), c:c + 20], src[0:20, t * P:(t + 1) * P], ident[0:20, 0:20])
                        c += 20
                mm.then_inc(filled, 1)
            products(pe, st, pr, (h_hi, h_lo0), [C_U - C_IK], norm=0)
            for n in range(2):
                products(pe, st, pr, (h_hi, h_lo0), [P, P])
            for times in (2, 3):
                with pe.Fori(0, times) as i:
                    st.begin(i, 4)
                    pr.begin(i, 1)
                    for n in range(2):
                        products(pe, st, pr, (h_hi, h_lo0), [P, P])
                st.end(times)
                pr.end(times)
            for j in range(10):
                m = UNITS["qkn"] + j
                fill_wait(pe, m)
                pe.wait_ge(squares, 4 + j + 1)
                T.matmul(ps[:, bank(m), 0:NT], ones, oT[:, j % 4, :], start=True, stop=True).then_inc(filled, 1)
                pe.wait_ge(filled, m + 1)
                pe.sem_inc(squares_used, 1)
            for j in range(19):
                m = UNITS["ropeq"] + j
                fill_wait(pe, m)
                if j < 10:
                    pe.wait_ge(head_normed, j + 1)
                    mm = T.matmul(ps[:, bank(m), 0:NT], turn_q, qkvT[:, j, :], start=True, stop=True)
                elif j < 18:
                    pe.wait_ge(a_out, 4)
                    mm = T.matmul(ps[:, bank(m), 0:NT], turn_i, iqT[:, j - 10, :], start=True, stop=True)
                else:
                    mm = T.matmul(ps[0:IDIM, bank(m), 0:NT], turn_i[0:IDIM, 0:IDIM], ikT[0:IDIM, :], start=True, stop=True)
                mm.then_inc(filled, 1)
            for n in range(6):
                m, tt = UNITS["tok"] + n, n // 2
                w, t0 = rows(tt), tt * P
                fill_wait(pe, m)
                pe.wait_ge(roped, 19)
                if n % 2 == 0:
                    for k in range(4):
                        mm = T.transpose(ps[0:w, bank(m), k * P:(k + 1) * P], qkvT[:, 8 + k, t0:t0 + w], ident)
                else:
                    mm = T.transpose(ps[0:w, bank(m), 0:80], ikT[0:80, t0:t0 + w], ident[0:80, 0:80])
                mm.then_inc(filled, 1)
            m = UNITS["wb"]
            fill_wait(pe, m)
            pe.wait_ge(consts_in, 80)
            T.matmul(ps[:, bank(m), 0:TS], headsel[:], ikT[0:80, TP:NT], start=True, stop=True).then_inc(filled, 1)
            def idx_keys(unit, b0):
                for n in range(8):
                    m, b, jh = UNITS[unit] + n, n // 2, n % 2
                    fill_wait(pe, m)
                    if n == 0:
                        pe.wait_ge(idx_in[b0 // 4], 64)
                    for k in range(4):
                        mm = T.transpose(ps[:, bank(m), k * P:(k + 1) * P], idx_raw[:, b, 4 * jh + k, :], ident)
                    mm.then_inc(filled, 1)

            idx_keys("idx", 0)
            for n in range(16):
                m, tt, i, par = UNITS["pidx"] + n, n // 8, n // 2 % 4, n % 2
                fill_wait(pe, m)
                r = slice(64 * par, 64 * par + 64)
                for k in range(2):
                    mm = T.matmul(ps[:, bank(m), k * 256:k * 256 + 256], iqT[r, 2 * i + k, tt * P:(tt + 1) * P],
                                  ik2[r, 0:TP], start=True, stop=True)
                mm.then_inc(filled, 1)
            idx_keys("idx2", 4)
            pe.wait_ge(wb_ready, 1)
            for s in range(2):
                pe.wait_ge(out[s], pr.n[s])

            def weigh(n):
                blk, b = n // NB, n % NB
                w = 512 if blk < 2 else TQ
                pe.wait_ge(relu_ready, 16 + n + 1)
                T.matmul(ps[0:2 * TS, blk, 0:w], wheads[:, b, :], relu[:, n % 4, 0:w], start=(b == 0),
                         stop=(b == NB - 1)).then_inc(relu_weighed, 1)
                if b == NB - 1:
                    pe.wait_ge(relu_weighed, n + 1)
                    pe.sem_inc(blk_scored, 1)

            for n in range(24):
                m, blk, b = UNITS["sidx"] + n, n // NB, n % NB
                fill_wait(pe, m)
                w, keys = (512, idxT[:, b, blk * 512:(blk + 1) * 512]) if blk < 2 else (TQ, nk[:, b, :])
                T.matmul(ps[:, bank(m), 0:w], qb[:, b, :], keys, start=True, stop=True).then_inc(filled, 1)
                if n:
                    weigh(n - 1)
            weigh(23)
            pe.wait_ge(blk_out, 5)
            with pe.Fori(0, 8) as i:
                st.begin(i, 4)
                pr.begin(i, 1)
                for n in range(2):
                    products(pe, st, pr, (h_hi, h_lo0), [P, P])
            st.end(8)
            pr.end(8)

            pe.wait_ge(ssm_tabs, 1)
            for n in range(2):
                m = UNITS["bt"] + n
                fill_wait(pe, m)
                for k in range(4):
                    src = bbd[:, 2 * n + k // 2, k % 2].rearrange("p j g c -> p (j g c)")
                    mm = T.transpose(ps[:, bank(m), k * P:(k + 1) * P], src, ident)
                mm.then_inc(filled, 1)
            for n in range(2):
                m = UNITS["ct"] + n
                fill_wait(pe, m)
                for k in range(4):
                    src = craw[:, 2 * n + k // 2, k % 2].rearrange("p d n -> p (d n)")
                    mm = T.transpose(ps[:, bank(m), k * P:(k + 1) * P], src, ident)
                mm.then_inc(filled, 1)
            m = UNITS["ini"]
            for k in range(2):
                fill_wait(pe, m + k)
                T.transpose(ps[:, bank(m + k), 0:P], ini_raw[:, k], ident).then_inc(filled, 1)
            for s in range(2):
                pe.wait_ge(out[s], pr.n[s])
            pe.wait_ge(ssm_tabs, 2)

            def c_states(j, src, t0, n):
                q, g = j // 4, 32 * (j % 4)
                for r in range(2):
                    mm = T.matmul(ps[g:g + 32, q, t0:t0 + n], cl[:, j, r, :], src(r), start=(r == 0), stop=(r == 1))
                mm.then_inc(state_used, 1)

            U = UNITS["step"]

            def scores(i, m):
                h, t = i // 2, i % 2
                fill_wait(pe, m)
                T.matmul(ps[:, bank(m), 0:P * (t + 1)], qkvT[:, h, t * P:(t + 1) * P], qkvT[:, 8 + h // GRP, 0:P * (t + 1)],
                         start=True, stop=True).then_inc(filled, 1)

            def idle_unit(m):
                fill_wait(pe, m)
                pe.wait_ge(filled, m)
                pe.sem_inc(filled, 1)
                pe.sem_inc(freed[m % 4], 1)

            pe.wait_ge(pb_ready, 2)
            scores(0, UNITS["first"])
            idle_unit(UNITS["first"] + 1)
            for i in range(16):
                m = U + 6 * i
                q, g = i // 4, slice(32 * (i % 4), 32 * (i % 4) + 32)
                for r in range(2):
                    fill_wait(pe, m + r)
                    T.matmul(ps[:, bank(m + r), 0:NT], bl[g, q, r, :], uT[g, q, :], start=True, stop=True).then_inc(filled, 1)
                if i < 15:
                    scores(i + 1, m + 2)
                else:
                    idle_unit(m + 2)
                if i:
                    pe.wait_ge(state_ready, i)
                    c_states(i - 1, lambda r: states[(i - 1) % 2][:, r, :], 0, TP)
                h, t = i // 2, i % 2
                fill_wait(pe, m + 3)
                pe.wait_ge(p_norm, i + 1)
                for k in range(t + 1):
                    mm = T.transpose(ps[:, bank(m + 3), k * P:(k + 1) * P], psc[i % 2][:, k * P:(k + 1) * P], ident)
                mm.then_inc(filled, 1)
                fill_wait(pe, m + 4)
                pe.wait_ge(p_turned, i + 1)
                g0 = 256 + h // GRP * HD
                for k in range(t + 1):
                    mm = T.matmul(ps[:, bank(m + 4), 0:P], tok[:, k, g0:g0 + HD], ppt[i % 2][:, k, :], start=(k == 0), stop=(k == t))
                mm.then_inc(filled, 1)
                idle_unit(m + 5)
            pe.wait_ge(state_ready, 16)
            c_states(15, lambda r: states[1][:, r, :], 0, TP)
            pe.wait_ge(samples_ready, 1)
            for j in range(SPAIR):
                c_states(j, lambda r: sst[:, r, :, j, :], TP, TS)
            m = UNITS["fin"]
            fill_wait(pe, m)
            T.transpose(ps[0:32, bank(m), 0:P], ssmv[:, 20:22, :].rearrange("p r j -> p (r j)"), ident).then_inc(filled, 1)
            fill_wait(pe, m + 1)
            for r in range(2):
                src = sst[:, r].rearrange("p b j t -> p (b j) t")[:, :, TQ - 1]
                mm = T.transpose(ps[:, bank(m + 1), r * P:(r + 1) * P], src, ident)
            mm.then_inc(filled, 1)
            pe.wait_ge(z_ready, 4)
            for n in range(2):
                pe.wait_ge(out[pr.s], pr.before())
                pe.wait_ge(landed[st.slot()], st.landed())
                w = ring[:, st.slot(), 0:1024].rearrange("p (k n) -> p k n", k=4)
                for c in range(2):
                    for k in range(4):
                        mm = T.matmul(ps[:, 2 * pr.s + c, 0:NT], w[:, k, c * P:(c + 1) * P], uT[:, k, :], start=(k == 0),
                                      stop=(k == 3))
                mm.then_inc(used, 1)
                st.c += 1
                pr.step()
            st.whole += 2
            kk = Turns()

            def turn():
                k = kk.next()
                if k >= 2:
                    pe.wait_ge(k_freed[k % 2], k // 2)
                return k % 2

            pe.wait_ge(qz_ready, 1)
            for s in range(2):
                pe.wait_ge(out[s], pr.n[s])
            for m in range(UNITS["norm1"] - 4, UNITS["norm1"]):
                pe.wait_ge(freed[m % 4], m // 4 + 1)
            for half in range(2):
                if half:
                    pe.wait_ge(s_exp, 2)
                for n in range(4):
                    T.matmul(ps[:, 4 + n, :], rowsb[:, half, :], selb[:, n * 512:n * 512 + 512], start=True, stop=False,
                             skip_group_check=True)
                if half:
                    pe.wait_ge(os_ready, 4)
                T.matmul(ps[:, 3, 0:TS], rowsb[:, half, :], selb[:, PAST:PAST + TS], start=True, stop=False,
                         skip_group_check=True)

                def score(u):
                    b, g, n = u // 8, u // 4 % 2, u % 4
                    last = u % 32 >= 28
                    s = (turn0 + u % 32) % 2
                    pe.wait_ge(k_freed[s], (turn0 + u % 32) // 2 + 1)
                    mm = T.matmul(ps[:, 4 + n, :], qz[:, b, g, :], kT[:, g, n * 512:n * 512 + 512], start=False,
                                  stop=last, skip_group_check=True)
                    if n == 3:
                        mm = T.matmul(ps[:, 3, 0:TS], qz[:, b, g, :], qkvT[:, 8 + g, TP:NT], start=False,
                                      stop=last, skip_group_check=True)
                    mm.then_inc(s_free, 1)

                turn0 = kk.k
                for u in range(32 * half, 32 * half + 32):
                    b, g, n = u // 8, u // 4 % 2, u % 4
                    if u % 8 == 0:
                        pe.wait_ge(k_in[b % 2], 16 * (b // 2 + 1))
                    s = turn()
                    for k in range(4):
                        mm = T.transpose(ps[:, s, k * P:(k + 1) * P], kraw[b % 2][:, n * 4 + k, g * P:(g + 1) * P], ident)
                    mm.then_inc(k_filled, 1)
                    if u % 32 >= 4:
                        score(u - 4)
                    if u % 8 == 7:
                        pe.wait_ge(k_filled, kk.k)
                        pe.sem_inc(k_used, 1)
                for u in range(32 * half + 28, 32 * half + 32):
                    score(u)
                pe.wait_ge(s_free, 32 * (half + 1))
                pe.sem_inc(s_scored, 1)
                for n in range(5):
                    s = turn()
                    pe.wait_ge(s_norm, 4 * half + min(n, 3) + 1)
                    if n < 4:
                        for k in range(4):
                            j = 4 * n + k
                            mm = T.transpose(ps[:, s, k * P:(k + 1) * P], sp_[:, j * P:(j + 1) * P], ident)
                    else:
                        mm = T.transpose(ps[0:TS, s, 0:P], sp_[:, PAST:PAST + TS], ident)
                    mm.then_inc(k_filled, 1)
                for s in range(2):
                    pe.wait_ge(k_freed[s], (kk.k + 1 - s) // 2)

                def turn_rows(b):
                    s = turn()
                    pe.wait_ge(os_ready, b + 1)
                    for g in range(2):
                        mm = T.transpose(ps[:, s, g * 32:g * 32 + 32], os_[b % 2][:, g * P:(g + 1) * P], ident[0:TS, 0:TS])
                    mm.then_inc(k_filled, 1)

                for b in range(4 * half, 4 * half + 4):
                    c = slice(b % 4 * 32, b % 4 * 32 + 32)
                    pe.wait_ge(v_in[b % 2], 16 * (b // 2 + 1))
                    if b % 4 >= 2:
                        pe.wait_ge(os_ready, b - 1)
                    dst = ps[0:TS, 2 + b % 2, 0:256]
                    for j in range(SLOT):
                        T.matmul(dst, spT[:, j, c], vraw[b % 2][:, j, :], start=(j == 0), stop=False)
                    T.matmul(dst, spN[:, c], tok[0:TS, 2, 256:512], start=False, stop=True).then_inc(pv_done, 1)
                    if b % 4:
                        turn_rows(b - 1)
                turn_rows(4 * half + 3)
            pe.wait_ge(o_ready, 2)
            pe.wait_ge(o_split, 1)
            pe.wait_ge(z_split, 1)
            for n in range(8):
                s = n % 2
                if n >= 2:
                    pe.wait_ge(merged, n - 1)
                for kt, rhs, b0 in ((8, (o_hi, o_lo), 4 * s), (4, (z_hi, z_lo), 4 * s + 2)):
                    chunk(pe, st, [(b0, P), (b0 + 1, P)], rhs, 0, kt, True, True)
            pe.wait_ge(merged, 8)
            with pe.Fori(0, 4) as i:
                st.begin(i, 4)
                pr.begin(i, 1)
                for n in range(2):
                    products(pe, st, pr, (m_hi, m_lo), [P, P])
            st.end(4)
            pr.end(4)
            square_sum(UNITS["norm1"], 14)

            def up(t, g, j):
                if pr.off is not None or pr.n[pr.s] > 0:
                    pe.wait_ge(out[pr.s], pr.before())
                for half in range(2):
                    chunk(pe, st, [(2 * pr.s + half, P)], (h_hi, h_lo), 0, KD, True, True,
                          1 if pr.off is None and g == j == half == 0 else None)
                pr.step()

            def down(t, g, k):
                pe.wait_ge(act_ready, t + k)
                for n in range(8):
                    products(pe, st, pr, (acts_hi[:, g], acts_lo[:, g]), [P, P], 1, k)

            ffn(pe, st, pr, up, down)
            for n in range(22):
                m = UNITS["cout"] + n
                fill_wait(pe, m)
                for k in range(min(4, 2 * FT - 4 * n)):
                    f = 4 * n + k
                    mm = T.transpose(ps[0:18, bank(m), k * P:(k + 1) * P], cout[:, f // FT, f % FT, :], ident)
                mm.then_inc(filled, 1)
            pe.wait_ge(p_in, 48)
            for n in range(2):
                m = UNITS["pt"] + n
                fill_wait(pe, m)
                for j in range(3):
                    w = rows(j)
                    mm = T.transpose(ps[:, bank(m), j * P:j * P + w], pn[0:w, j, n * P:(n + 1) * P], ident[0:w, 0:w])
                mm.then_inc(filled, 1)
            pe.wait_ge(ple_ready_p, 2)
            square_sum(UNITS["norm2"], 18)
            for n in range(8):
                pe.wait_ge(out[pr.s], pr.before())
                pe.wait_ge(landed[st.slot()], st.landed())
                w = ring[:, st.slot(), :].rearrange("p (k n) -> p k n", k=2)
                for c in range(2):
                    c0 = (n % 4 * 2 + c) * P
                    for k in range(2):
                        mm = T.matmul(ps[:, 2 * pr.s + c, 0:NT], w[:, k, c0:c0 + P], pT[:, k, :], start=(k == 0), stop=(k == 1))
                mm.then_inc(ple_filled, 1)
                pr.step()
                if n % 4 == 3:
                    pe.wait_ge(ple_filled, n + 1)
                    pe.sem_inc(used, 1)
                    st.c += 1
            st.whole += 2
            products(pe, st, pr, (h_hi, h_lo), [P, P], norm=2)
            square_sum(UNITS["norm3"], 22)
            products(pe, st, pr, (h_hi, h_lo), [P, P])
            with pe.Fori(0, 3) as i:
                st.begin(i, 4)
                pr.begin(i, 1)
                for n in range(2):
                    products(pe, st, pr, (h_hi, h_lo), [P, P])
            st.end(3)
            pr.end(3)
            pe.wait_ge(ple_ready, 10)
            for n in range(12):
                m, j, q = UNITS["y"] + n, n // 4, n % 4
                w = rows(j)
                fill_wait(pe, m)
                for k in range(4):
                    mm = T.transpose(ps[0:w, bank(m), k * P:(k + 1) * P], xT[:, 4 * q + k, j * P:j * P + w], ident)
                mm.then_inc(filled, 1)


INPUTS = ["x_prompt", "x_sample", "cache_k", "cache_v", "cache_idx_k", "state_ssm_re", "state_ssm_im", "state_conv",
          "page_table", "p_prompt", "p_sample", "g_mix", "w_in", "g_q", "g_k", "ssm_a_re", "ssm_a_im", "ssm_log_dt",
          "ssm_b_re", "ssm_b_im", "ssm_c_re", "ssm_c_im", "ssm_d", "w_glu", "w_att_br", "w_ssm_br", "w_o", "g_ffn",
          "w_up", "conv_w", "conv_b", "w_down", "w_ple", "g_ple", "g_pg", "w_pg"]
OUTPUTS = [("y_prompt", (TP, D), (1, TP, D)), ("y_sample", (TS, D), (NB, TQ, D)),
           ("k_prompt", (TP, 256), (1, 1, TP, KVH, HD)), ("v_prompt", (TP, 256), (1, 1, TP, KVH, HD)),
           ("idx_k_prompt", (TP, IDIM), (1, 1, TP, IDIM)),
           ("ssm_re_prompt", (SPAIR, P), (1, 1, G_SSM, N_SSM)), ("ssm_im_prompt", (SPAIR, P), (1, 1, G_SSM, N_SSM)),
           ("conv_prompt", (2, 2 * FF), (1, 1, 2, 2 * FF)),
           ("k_sample", (TS, 256), (1, NB, TQ, KVH, HD)), ("v_sample", (TS, 256), (1, NB, TQ, KVH, HD)),
           ("idx_k_sample", (TS, IDIM), (1, NB, TQ, IDIM)),
           ("ssm_re_sample", (P, P), (1, NB, G_SSM, N_SSM)), ("ssm_im_sample", (P, P), (1, NB, G_SSM, N_SSM)),
           ("conv_sample", (2 * NB, 2 * FF), (1, NB, 2, 2 * FF))]


def kernel(**inputs):
    import concourse.bacc as bacc
    from concourse.bass_utils import run_bass_kernel_spmd

    nc = bacc.Bacc("TRN2", target_bir_lowering=False, num_devices=1)
    arrays, a, o = {}, {}, {}
    for name, x in [(n, np.ascontiguousarray(inputs[n])) for n in INPUTS] + sorted(constants().items()):
        arrays[f"in_{name}"] = x
        a[name] = nc.dram_tensor(f"in_{name}", x.shape, mybir.dt.from_np(x.dtype), kind="ExternalInput").ap()
    for name, shape, _ in OUTPUTS:
        o[name] = nc.dram_tensor(f"out_{name}", shape, F32, kind="ExternalOutput").ap()
    build(nc, a, o)
    r = run_bass_kernel_spmd(nc, [arrays], core_ids=[0])
    return tuple(r.results[0][f"out_{name}"].reshape(shape) for name, _, shape in OUTPUTS)
```
